# Optimizing a Trainium2 kernel written in Bass

```python
import math
import jax, jax.numpy as jnp
from jax import lax
import numpy as np

D_MODEL = 1024
BATCH = 1
SEQ = 128
DEPTH = 2
DEC_BATCH = 1
DEC_SEQ = 256
PAST_LEN = 128

GRID_W = 64
N_EVEN = (DEPTH + 1) // 2
N_ODD = DEPTH // 2
EPS = 1e-6
Q_BLOCK = 128
ROPE_THETA = 10000.0

SSD_HEADS = 16
SSD_HEADDIM = 64
SSD_INNER = SSD_HEADS * SSD_HEADDIM
SSD_GROUPS = 2
SSD_STATE = 64
SSD_CONV = 3
SSD_CHUNK = 128
SSD_CONV_DIM = SSD_INNER + 2 * SSD_GROUPS * SSD_STATE

MLA_HEADS = 8
MLA_Q_LORA = 256
MLA_KV_LORA = 128
MLA_NOPE = 64
MLA_ROPE = 32
MLA_V = 64
MLA_QK = MLA_NOPE + MLA_ROPE

EVEN_SPLITS = (SSD_INNER,
               SSD_INNER + SSD_CONV_DIM,
               SSD_INNER + SSD_CONV_DIM + SSD_HEADS,
               SSD_INNER + SSD_CONV_DIM + SSD_HEADS + MLA_Q_LORA)
E_IN = EVEN_SPLITS[-1] + MLA_KV_LORA + MLA_ROPE
E_OUT = SSD_INNER + MLA_HEADS * MLA_V

GQA_HEADS = 16
GQA_KV_HEADS = 4
GQA_HEAD_DIM = 64
ODD_SPLITS = (GQA_HEADS * GQA_HEAD_DIM, (GQA_HEADS + GQA_KV_HEADS) * GQA_HEAD_DIM)
O_IN = (GQA_HEADS + 2 * GQA_KV_HEADS) * GQA_HEAD_DIM
O_OUT = GQA_HEADS * GQA_HEAD_DIM

N_EXPERTS = 16
N_GROUPS = 4
GROUP_SIZE = N_EXPERTS // N_GROUPS
TOP_K = 2
D_EXPERT = 256

kernel_name = 'hybrid_ssd_mla_gqa_moe_diffusion_step'

def rms_norm(x, g):
    xf = x.astype(jnp.float32)
    y = xf * lax.rsqrt(jnp.mean(xf * xf, axis=-1, keepdims=True) + EPS)
    return (y * g.astype(jnp.float32)).astype(x.dtype)

def split_heads(x, n):
    return x.reshape(x.shape[:-1] + (n, x.shape[-1] // n))

def rope_1d(x, pos):
    half = x.shape[-1] // 2
    inv = jnp.power(ROPE_THETA, -jnp.arange(half, dtype=jnp.float32) / half)
    ang = pos.astype(jnp.float32)[:, None] * inv[None, :]
    cos = jnp.cos(ang)[:, None, :]
    sin = jnp.sin(ang)[:, None, :]
    x1, x2 = x[..., :half], x[..., half:]
    return jnp.concatenate([x1 * cos - x2 * sin, x2 * cos + x1 * sin], axis=-1).astype(x.dtype)

def rope_2d(x, row, col):
    a = x.shape[-1] // 2
    return jnp.concatenate([rope_1d(x[..., :a], row), rope_1d(x[..., a:], col)], axis=-1)

def rope_tail(x, n, row, col):
    return jnp.concatenate([x[..., :-n], rope_2d(x[..., -n:], row, col)], axis=-1)

def block_attention(q, k, v):
    b, lq, h, d = q.shape
    hk = k.shape[2]
    r = h // hk
    nb = lq // Q_BLOCK
    scale = d ** -0.5
    qb = q.reshape(b, nb, Q_BLOCK, hk, r, d).transpose(1, 0, 2, 3, 4, 5)

    def one_block(qi):
        s = jnp.einsum('bqgrd,bkgd->bgrqk', qi, k, preferred_element_type=jnp.float32) * scale
        p = jax.nn.softmax(s, axis=-1).astype(v.dtype)
        return jnp.einsum('bgrqk,bkgv->bqgrv', p, v)

    o = lax.map(one_block, qb)
    return o.transpose(1, 0, 2, 3, 4, 5).reshape(b, lq, h, v.shape[-1])

def dw_conv(x, w, bias):
    out = lax.conv_general_dilated(
        x, w[:, None, :].astype(x.dtype), window_strides=(1,),
        padding=[(SSD_CONV // 2, SSD_CONV // 2)],
        dimension_numbers=('NWC', 'WIO', 'NWC'), feature_group_count=x.shape[-1])
    return out + bias

def ssd_scan(x, dt, a, bmat, cmat, h0):
    b, l, h, p = x.shape
    g, n = bmat.shape[2], bmat.shape[3]
    nc = l // SSD_CHUNK
    q = SSD_CHUNK
    rep = h // g
    bh = jnp.repeat(bmat, rep, axis=2).astype(jnp.float32).reshape(b, nc, q, h, n)
    ch = jnp.repeat(cmat, rep, axis=2).astype(jnp.float32).reshape(b, nc, q, h, n)
    dtc = dt.reshape(b, nc, q, h)
    xdt = x.astype(jnp.float32).reshape(b, nc, q, h, p) * dtc[..., None]
    cum = jnp.cumsum(dtc * a, axis=2)
    seg = cum[:, :, :, None, :] - cum[:, :, None, :, :]
    mask = jnp.tril(jnp.ones((q, q), dtype=bool))[:, :, None]
    decay = jnp.exp(jnp.where(mask, seg, -jnp.inf))
    scores = jnp.einsum('bcihn,bcjhn->bcijh', ch, bh) * decay
    y_diag = jnp.einsum('bcijh,bcjhp->bcihp', scores, xdt)
    decay_end = jnp.exp(cum[:, :, -1:, :] - cum)
    states = jnp.einsum('bcjhn,bcjh,bcjhp->bchpn', bh, decay_end, xdt)
    chunk_decay = jnp.exp(cum[:, :, -1, :])

    def step(s, inp):
        st, dc = inp
        return s * dc[:, :, None, None] + st, s

    final, s_in = lax.scan(step, h0.astype(jnp.float32),
                           (jnp.moveaxis(states, 1, 0), jnp.moveaxis(chunk_decay, 1, 0)))
    s_in = jnp.moveaxis(s_in, 0, 1)
    y_off = jnp.einsum('bcihn,bchpn,bcih->bcihp', ch, s_in, jnp.exp(cum))
    return (y_diag + y_off).reshape(b, l, h, p), final

def ssd_mixer(z, xbc, dt_raw, p, h0_f, h0_b):
    b, l, _ = z.shape
    xbc = jax.nn.silu(dw_conv(xbc, p['conv_w'], p['conv_b']))
    xs, bm, cm = jnp.split(xbc, (SSD_INNER, SSD_INNER + SSD_GROUPS * SSD_STATE), axis=-1)
    x = xs.reshape(b, l, SSD_HEADS, SSD_HEADDIM)
    bm = bm.reshape(b, l, SSD_GROUPS, SSD_STATE)
    cm = cm.reshape(b, l, SSD_GROUPS, SSD_STATE)
    dtf = dt_raw.astype(jnp.float32)
    a_f = -jnp.exp(p['a_log_f'].astype(jnp.float32))
    a_b = -jnp.exp(p['a_log_b'].astype(jnp.float32))
    y_f, s_f = ssd_scan(x, jax.nn.softplus(dtf + p['dt_bias_f'].astype(jnp.float32)), a_f, bm, cm, h0_f)
    rev = lambda t: jnp.flip(t, axis=1)
    y_b, s_b = ssd_scan(rev(x), jax.nn.softplus(rev(dtf) + p['dt_bias_b'].astype(jnp.float32)),
                        a_b, rev(bm), rev(cm), h0_b)
    y = y_f + rev(y_b) + x.astype(jnp.float32) * p['d_skip'].astype(jnp.float32)[:, None]
    y = y.reshape(b, l, SSD_INNER).astype(z.dtype)
    y = rms_norm(y * jax.nn.silu(z), p['ssd_norm'])
    return y, s_f.astype(z.dtype), s_b.astype(z.dtype)

def mla_queries(q_lat, p):
    q = split_heads(rms_norm(q_lat, p['q_a_norm']) @ p['w_q_b'], MLA_HEADS)
    return rms_norm(q, p['q_norm'])

def mla_keys_values(ckv, kpe, p):
    kv = split_heads(ckv @ p['w_kv_b'], MLA_HEADS)
    k_nope, v = jnp.split(kv, (MLA_NOPE,), axis=-1)
    k_pe = jnp.broadcast_to(kpe[:, :, None, :], k_nope.shape[:-1] + (MLA_ROPE,))
    k = rms_norm(jnp.concatenate([k_nope, k_pe], axis=-1), p['k_norm'])
    return k, v

def even_mixer(h, p, pos, ctx):
    b, l, _ = h.shape
    z, xbc, dt_raw, q_lat, kv_a = jnp.split(h @ p['w_in'], EVEN_SPLITS, axis=-1)
    if ctx is None:
        h0 = jnp.zeros((b, SSD_HEADS, SSD_HEADDIM, SSD_STATE), jnp.float32)
        h0_f, h0_b = h0, h0
    else:
        h0_f, h0_b = ctx[0], ctx[1]
    y_ssd, s_f, s_b = ssd_mixer(z, xbc, dt_raw, p, h0_f, h0_b)
    ckv = rms_norm(kv_a[..., :MLA_KV_LORA], p['kv_a_norm'])
    kpe = kv_a[..., MLA_KV_LORA:]
    q = mla_queries(q_lat, p)
    k, v = mla_keys_values(ckv, kpe, p)
    if ctx is None:
        state = (s_f, s_b, ckv, kpe)
    else:
        row, col = pos
        q = rope_tail(q, MLA_ROPE, row, col)
        k = rope_tail(k, MLA_ROPE, row, col)
        k_ctx, v_ctx = mla_keys_values(ctx[2], ctx[3], p)
        k = jnp.concatenate([k_ctx, k], axis=1)
        v = jnp.concatenate([v_ctx, v], axis=1)
        state = None
    o = block_attention(q, k, v).reshape(b, l, MLA_HEADS * MLA_V)
    return jnp.concatenate([y_ssd, o], axis=-1) @ p['w_out'], state

def odd_mixer(h, p, pos, ctx):
    b, l, _ = h.shape
    q, k, v = jnp.split(h @ p['w_in'], ODD_SPLITS, axis=-1)
    q = rms_norm(split_heads(q, GQA_HEADS), p['q_norm'])
    k = rms_norm(split_heads(k, GQA_KV_HEADS), p['k_norm'])
    v = split_heads(v, GQA_KV_HEADS)
    if ctx is None:
        state = (k, v)
    else:
        row, col = pos
        q = rope_2d(q, row, col)
        k = jnp.concatenate([ctx[0], rope_2d(k, row, col)], axis=1)
        v = jnp.concatenate([ctx[1], v], axis=1)
        state = None
    o = block_attention(q, k, v).reshape(b, l, O_OUT)
    return o @ p['w_out'], state

def moe_ffn(h, w_router, router_bias, w_gate, w_up, w_down):
    scores = jax.nn.sigmoid(jnp.einsum('bld,de->ble', h, w_router, preferred_element_type=jnp.float32))
    sel = (scores + router_bias.astype(jnp.float32)).reshape(scores.shape[:-1] + (N_GROUPS, GROUP_SIZE))
    group_score = lax.top_k(sel, TOP_K)[0].sum(axis=-1)
    best = jnp.argmax(group_score, axis=-1)
    in_group = jnp.arange(N_GROUPS) == best[..., None]
    masked = jnp.where(in_group[..., None], sel, -jnp.inf).reshape(scores.shape)
    _, idx = lax.top_k(masked, TOP_K)
    w = jnp.take_along_axis(scores, idx, axis=-1)
    w = w / jnp.sum(w, axis=-1, keepdims=True)
    gates = jnp.sum(jax.nn.one_hot(idx, N_EXPERTS, dtype=jnp.float32) * w[..., None], axis=-2).astype(h.dtype)
    a = jnp.einsum('bld,edf->blef', h, w_gate)
    u = jnp.einsum('bld,edf->blef', h, w_up)
    return jnp.einsum('blef,efd->bld', jax.nn.silu(a) * u * gates[..., None], w_down)

def ada_mod(cond, w, b):
    return (jax.nn.silu(cond) @ w + b)[:, None, :]

def trunk_layer(x, mod, g_mix, g_ffn, mixer, p, moe_p, pos, ctx):
    sh1, sc1, gt1, sh2, sc2, gt2 = jnp.split(mod, 6, axis=-1)
    h = rms_norm(x, g_mix) * (1 + sc1) + sh1
    out, state = mixer(h, p, pos, ctx)
    x = x + gt1 * out
    h = rms_norm(x, g_ffn) * (1 + sc2) + sh2
    x = x + gt2 * moe_ffn(h, *moe_p)
    return x, state

def setup_inputs(seed: int = 0) -> dict:
    key = jax.random.key(seed)
    ks = iter(jax.random.split(key, 64))
    D = D_MODEL

    def nrm(shape, scale):
        return jax.random.normal(next(ks), shape, jnp.float32) * scale

    def gain(shape):
        return 1.0 + nrm(shape, 0.02)

    def a_log():
        return jnp.log(jax.random.uniform(next(ks), (N_EVEN, SSD_HEADS), jnp.float32, 1.0, 16.0))

    def dt_bias():
        dt = jnp.exp(jax.random.uniform(next(ks), (N_EVEN, SSD_HEADS), jnp.float32,
                                        math.log(1e-3), math.log(1e-1)))
        return dt + jnp.log(-jnp.expm1(-dt))

    return {
        'x_prompt': nrm((BATCH, SEQ, D), 1.0),
        'x_sample': nrm((DEC_BATCH, DEC_SEQ, D), 1.0),
        'c': nrm((DEC_BATCH, D), 1.0),
        'state_ssd_fwd': nrm((DEC_BATCH, N_EVEN, SSD_HEADS, SSD_HEADDIM, SSD_STATE), 0.1),
        'state_ssd_bwd': nrm((DEC_BATCH, N_EVEN, SSD_HEADS, SSD_HEADDIM, SSD_STATE), 0.1),
        'cache_mla_ckv': nrm((DEC_BATCH, N_EVEN, PAST_LEN, MLA_KV_LORA), 1.0),
        'cache_mla_kpe': nrm((DEC_BATCH, N_EVEN, PAST_LEN, MLA_ROPE), 1.0),
        'cache_gqa_k': nrm((DEC_BATCH, N_ODD, PAST_LEN, GQA_KV_HEADS, GQA_HEAD_DIM), 1.0),
        'cache_gqa_v': nrm((DEC_BATCH, N_ODD, PAST_LEN, GQA_KV_HEADS, GQA_HEAD_DIM), 1.0),
        'c_ctx': nrm((D,), 1.0),
        'g_mix': gain((DEPTH, D)),
        'g_ffn': gain((DEPTH, D)),
        'w_ada': nrm((DEPTH, D, 6 * D), 0.5 * D ** -0.5),
        'b_ada': nrm((DEPTH, 6 * D), 0.02),
        'w_router': nrm((D, N_EXPERTS), D ** -0.5),
        'router_bias': nrm((N_EXPERTS,), 0.01),
        'w_exp_gate': nrm((DEPTH, N_EXPERTS, D, D_EXPERT), D ** -0.5),
        'w_exp_up': nrm((DEPTH, N_EXPERTS, D, D_EXPERT), D ** -0.5),
        'w_exp_down': nrm((DEPTH, N_EXPERTS, D_EXPERT, D), D_EXPERT ** -0.5),
        'w_in_even': nrm((N_EVEN, D, E_IN), D ** -0.5),
        'ssd_conv_w': nrm((N_EVEN, SSD_CONV, SSD_CONV_DIM), SSD_CONV ** -0.5),
        'ssd_conv_b': nrm((N_EVEN, SSD_CONV_DIM), 0.02),
        'ssd_a_log_fwd': a_log(),
        'ssd_a_log_bwd': a_log(),
        'ssd_dt_bias_fwd': dt_bias(),
        'ssd_dt_bias_bwd': dt_bias(),
        'ssd_d': gain((N_EVEN, SSD_HEADS)),
        'ssd_norm': gain((N_EVEN, SSD_INNER)),
        'mla_q_a_norm': gain((N_EVEN, MLA_Q_LORA)),
        'mla_w_q_b': nrm((N_EVEN, MLA_Q_LORA, MLA_HEADS * MLA_QK), MLA_Q_LORA ** -0.5),
        'mla_kv_a_norm': gain((N_EVEN, MLA_KV_LORA)),
        'mla_w_kv_b': nrm((N_EVEN, MLA_KV_LORA, MLA_HEADS * (MLA_NOPE + MLA_V)), MLA_KV_LORA ** -0.5),
        'mla_q_norm': gain((N_EVEN, MLA_QK)),
        'mla_k_norm': gain((N_EVEN, MLA_QK)),
        'w_out_even': nrm((N_EVEN, E_OUT, D), E_OUT ** -0.5),
        'w_in_odd': nrm((N_ODD, D, O_IN), D ** -0.5),
        'gqa_q_norm': gain((N_ODD, GQA_HEAD_DIM)),
        'gqa_k_norm': gain((N_ODD, GQA_HEAD_DIM)),
        'w_out_odd': nrm((N_ODD, O_OUT, D), O_OUT ** -0.5),
    }

def reference(x_prompt, x_sample, c, state_ssd_fwd, state_ssd_bwd, cache_mla_ckv, cache_mla_kpe,
              cache_gqa_k, cache_gqa_v, c_ctx, g_mix, g_ffn, w_ada, b_ada, w_router, router_bias,
              w_exp_gate, w_exp_up, w_exp_down, w_in_even, ssd_conv_w, ssd_conv_b, ssd_a_log_fwd,
              ssd_a_log_bwd, ssd_dt_bias_fwd, ssd_dt_bias_bwd, ssd_d, ssd_norm, mla_q_a_norm,
              mla_w_q_b, mla_kv_a_norm, mla_w_kv_b, mla_q_norm, mla_k_norm, w_out_even, w_in_odd,
              gqa_q_norm, gqa_k_norm, w_out_odd):
    rows = x_sample.shape[1] // GRID_W
    pos = (jnp.repeat(jnp.arange(rows), GRID_W), jnp.tile(jnp.arange(GRID_W), rows))
    xc, xl = x_prompt, x_sample
    even_states, odd_states = [], []
    for i in range(DEPTH):
        j = i // 2
        if i % 2 == 0:
            mixer = even_mixer
            p = {'w_in': w_in_even[j], 'conv_w': ssd_conv_w[j], 'conv_b': ssd_conv_b[j],
                 'a_log_f': ssd_a_log_fwd[j], 'a_log_b': ssd_a_log_bwd[j],
                 'dt_bias_f': ssd_dt_bias_fwd[j], 'dt_bias_b': ssd_dt_bias_bwd[j],
                 'd_skip': ssd_d[j], 'ssd_norm': ssd_norm[j], 'q_a_norm': mla_q_a_norm[j],
                 'w_q_b': mla_w_q_b[j], 'kv_a_norm': mla_kv_a_norm[j], 'w_kv_b': mla_w_kv_b[j],
                 'q_norm': mla_q_norm[j], 'k_norm': mla_k_norm[j], 'w_out': w_out_even[j]}
            lat_ctx = (state_ssd_fwd[:, j], state_ssd_bwd[:, j], cache_mla_ckv[:, j], cache_mla_kpe[:, j])
        else:
            mixer = odd_mixer
            p = {'w_in': w_in_odd[j], 'q_norm': gqa_q_norm[j], 'k_norm': gqa_k_norm[j],
                 'w_out': w_out_odd[j]}
            lat_ctx = (cache_gqa_k[:, j], cache_gqa_v[:, j])
        moe_p = (w_router, router_bias, w_exp_gate[i], w_exp_up[i], w_exp_down[i])
        mod_ctx = ada_mod(c_ctx[None, :], w_ada[i], b_ada[i])
        mod_lat = ada_mod(c, w_ada[i], b_ada[i])
        xc, st = trunk_layer(xc, mod_ctx, g_mix[i], g_ffn[i], mixer, p, moe_p, None, None)
        xl, _ = trunk_layer(xl, mod_lat, g_mix[i], g_ffn[i], mixer, p, moe_p, pos, lat_ctx)
        if i % 2 == 0:
            even_states.append(st)
        else:
            odd_states.append(st)
    new_ssd_fwd = jnp.stack([s[0] for s in even_states], axis=1)
    new_ssd_bwd = jnp.stack([s[1] for s in even_states], axis=1)
    new_mla_ckv = jnp.stack([s[2] for s in even_states], axis=1)
    new_mla_kpe = jnp.stack([s[3] for s in even_states], axis=1)
    new_gqa_k = jnp.stack([s[0] for s in odd_states], axis=1)
    new_gqa_v = jnp.stack([s[1] for s in odd_states], axis=1)
    return (xc, xl, new_ssd_fwd, new_ssd_bwd, new_mla_ckv, new_mla_kpe, new_gqa_k, new_gqa_v)


_drawn_inputs = setup_inputs


def setup_inputs(seed=0):
    import zlib

    import numpy as np

    out = dict(_drawn_inputs(seed))
    spreads = {}
    factors = {'cache_mla_kpe': 3.264,
     'cache_gqa_k': 3.119,
     'ssd_d': 4.072,
     'mla_q_a_norm': 5.067,
     'mla_kv_a_norm': 2.789,
     'mla_q_norm': 5.068,
     'mla_k_norm': 8.0,
     'gqa_q_norm': 8.0,
     'gqa_k_norm': 2.681}
    for name, (base, spread) in spreads.items():
        noise = np.random.default_rng([zlib.crc32(name.encode()), seed]).standard_normal(out[name].shape)
        drawn = base * np.exp(spread * noise) if base else spread * noise
        out[name] = __import__('jax').numpy.asarray(drawn.astype(out[name].dtype))
    for name, factor in factors.items():
        out[name] = (out[name] * factor).astype(out[name].dtype)
    return out
```

```python
import math
from contextlib import ExitStack

import numpy as np

import concourse.bass as bass
from concourse import mybir

P = 128
D = 1024
DC = D // P
T = 384
NT = T // P
DEPTH = 2
EPS = 1e-6
HS, PS, NS = 16, 64, 64
HG = HS // 2
HM, NOPE, ROPE, VM = 8, 64, 32, 64
QM = NOPE + ROPE
HQ, HKV, HD = 16, 4, 64
NE, NG, GS, FE = 16, 4, 4, 256
GRID_W = 64
THETA = 10000.0
CONV_C = 10
SLOT = 3072
RING = 8
N_ADA, N_INE, N_OUTE, N_MOE, N_INO, N_OUTO = 16, 7, 4, 32, 4, 3
S_ADA0 = 0
S_INE = S_ADA0 + N_ADA
S_ADA1 = S_INE + N_INE
S_OUTE = S_ADA1 + N_ADA
S_MOE0 = S_OUTE + N_OUTE
S_INO = S_MOE0 + N_MOE
S_OUTO = S_INO + N_INO
S_MOE1 = S_OUTO + N_OUTO
N_SLOTS = S_MOE1 + N_MOE
BIG = 1e30

SMALL = [("ident", P), ("ones", P), ("tri_f", P), ("tri_b", P), ("mask_f", P), ("mask_b", P),
         ("cos_e", 2 * ROPE), ("sin_e", 2 * ROPE), ("cos_o", 2 * HD), ("sin_o", 2 * HD),
         ("g_mix", DEPTH * DC), ("g_ffn", DEPTH * DC), ("b_ada", DEPTH * 48), ("conv_w", 3 * CONV_C), ("conv_b", CONV_C),
         ("ssd_norm", DC), ("q_a_norm", 2), ("kv_a_norm", 1), ("cond", 2 * DC),
         ("q_norm", QM), ("k_norm", QM), ("gq_norm", HD), ("gk_norm", HD), ("router_bias", NE),
         ("a_log", 2 * HS), ("dt_bias", 2 * HS), ("d_skip", HS), ("first_wins", NG + NE),
         ("ckv_cache", P), ("kpe_cache", ROPE), ("k_cache", HKV * HD), ("v_cache", HKV * HD), ("h0", 2 * HG * PS),
         ("w_router", DC * NE), ("w_dk", DC * 48), ("w_q_b", 2 * HM * QM), ("w_kv_b", HM * (NOPE + VM))]
OFF, _at = {}, 0
for _n, _w in SMALL:
    OFF[_n] = (_at, _w)
    _at += _w
N_SMALL = _at


def build(nc, small_d, x_d, w_d, y_d, stf_d, stb_d, ckv_d, kpe_d, gk_d, gv_d):
    f32 = mybir.dt.float32
    ALU = mybir.AluOpType
    ACT = mybir.ActivationFunctionType
    AX = mybir.AxisListType
    MUL, ADD, SUB, MAX, MIN, EQ = ALU.mult, ALU.add, ALU.subtract, ALU.max, ALU.min, ALU.is_equal

    ctx = ExitStack()
    with ctx:
        sb = lambda name, n: ctx.enter_context(nc.sbuf_tensor(name, [P, n], f32))
        sem = lambda name: ctx.enter_context(nc.semaphore(name))
        ring = ctx.enter_context(nc.sbuf_tensor("ring", [P, RING, SLOT], f32))
        xT = ctx.enter_context(nc.sbuf_tensor("xT", [P, DC, T], f32))
        hTt = sb("hT", DC * T)
        small = sb("small", N_SMALL)
        misc = sb("misc", 256)
        U_SIZE = 15240
        U = sb("U", U_SIZE)
        ps = ctx.enter_context(nc.psum_tensor("ps", [P, 8, 512], f32))

        hT = hTt[:, :].rearrange("p (c t) -> p c t", c=DC)

        def sm(name):
            o, w = OFF[name]
            return small[:, o:o + w]

        ident, ones = sm("ident"), sm("ones")
        tri = [sm("tri_f"), sm("tri_b")]
        mask = [sm("mask_f"), sm("mask_b")]

        def region(base, *widths):
            out, at = [], base
            for w in widths:
                out.append(U[:, at:at + w])
                at += w
            assert at <= U_SIZE, at
            return out

        mod = [misc[:, 0:96], misc[:, 96:192]]
        condS = misc[:, 192:208]
        AB = misc[:, 208:240]
        ssd_r = misc[:, 240:241]
        zs, xc, oTy, oTm, lat, dk, e_sm = region(0, 3072, CONV_C * 385, 3072, 1536, 1152, 144, 1000)
        TAIL = 3072 + CONV_C * 385 + 3072 + 1536 + 1152 + 144 + 1000
        rn, = region(TAIL, 384)
        xr = [region(TAIL + 387 * i, 387)[0] for i in range(2)]
        zs3 = zs.rearrange("p (t n) -> p t n", t=NT)
        xc3 = xc.rearrange("p (c t) -> p c t", c=CONV_C)
        oTy3 = oTy.rearrange("p (c t) -> p c t", c=8)
        oTm3 = oTm.rearrange("p (c t) -> p c t", c=4)
        latT = lat.rearrange("p (c t) -> p c t", c=3)
        dk3 = dk.rearrange("p (t n) -> p t n", t=NT)
        e96 = [e_sm[:, 96 * i:96 * i + 96] for i in range(10)]
        xdt = [hTt[:, 0:1024], hTt[:, 1024:2048]]
        xtok = hTt[:, 2048:3072]
        dec = [oTm[:, 0:512], oTm[:, 512:1024]]
        xw = ytok = oTm[:, 0:1024]
        ytmp = oTm[:, 1024:1536]
        s_b1, Gs, Btok = region(TAIL, 512, 256, 128)
        h0 = [sm("h0")[:, 0:512], sm("h0")[:, 512:1024]]
        Gs2 = [Gs[:, 0:128], Gs[:, 128:256]]
        mkT, mv, mPb = region(0, HM * 512, 4 * HM * VM, 768)
        mkT3 = mkT.rearrange("p (h n) -> p h n", h=HM)
        mv3 = mv.rearrange("p (s n) -> p s n", s=4)
        mqT3 = hTt[:, :].rearrange("p (h n) -> p h n", h=HM)
        msq = e_sm[:, 0:768]
        mnm, mrs = e_sm[:, 768:816], e_sm[:, 816:864]
        mkt, mot = region(TAIL, HM * QM, HM * VM)
        mss = e_sm[:, 864:872]
        lsq = hTt[:, 0:1152]
        lr = [mkT[:, 0:384], mkT[:, 384:768]]
        qkv, gkT, gPb, gPTb, oT, gkt, gsq, got, odd_sm = region(
            0, NT * 1536, HKV * 512, 768, 768, 3072, 512, 1024, 1024, 200)
        qkv3 = qkv.rearrange("p (t n) -> p t n", t=NT)
        gkT3 = gkT.rearrange("p (h n) -> p h n", h=HKV)
        gqT3 = hTt[:, :].rearrange("p (h n) -> p h n", h=8)
        oT3 = oT.rearrange("p (c t) -> p c t", c=8)
        gnm, grs, gss = odd_sm[:, 0:48], odd_sm[:, 48:96], odd_sm[:, 96:112]
        yacc, sil, act_b, actT, gcur, rt = region(0, NT * D, 512, 512, 512, NT * GS, 1600)
        yacc3 = yacc.rearrange("p (t n) -> p t n", t=NT)
        rt48 = [rt[:, 48 * i:48 * i + 48] for i in range(12)]
        rt12 = [rt[:, 576 + 12 * i:576 + 12 * i + 12] for i in range(12)]
        rt3 = [rt[:, 720 + 3 * i:720 + 3 * i + 3] for i in range(8)]
        gates = rt48[11]

        names = """in_small in_x cond_ready ada_done mod_ready sq_ready ss_used r_ready h_ready ab_ready slot_used job_done
            free_act free_dve chain_dve chain_act xr_ready xr_used xc_raw xc_ready z_ready lat_copied
            dk_copied e_in e_mid dt_ready cum_copied e_cum
            xtok_ready xtok_used xdt_ready g_ready seg_ready dec_ready s_ready diag_done xw_ready st_done
            ytok_ready ysq_ready ynorm_ready ynormed yT_ready ssd_done lsq_ready lr_ready latn_ready
            qt_copied qk_sq qk_r qk_ready kt_nope qkT_ready
            max_ready p_ready pt_ready pv_done o_tok o_ready x_new
            qkv_ready rt_exp gates_ready sil_ready act_ready tr_done trc_ready dn_done acc_ready au_done gcur_ready""".split()
        S = {n: sem(n) for n in names}
        slot_full = [sem(f"slot_full{i}") for i in range(RING)]
        outs = {n: sem("stored_" + n) for n in ("y", "stf", "stb", "ckv", "kpe", "gk", "gv")}

        jobs = []

        def job(name, by):
            jobs.append((name, by))

        STEPS = [(2, False), (1, True), (2, True), (0, True)]
        STATES = [(1,), (0,), (), (0, 1)]

        def attention_jobs(kind, heads):
            units = [(t, h) for t in range(NT) for h in range(heads)]
            job((kind, "s", 0), "A")
            for u in range(len(units)):
                if u + 1 < len(units):
                    job((kind, "s", u + 1), "A")
                job((kind, "pT", u), "D")
                if units[u][1] == heads - 1:
                    for k in range(heads // 8):
                        job((kind, "oT", units[u][0], k), "A")

        for l in range(DEPTH):
            job(("ss", l, 0), "A")
            if l == 0:
                job(("dk",), "D")
                for c in range(CONV_C):
                    job(("xbc", c), "A")
                for c in range(3):
                    job(("lat", c), "D")
                for i in range(3):
                    for t in range(NT):
                        job(("z", i, t), "A")
                job(("cum",), "D")
                job(("tot",), "D")
                for i, (t, full) in enumerate(STEPS):
                    job(("xt", i, 0), "A")
                    job(("xt", i, 1), "A")
                    job(("bt", i), "A")
                    if full:
                        job(("g", i, 0), "A")
                        job(("g", i, 1), "A")
                        for u in range(8):
                            job(("bc", i, u), "D")
                        if t:
                            for d in range(2):
                                for g in range(2):
                                    job(("off", i, d, g), "D")
                        job(("yT", i, 0), "A")
                        job(("yT", i, 1), "A")
                    for d in STATES[i]:
                        job(("st", i, d), "D")
                job(("sl", 0), "A")
                job(("sl", 1), "A")
                for t in range(NT):
                    job(("q", t, 0), "A")
                    job(("q", t, 1), "A")
                    job(("qT", t, 0), "A")
                    job(("qT", t, 1), "A")
                for s in range(4):
                    job(("kv", s, 0), "A")
                    job(("kv", s, 1), "A")
                    job(("kT", s, 0), "A")
                    job(("kT", s, 1), "A")
                attention_jobs("mla", HM)
            else:
                for s in range(N_INO):
                    for t in range(NT):
                        job(("in", s, t), "A" if s % 2 else "D")
                for t in range(NT):
                    job(("gqT", t, 0), "A")
                    job(("gqT", t, 1), "A")
                    job(("gkT", t), "A")
                job(("gkT", 3), "A")
                attention_jobs("gqa", HQ)
            for c in range(DC):
                job(("out", l, c), "D")
            job(("ss", l, 1), "A")
            job(("rt", l), "A")
            for c in range(DC):
                job(("moe", l, c), "D")
        RB = 5
        index = {n: i for i, (n, _) in enumerate(jobs)}
        assert len(index) == len(jobs)
        emptied, _cnt = [], {"A": 0, "D": 0}
        for n, by in jobs:
            _cnt[by] += 1
            emptied.append((by, _cnt[by]))
        free_of = {"A": S["free_act"], "D": S["free_dve"]}
        bank = lambda j: ps[:, j % RB, :]

        KSLOT = [0, 2, 3, 1]
        KEYS = [(0, 128), (128, 384), (128, 384)]
        XC0 = [0, 129, 257]
        TILE = [slice(P * t, P * t + P) for t in range(NT)]
        SEG = [slice(0, P), slice(P, T)]

        block = ctx.enter_context(nc.Block())

        @block.sync
        def _(sp):
            def load(n, at, wait):
                if wait is not None:
                    sp.wait_ge(S["slot_used"], wait)
                sp.dma_start(ring[:, at, :], w_d[bass.ds(n, 1), :, :].rearrange("a p n -> p (a n)")).then_inc(slot_full[at], 16)

            for n in range(RING):
                load(n, n, None)
            with sp.Fori(1, N_SLOTS // RING) as i:
                for j in range(RING):
                    load(i * RING + j, j, i * RING + (j - RING + 1))
            for n in range(N_SLOTS // RING * RING, N_SLOTS):
                load(n, n % RING, n - RING + 1)
            sp.wait_ge(S["x_new"], 4 * DC)
            sp.dma_start(y_d, xT[:, :, :]).then_inc(outs["y"], 16)
            for n in outs:
                sp.wait_ge(outs[n], 16)

        @block.tensor
        def _(pe):
            at = [0]

            def fill(*name):
                j = at[0]
                assert jobs[j][0] == name, (jobs[j], name)
                if j >= RB:
                    by, n = emptied[j - RB]
                    pe.wait_ge(free_of[by], n)
                at[0] += 1
                return bank(j)

            def filled(ins):
                ins.then_inc(S["job_done"], 1)

            def slot(n):
                pe.wait_ge(slot_full[n % RING], 16 * (n // RING + 1))
                return ring[:, n % RING, :]

            def used(ins):
                ins.then_inc(S["slot_used"], 1)

            mm = pe.matmul

            def ada(l, j):
                if j == 0:
                    pe.wait_ge(S["cond_ready"], 1)
                    if l:
                        pe.wait_ge(S["mod_ready"], l)
                w = slot((S_ADA1 if l else S_ADA0) + j).rearrange("p (k n) -> p k n", k=DC)
                for m in range(3):
                    c = 2 * (3 * j + m)
                    for k in range(DC):
                        ins = mm(ps[:, 7, c:c + 2], w[:, k, P * m:P * m + P], condS[:, 2 * k:2 * k + 2],
                                 start=(k == 0), stop=(k == DC - 1))
                used(ins)
                if j == N_ADA - 1:
                    pe.drain().then_inc(S["ada_done"], 1)

            def sum_squares(l, i):
                pe.wait_ge(S["sq_ready"], 2 * l + i + 1)
                b = fill("ss", l, i)
                for k in range(DC):
                    ins = mm(b[:, 0:T], ones, hT[:, k, :], start=(k == 0), stop=(k == DC - 1))
                filled(ins)

            def project(name, out, lhs, rhs, n=DC):
                for k in range(n):
                    ins = mm(out, lhs(k), rhs(k), start=(k == 0), stop=(k == n - 1))
                return ins

            def attention(kind, heads, q_of, k_of, v_of, Pb, PTb, ot):
                base = 0 if kind == "mla" else NT * HM
                tb = 0 if kind == "mla" else NT
                units = [(t, h) for t in range(NT) for h in range(heads)]

                def scores(u):
                    t, h = units[u]
                    k0, nk = KEYS[t]
                    b = fill(kind, "s", u)
                    filled(mm(b[:, 0:nk], q_of(t, h), k_of(h, k0, nk), start=True, stop=True))

                def turn_p(u):
                    t, h = units[u]
                    nk = KEYS[t][1]
                    pe.wait_ge(S["p_ready"], base + u + 1)
                    b = fill(kind, "pT", u)
                    for k in range(nk // P):
                        ins = pe.transpose(b[:, P * k:P * k + P], Pb[:, 384 * (u % 2) + P * k:384 * (u % 2) + P * k + P], ident)
                    filled(ins)

                def values(u):
                    t, h = units[u]
                    k0, nk = KEYS[t]
                    if h == 0 and t:
                        pe.wait_ge(S["o_tok"], tb + t)
                    pe.wait_ge(S["pt_ready"], base + u + 1)
                    for k in range(nk // P):
                        ins = mm(ps[:, 5 + h // 8, 64 * (h % 8):64 * (h % 8) + 64],
                                 PTb[:, 384 * (u % 2) + P * k:384 * (u % 2) + P * k + P], v_of(k0 // P + k, h),
                                 start=(k == 0), stop=(k == nk // P - 1))
                    ins.then_inc(S["pv_done"], 1)

                scores(0)
                for u in range(len(units)):
                    if u + 1 < len(units):
                        scores(u + 1)
                    turn_p(u)
                    values(u)
                    t, h = units[u]
                    if h == heads - 1:
                        pe.wait_ge(S["o_tok"], tb + t + 1)
                        for k in range(heads // 8):
                            b = fill(kind, "oT", t, k)
                            for c in range(4):
                                ins = pe.transpose(b[:, P * c:P * c + P], ot[:, 512 * k + P * c:512 * k + P * c + P], ident)
                            filled(ins)

            def project_out(l, n_k, cols, first, src):
                pe.wait_ge(S["o_ready"], NT * (l + 1))
                for j, n in enumerate(cols):
                    w = slot(first + j)[:, 0:n_k * P * n].rearrange("p (k n) -> p k n", k=n_k)
                    for m in range(n):
                        b = fill("out", l, sum(cols[:j]) + m)
                        ins = project("out", b[:, 0:T], lambda k: w[:, k, P * m:P * m + P], src, n_k)
                        filled(ins)
                    pe.drain().then_inc(S["slot_used"], 1)

            def moe(l):
                sum_squares(l, 1)
                pe.wait_ge(S["h_ready"], 2 * l + 2)
                b = fill("rt", l)
                wr = sm("w_router").rearrange("p (k e) -> p k e", k=DC)
                for t in range(NT):
                    ins = project("rt", b[:, NE * t:NE * t + NE], lambda k: hT[:, k, TILE[t]], lambda k: wr[:, k, :])
                filled(ins)
                for by in "AD":
                    pe.wait_ge(free_of[by], max([n for o, n in emptied[:at[0]] if o == by]))
                pe.wait_ge(S["mod_ready"], 2)
                pe.wait_ge(S["gates_ready"], l + 1)
                first = S_MOE1 if l else S_MOE0
                n_u = 4 * NT
                tot = NG * n_u * l
                with pe.Fori(0, NG) as g:
                    def down(v):
                        e, t = v // NT, v % NT
                        a2 = (first + 2 * e + 1) % RING
                        pe.wait_ge(S["act_ready"], g * n_u + (tot + v + 1))
                        for j in range(2):
                            ins = pe.transpose(ps[:, 2 + v % 2, P * j:P * j + P], act_b[:, 256 * (v % 2) + P * j:256 * (v % 2) + P * j + P], ident)
                        ins.then_inc(S["tr_done"], 1)
                        pe.wait_ge(S["trc_ready"], g * n_u + (tot + v + 1))
                        if v >= 2:
                            pe.wait_ge(S["acc_ready"], g * n_u + (tot + v - 1))
                        for hh in range(2):
                            for j in range(2):
                                ins = mm(ps[:, 4 + 2 * (v % 2) + hh, :], actT[:, 256 * (v % 2) + P * j:256 * (v % 2) + P * j + P],
                                         ring[:, a2, 1024 + 1024 * j + 512 * hh:1024 + 1024 * j + 512 * hh + 512], start=(j == 0), stop=(j == 1))
                        ins.then_inc(S["dn_done"], 1)
                        if t == NT - 1:
                            pe.drain().then_inc(S["slot_used"], 2)

                    for u in range(n_u):
                        e, t = u // NT, u % NT
                        a1, a2 = (first + 2 * e) % RING, (first + 2 * e + 1) % RING
                        if t == 0:
                            pe.wait_ge(slot_full[a1], g * 16 + 16 * ((first + 2 * e) // RING + 1))
                            pe.wait_ge(slot_full[a2], g * 16 + 16 * ((first + 2 * e + 1) // RING + 1))
                        if u >= 2:
                            pe.wait_ge(S["act_ready"], g * n_u + (tot + u - 1))
                        for k in range(DC):
                            w = ring[:, a1, 512 * k:512 * k + 512] if k < 6 else ring[:, a2, 512 * (k - 6):512 * (k - 6) + 512]
                            ins = mm(ps[:, u % 2, :], hT[:, k, TILE[t]], w, start=(k == 0), stop=(k == DC - 1))
                        ins.then_inc(S["au_done"], 1)
                        if u:
                            down(u - 1)
                    down(n_u - 1)
                    pe.wait_ge(S["acc_ready"], g * n_u + (tot + n_u))
                for c in range(DC):
                    b = fill("moe", l, c)
                    for t in range(NT):
                        ins = pe.transpose(b[:, P * t:P * t + P], yacc3[:, t, P * c:P * c + P], ident)
                    filled(ins)

            pe.wait_ge(S["in_small"], 16)
            for j in range(N_ADA):
                ada(0, j)
            sum_squares(0, 0)
            pe.wait_ge(S["h_ready"], 1)
            wdk = sm("w_dk").rearrange("p (k n) -> p k n", k=DC)
            b = fill("dk")
            for t in range(NT):
                ins = project("dk", b[:, 48 * t:48 * t + 48], lambda k: hT[:, k, TILE[t]], lambda k: wdk[:, k, :])
            filled(ins)
            for s in range(N_INE):
                w = slot(S_INE + s).rearrange("p (k n) -> p k n", k=DC)
                for m in range(3):
                    c = 3 * s + m
                    if c < 13:
                        b = fill("xbc", c) if c < CONV_C else fill("lat", c - CONV_C)
                        filled(project("in", b[:, 0:T], lambda k: w[:, k, P * m:P * m + P], lambda k: hT[:, k, :]))
                if s >= 4:
                    lo = P if s == 4 else 0
                    for t in range(NT):
                        b = fill("z", s - 4, t)
                        filled(project("z", b[:, 0:T - lo], lambda k: hT[:, k, TILE[t]], lambda k: w[:, k, lo:T]))
                pe.drain().then_inc(S["slot_used"], 1)
            ada_at = [0]
            pe.wait_ge(S["dt_ready"], 1)
            b = fill("cum")
            for d in range(2):
                ins = mm(b[:, 48 * d:48 * d + 48], tri[d], e96[3][:, 48 * d:48 * d + 48], start=True, stop=True)
            filled(ins)
            b = fill("tot")
            filled(mm(b[:, 0:96], ones, e96[3], start=True, stop=True))
            pe.wait_ge(S["xc_ready"], CONV_C)
            nfull = 0
            for i, (t, full) in enumerate(STEPS):
                c0 = XC0[t]
                for k in range(2):
                    b = fill("xt", i, k)
                    for c in range(4):
                        ins = pe.transpose(b[:, P * c:P * c + P], xc3[:, 4 * k + c, c0:c0 + P], ident)
                    filled(ins)
                b = fill("bt", i)
                filled(pe.transpose(b[:, 0:P], xc3[:, 8, c0:c0 + P], ident))
                if full:
                    for g in range(2):
                        b = fill("g", i, g)
                        filled(mm(b[:, 0:P], xc3[64 * g:64 * g + 64, 8, c0:c0 + P], xc3[64 * g:64 * g + 64, 9, c0:c0 + P], start=True, stop=True))
                    base = 8 * nfull

                    def cums(u):
                        q, d = u // 2, u % 2
                        b = fill("bc", i, u)
                        for h in range(4):
                            col = 48 * d + HS * t + 4 * q + h
                            ins = mm(b[:, P * h:P * h + P], e96[3][:, col:col + 1].broadcast_to([P, P]), tri[d], start=True, stop=True)
                        filled(ins)

                    def diag(u):
                        q, d = u // 2, u % 2
                        pe.wait_ge(S["s_ready"], base + u + 1)
                        for h in range(4):
                            hh = 4 * (q % 2) + h
                            ins = mm(ps[:, 5 + q // 2, 64 * hh:64 * hh + 64], dec[d][:, P * h:P * h + P],
                                     xdt[d][:, 64 * (4 * q + h):64 * (4 * q + h) + 64],
                                     start=(u % 4 == 0 and h == 0), stop=(d == 1), skip_group_check=True)
                        ins.then_inc(S["diag_done"], 1)

                    cums(0)
                    for u in range(8):
                        if u + 1 < 8:
                            cums(u + 1)
                        diag(u)
                        if u % 8 in (0, 1, 3, 5, 6, 7) and ada_at[0] < N_ADA:
                            ada(1, ada_at[0])
                            ada_at[0] += 1
                    if t:
                        for d in range(2):
                            s_in = {(0, 1): h0[0], (0, 2): h0[0], (1, 2): h0[1], (1, 1): s_b1}[d, t]
                            if d == 0:
                                pe.wait_ge(S["st_done"], 1 if t == 1 else 2)
                            for g in range(2):
                                b = fill("off", i, d, g)
                                filled(mm(b[:, 0:512], xc3[64 * g:64 * g + 64, 9, c0:c0 + P], s_in[64 * g:64 * g + 64, :], start=True, stop=True))
                    pe.wait_ge(S["ynormed"], nfull + 1)
                    for k in range(2):
                        b = fill("yT", i, k)
                        for c in range(4):
                            ins = pe.transpose(b[:, P * c:P * c + P], ytok[:, 512 * k + P * c:512 * k + P * c + P], ident)
                        filled(ins)
                    nfull += 1
                for d in STATES[i]:
                    pe.wait_ge(S["xw_ready"], sum(len(x) for x in STATES[:i]) + STATES[i].index(d) + 1)
                    b = fill("st", i, d)
                    for g in range(2):
                        ins = mm(b[64 * g:64 * g + 64, 0:512], Btok[:, 64 * g:64 * g + 64], xw[:, 512 * g:512 * g + 512], start=True, stop=True)
                    filled(ins)
            while ada_at[0] < N_ADA:
                ada(1, ada_at[0])
                ada_at[0] += 1
            pe.wait_ge(S["lsq_ready"], 1)
            b = fill("sl", 0)
            for k in range(2):
                ins = mm(b[:, 0:T], ones, lsq[:, T * k:T * k + T], start=(k == 0), stop=(k == 1))
            filled(ins)
            b = fill("sl", 1)
            filled(mm(b[:, 0:T], ones, lsq[:, 2 * T:3 * T], start=True, stop=True))
            pe.wait_ge(S["latn_ready"], 1)
            wq = sm("w_q_b").rearrange("p (k n) -> p k n", k=2)
            wkv = sm("w_kv_b")
            for t in range(NT):
                for hh in range(2):
                    b = fill("q", t, hh)
                    filled(project("q", b[:, 0:384], lambda k: latT[:, k, TILE[t]], lambda k: wq[:, k, 384 * hh:384 * hh + 384], 2))
                pe.wait_ge(S["qk_ready"], t + 1)
                for hh in range(2):
                    b = fill("qT", t, hh)
                    for h in range(4):
                        ins = pe.transpose(b[0:QM, P * h:P * h + P], mkt[:, QM * (4 * hh + h):QM * (4 * hh + h) + QM], ident)
                    filled(ins)
            for s in range(4):
                src = latT[:, 2, TILE[s]] if s < NT else sm("ckv_cache")
                for hh in range(2):
                    b = fill("kv", s, hh)
                    filled(mm(b[:, 0:512], src, wkv[:, 512 * hh:512 * hh + 512], start=True, stop=True))
                pe.wait_ge(S["qk_ready"], NT + s + 1)
                for hh in range(2):
                    b = fill("kT", s, hh)
                    for h in range(4):
                        ins = pe.transpose(b[0:QM, P * h:P * h + P], mkt[:, QM * (4 * hh + h):QM * (4 * hh + h) + QM], ident)
                    filled(ins)
            pe.wait_ge(S["qkT_ready"], 2 * (NT + 4))
            attention("mla", HM, lambda t, h: mqT3[0:QM, h, TILE[t]], lambda h, k0, nk: mkT3[0:QM, h, k0:k0 + nk],
                      lambda s, h: mv3[:, s, 64 * h:64 * h + 64], mPb, msq, mot)
            project_out(0, 12, (2, 2, 2, 2), S_OUTE, lambda k: oTy3[:, k, :] if k < 8 else oTm3[:, k - 8, :])
            moe(0)
            sum_squares(1, 0)
            pe.wait_ge(S["h_ready"], 3)
            for s in range(N_INO):
                w = slot(S_INO + s).rearrange("p (k n) -> p k n", k=DC)
                for t in range(NT):
                    b = fill("in", s, t)
                    filled(project("in", b[:, 0:384], lambda k: hT[:, k, TILE[t]], lambda k: w[:, k, :]))
                pe.drain().then_inc(S["slot_used"], 1)
            for t in range(NT):
                pe.wait_ge(S["qk_ready"], NT + 4 + 2 * t + 1)
                for k in range(2):
                    b = fill("gqT", t, k)
                    for c in range(4):
                        ins = pe.transpose(b[:, P * c:P * c + P], qkv3[:, t, 512 * k + P * c:512 * k + P * c + P], ident)
                    filled(ins)
                pe.wait_ge(S["qk_ready"], NT + 4 + 2 * t + 2)
                b = fill("gkT", t)
                for c in range(4):
                    ins = pe.transpose(b[:, P * c:P * c + P], gkt[:, P * c:P * c + P], ident)
                filled(ins)
            pe.wait_ge(S["qk_ready"], NT + 4 + 2 * NT + 1)
            b = fill("gkT", 3)
            for c in range(4):
                ins = pe.transpose(b[:, P * c:P * c + P], gkt[:, P * c:P * c + P], ident)
            filled(ins)
            pe.wait_ge(S["qkT_ready"], 2 * (NT + 4) + 3 * NT + 1)
            attention("gqa", HQ, lambda t, h: gqT3[64 * (h % 2):64 * (h % 2) + 64, h // 2, TILE[t]],
                      lambda h, k0, nk: gkT3[64 * (h % 2):64 * (h % 2) + 64, h // 4, k0:k0 + nk],
                      lambda s, h: (sm("v_cache")[:, 64 * (h // 4):64 * (h // 4) + 64] if s == 1 else
                                    qkv3[:, {0: 0, 2: 1, 3: 2}[s], 1280 + 64 * (h // 4):1280 + 64 * (h // 4) + 64]), gPb, gPTb, got)
            project_out(1, 8, (3, 3, 2), S_OUTO, lambda k: oT3[:, k, :])
            moe(1)

        @block.scalar
        def _(act):
            n_chain, n_taken = [0], [0]
            mine = [j for j, (_, by) in enumerate(jobs) if by == "A"]

            def link(ins):
                n_chain[0] += 1
                ins.then_inc(S["chain_act"], 1)
                act.wait_ge(S["chain_act"], n_chain[0])

            def take(*name):
                j = mine[n_taken[0]]
                assert jobs[j][0] == name, (jobs[j], name)
                act.wait_ge(S["job_done"], j + 1)
                n_taken[0] += 1
                return bank(j)

            def emptied_by(ins):
                ins.then_inc(S["free_act"], 1)

            def after(name):
                act.wait_ge(S["job_done"], index[name] + 1)

            A = act.activation

            def rsqrt(out, src, n, scale=1.0):
                link(A(out, src, ACT.Ln, bias=EPS, scale=1.0 / n))
                return A(out, out, ACT.Exp, bias=math.log(scale), scale=-0.5)

            act.dma_start(small[:, :], small_d).then_inc(S["in_small"], 16)
            act.dma_start(xT[:, :, :], x_d).then_inc(S["in_x"], 16)
            act.wait_ge(S["in_small"], 16)
            A(condS, sm("cond"), ACT.Silu).then_inc(S["cond_ready"], 1)

            def norm(l, i):
                if l == 0 and i == 0:
                    act.wait_ge(S["in_x"], 16)
                else:
                    act.wait_ge(S["x_new"], DC * (2 * l + i))
                A(hT, xT[:, :, :], ACT.Square).then_inc(S["sq_ready"], 1)
                b = take("ss", l, i)
                link(A(rn, b[:, 0:T], ACT.Ln, bias=EPS, scale=1.0 / D))
                A(rn, rn, ACT.Exp, scale=-0.5).then_inc(S["r_ready"], 1)
                act.wait_ge(S["r_ready"], 2 * l + i + 1)
                act.sem_inc(S["free_act"], 1)

            def attention(kind, heads, Pb, nm, rs, oT_of):
                base = 0 if kind == "mla" else NT * HM
                units = [(t, h) for t in range(NT) for h in range(heads)]
                for u, (t, h) in enumerate(units):
                    b = take(kind, "s", u)
                    act.wait_ge(S["max_ready"], base + u + 1)
                    if u >= 2:
                        after((kind, "pT", u - 2))
                    nk = KEYS[t][1]
                    A(Pb[:, 384 * (u % 2):384 * (u % 2) + nk], b[:, 0:nk], ACT.Exp, bias=nm[:, u:u + 1],
                      accum_out=rs[:, u:u + 1]).then_inc(S["p_ready"], 1)
                    act.wait_ge(S["p_ready"], base + u + 1)
                    act.sem_inc(S["free_act"], 1)
                    if h == 0 and t:
                        turned(kind, heads, t - 1, oT_of)
                turned(kind, heads, NT - 1, oT_of)

            def turned(kind, heads, t, oT_of):
                for k in range(heads // 8):
                    b = take(kind, "oT", t, k)
                    ins = act.copy(oT_of(t, k), b[:, 0:512].rearrange("p (c t) -> p c t", c=4))
                    emptied_by(ins)
                act.wait_ge(S["free_act"], emptied[index[(kind, "oT", t, heads // 8 - 1)]][1])
                act.sem_inc(S["o_ready"], 1)

            def qk_rsqrt(n_step, ss, n, scale):
                act.wait_ge(S["qk_sq"], n_step + 1)
                rsqrt(ss, ss, n, scale).then_inc(S["qk_r"], 1)

            def moe(l):
                norm(l, 1)
                b = take("rt", l)
                A(rt48[0], b[:, 0:48], ACT.Exp, scale=-1.0).then_inc(S["rt_exp"], 1)
                act.wait_ge(S["rt_exp"], l + 1)
                act.sem_inc(S["free_act"], 1)
                n_u = 4 * NT
                tot = NG * n_u * l
                with act.Fori(0, NG) as g:
                    def turned_act(v):
                        act.wait_ge(S["tr_done"], g * n_u + (tot + v + 1))
                        act.copy(actT[:, 256 * (v % 2):256 * (v % 2) + 256], ps[:, 2 + v % 2, 0:256]).then_inc(S["trc_ready"], 1)

                    for u in range(n_u):
                        act.wait_ge(S["au_done"], g * n_u + (tot + u + 1))
                        A(sil[:, 256 * (u % 2):256 * (u % 2) + 256], ps[:, u % 2, 0:256], ACT.Silu).then_inc(S["sil_ready"], 1)
                        if u:
                            turned_act(u - 1)
                    turned_act(n_u - 1)

            norm(0, 0)
            convb = sm("conv_b")

            def conv_silu(c):
                act.wait_ge(S["xc_raw"], c + 1)
                A(xc3[:, c, :], xc3[:, c, :], ACT.Silu, bias=convb[:, c:c + 1]).then_inc(S["xc_ready"], 1)

            act.wait_ge(S["h_ready"], 1)
            for c in range(CONV_C):
                b = take("xbc", c)
                if c >= 2:
                    act.wait_ge(S["xc_raw"], c - 1)
                else:
                    act.wait_ge(S["xr_used"], 1)
                act.copy(xr[c % 2][:, 1:129], b[:, 0:P])
                act.copy(xr[c % 2][:, 130:386], b[:, P:T]).then_inc(S["xr_ready"], 1)
                act.wait_ge(S["xr_ready"], c + 1)
                act.sem_inc(S["free_act"], 1)
                if c:
                    conv_silu(c - 1)
            conv_silu(CONV_C - 1)
            for i, (lo, w) in enumerate([(0, 256), (256, 384), (640, 384)]):
                for t in range(NT):
                    b = take("z", i, t)
                    A(zs3[:, t, lo:lo + w], b[:, 0:w], ACT.Silu).then_inc(S["z_ready"], 1)
                    act.wait_ge(S["z_ready"], 3 * i + t + 1)
                    act.sem_inc(S["free_act"], 1)
            act.wait_ge(S["e_in"], 1)
            A(e96[6][:, 0:32], sm("a_log"), ACT.Exp)
            link(A(e96[1], e96[1], ACT.Exp))
            A(e96[1], e96[1], ACT.Ln, bias=1.0).then_inc(S["e_mid"], 1)
            act.wait_ge(S["cum_copied"], 1)
            A(e96[5], e96[4], ACT.Exp, scale=-1.0)
            A(e96[9], e96[9], ACT.Exp)
            A(e96[8], e96[6], ACT.Exp).then_inc(S["e_cum"], 1)
            nfull = 0
            ssdn = sm("ssd_norm")
            for i, (t, full) in enumerate(STEPS):
                if i:
                    act.wait_ge(S["xtok_used"], i)
                for k in range(2):
                    b = take("xt", i, k)
                    emptied_by(act.copy(xtok[:, 512 * k:512 * k + 512], b[:, :]))
                b = take("bt", i)
                emptied_by(act.copy(Btok, b[:, 0:P]))
                act.wait_ge(S["free_act"], emptied[index[("bt", i)]][1])
                act.sem_inc(S["xtok_ready"], 1)
                if full:
                    for g in range(2):
                        b = take("g", i, g)
                        emptied_by(act.copy(Gs2[g], b[:, 0:P]))
                    act.wait_ge(S["free_act"], emptied[index[("g", i, 1)]][1])
                    act.sem_inc(S["g_ready"], 1)
                    for u in range(8):
                        act.wait_ge(S["seg_ready"], 8 * nfull + u + 1)
                        A(dec[u % 2], dec[u % 2], ACT.Exp).then_inc(S["dec_ready"], 1)
                    act.wait_ge(S["ysq_ready"], nfull + 1)
                    link(A(zs3[:, t, :], ytok, ACT.Square, accum_out=ssd_r))
                    rsqrt(ssd_r, ssd_r, D).then_inc(S["ynorm_ready"], 1)
                    for k in range(2):
                        b = take("yT", i, k)
                        for c in range(4):
                            ins = A(oTy3[:, 4 * k + c, TILE[t]], b[:, P * c:P * c + P], ACT.Copy, scale=ssdn[:, 4 * k + c:4 * k + c + 1])
                        emptied_by(ins)
                    nfull += 1
            for k, n in ((0, 2 * P), (1, P)):
                b = take("sl", k)
                link(A(lr[k], b[:, 0:T], ACT.Ln, bias=EPS, scale=1.0 / n))
                act.sem_inc(S["free_act"], 1)
                A(lr[k], lr[k], ACT.Exp, scale=-0.5).then_inc(S["lr_ready"], 1)
            mkt3 = mkt.rearrange("p (h n) -> p h n", h=HM)

            def turn_qk(name, i, out):
                for hh in range(2):
                    b = take(name, i, hh)
                    act.copy(out(hh), b[0:QM, :].rearrange("p (h n) -> p h n", h=4)).then_inc(S["qkT_ready"], 1)
                    act.wait_ge(S["qkT_ready"], 2 * (i + (NT if name == "kT" else 0)) + hh + 1)
                    act.sem_inc(S["free_act"], 1)

            for t in range(NT):
                for hh in range(2):
                    b = take("q", t, hh)
                    emptied_by(act.copy(mkt[:, 384 * hh:384 * hh + 384], b[:, 0:384]))
                act.wait_ge(S["free_act"], emptied[index[("q", t, 1)]][1])
                act.sem_inc(S["qt_copied"], 1)
                qk_rsqrt(t, mss, QM, QM ** -0.5)
                turn_qk("qT", t, lambda hh: mqT3[0:QM, 4 * hh:4 * hh + 4, TILE[t]])
            for s in range(4):
                for hh in range(2):
                    b = take("kv", s, hh)
                    b3 = b[:, :].rearrange("p (h n) -> p h n", h=4)
                    act.copy(mkt3[:, 4 * hh:4 * hh + 4, 0:NOPE], b3[:, :, 0:NOPE])
                    emptied_by(act.copy(mv3[:, KSLOT[s], 256 * hh:256 * hh + 256].rearrange("p (h n) -> p h n", h=4), b3[:, :, NOPE:P]))
                act.wait_ge(S["free_act"], emptied[index[("kv", s, 1)]][1])
                act.sem_inc(S["qt_copied"], 1)
                qk_rsqrt(NT + s, mss, QM, 1.0)
                turn_qk("kT", s, lambda hh: mkT3[0:QM, 4 * hh:4 * hh + 4, P * KSLOT[s]:P * KSLOT[s] + P])
            attention("mla", HM, mPb, mnm, mrs, lambda t, k: oTm3[:, :, TILE[t]])
            moe(0)
            norm(1, 0)
            for s in range(1, N_INO, 2):
                for t in range(NT):
                    b = take("in", s, t)
                    if s == 1 and t == 0:
                        act.wait_ge(S["xr_used"], 2)
                    act.copy(qkv3[:, t, 384 * s:384 * s + 384], b[:, 0:384]).then_inc(S["qkv_ready"], 1)
                    act.wait_ge(S["qkv_ready"], NT * (s // 2) + t + 1)
                    act.sem_inc(S["free_act"], 1)

            n_t = [2 * (NT + 4)]

            def turn_gqa(out, *name):
                b = take(*name)
                n_t[0] += 1
                act.copy(out, b[:, :].rearrange("p (h n) -> p h n", h=4)).then_inc(S["qkT_ready"], 1)
                act.wait_ge(S["qkT_ready"], n_t[0])
                act.sem_inc(S["free_act"], 1)

            for t in range(NT):
                qk_rsqrt(NT + 4 + 2 * t, gss[:, 0:HQ], HD, HD ** -0.5)
                for k in range(2):
                    turn_gqa(gqT3[:, 4 * k:4 * k + 4, TILE[t]], "gqT", t, k)
                qk_rsqrt(NT + 4 + 2 * t + 1, gss[:, 0:HKV], HD, 1.0)
                turn_gqa(gkT3[:, :, P * KSLOT[t]:P * KSLOT[t] + P], "gkT", t)
            turn_gqa(gkT3[:, :, P * KSLOT[3]:P * KSLOT[3] + P], "gkT", 3)
            attention("gqa", HQ, gPb, gnm, grs, lambda t, k: oT3[:, 4 * k:4 * k + 4, TILE[t]])
            moe(1)

        @block.vector
        def _(dve):
            n_chain, n_taken = [0], [0]
            mine = [j for j, (_, by) in enumerate(jobs) if by == "D"]

            def link(ins):
                n_chain[0] += 1
                ins.then_inc(S["chain_dve"], 1)
                dve.wait_ge(S["chain_dve"], n_chain[0])

            def take(*name):
                j = mine[n_taken[0]]
                assert jobs[j][0] == name, (jobs[j], name)
                dve.wait_ge(S["job_done"], j + 1)
                n_taken[0] += 1
                return bank(j)

            def emptied_by(ins):
                ins.then_inc(S["free_dve"], 1)

            def after(*name):
                dve.wait_ge(S["job_done"], index[name] + 1)

            tt, ts, stt = dve.tensor_tensor, dve.tensor_scalar, dve.scalar_tensor_tensor

            def spread(ap, n):
                return ap.unsqueeze(2).broadcast_to([ap.shape[0], ap.shape[1], n])

            def over(ap, n):
                return ap.unsqueeze(1).broadcast_to([ap.shape[0], n, ap.shape[1]])

            def cut(ap, n):
                return ap.rearrange("p (h n) -> p h n", h=n)

            def modulation(l):
                dve.wait_ge(S["ada_done"], l + 1)
                b_ada = sm("b_ada")[:, 48 * l:48 * l + 48]
                tt(mod[l].rearrange("p (c n) -> p c n", n=2), ps[:, 7, 0:96].rearrange("p (c n) -> p c n", n=2),
                   spread(b_ada, 2), ADD).then_inc(S["mod_ready"], 1)
                dve.wait_ge(S["mod_ready"], l + 1)

            def norm(l, i):
                g = sm("g_ffn" if i else "g_mix")[:, DC * l:DC * l + DC]
                sc = mod[l][:, 16 * (3 * i + 1):16 * (3 * i + 2)]
                sh = mod[l][:, 16 * 3 * i:16 * (3 * i + 1)]
                ab = AB[:, 16 * i:16 * i + 16]
                link(stt(cut(ab, 8), cut(sc, 8), 1.0, spread(g, 2), ADD, MUL))
                dve.wait_ge(S["r_ready"], 2 * l + i + 1)
                if l == 0 and i == 0:
                    dve.wait_ge(S["in_x"], 16)
                link(tt(hT, xT[:, :, :], rn.unsqueeze(1).broadcast_to([P, DC, T]), MUL))
                for c in range(DC):
                    for s in range(2):
                        ins = ts(hT[:, c, SEG[s]], hT[:, c, SEG[s]], ab[:, 2 * c + s:2 * c + s + 1], sh[:, 2 * c + s:2 * c + s + 1], MUL, ADD)
                ins.then_inc(S["h_ready"], 1)

            def residual(l, part, name):
                gt = mod[l][:, 16 * part:16 * part + 16]
                for c in range(DC):
                    b = take(name, l, c)
                    for s in range(2):
                        ins = stt(xT[:, c, SEG[s]], b[:, SEG[s]], gt[:, 2 * c + s:2 * c + s + 1], xT[:, c, SEG[s]], MUL, ADD)
                    ins.then_inc(S["x_new"], 1)
                    dve.wait_ge(S["x_new"], DC * (2 * l + (part == 5)) + c + 1)
                    dve.sem_inc(S["free_dve"], 1)

            def rope(x, cos, sin, tmp, nh, n):
                q = n // 4
                x5 = x.rearrange("p h (a f n) -> p h a f n", a=2, f=2)
                t5 = tmp.rearrange("p h (a f n) -> p h a f n", a=2, f=2)
                s4 = sin.rearrange("p (a f n) -> p a f n", a=2, f=2)
                for a in range(2):
                    for f in range(2):
                        ins = tt(t5[:, :, a, f, :], x5[:, :, a, 1 - f, :], over(s4[:, a, f, :], nh), MUL)
                link(ins)
                link(tt(x, x, over(cos, nh), MUL))
                link(tt(x, x, tmp, ADD))

            def qk_norm(n_step, x, nh, n, gain, ss, tmp, cos, sin, rope_at):
                link(tt(tmp, x, x, MUL))
                dve.tensor_reduce(ss, tmp, AX.X, ADD).then_inc(S["qk_sq"], 1)
                dve.wait_ge(S["qk_r"], n_step + 1)
                link(tt(x, x, spread(ss, n), MUL))
                link(tt(x, x, over(gain, nh), MUL))
                if cos is not None:
                    rope(x[:, :, rope_at:n], cos, sin, tmp[:, :, rope_at:n], nh, n - rope_at)

            def attention(kind, heads, nm, rs, Pb, PTb, ot):
                base = 0 if kind == "mla" else NT * HM
                units = [(t, h) for t in range(NT) for h in range(heads)]

                def row_max(u):
                    after(kind, "s", u)
                    j = index[(kind, "s", u)]
                    dve.tensor_reduce(nm[:, u:u + 1], bank(j)[:, 0:KEYS[units[u][0]][1]], AX.X, MAX, negate=True).then_inc(S["max_ready"], 1)

                row_max(0)
                for u, (t, h) in enumerate(units):
                    nk = KEYS[t][1]
                    if u + 1 < len(units):
                        row_max(u + 1)
                    b = take(kind, "pT", u)
                    if u >= 2:
                        dve.wait_ge(S["pv_done"], base + u - 1)
                    dve.tensor_copy(PTb[:, 384 * (u % 2):384 * (u % 2) + nk], b[:, 0:nk]).then_inc(S["pt_ready"], 1)
                    dve.wait_ge(S["pt_ready"], base + u + 1)
                    dve.sem_inc(S["free_dve"], 1)
                    if h == heads - 1:
                        r = rs[:, heads * t:heads * t + heads]
                        dve.wait_ge(S["pv_done"], base + u + 1)
                        link(dve.reciprocal(r, r))
                        if t:
                            after(kind, "oT", t - 1, heads // 8 - 1)
                        for k in range(heads // 8):
                            ins = tt(cut(ot[:, 512 * k:512 * k + 512], 8), cut(ps[:, 5 + k, :], 8), spread(r[:, 8 * k:8 * k + 8], 64), MUL)
                        ins.then_inc(S["o_tok"], 1)

            def gates_of(l):
                fw = sm("first_wins")
                s, sel, msel, key, oh1, ms2, oh2 = rt48[1], rt48[2], rt48[3], rt48[4], rt48[5], rt48[6], rt48[7]
                cut3 = lambda ap: ap.rearrange("p (t n) -> p t n", t=NT)
                link(ts(s, rt48[0], 1.0, None, ADD))
                link(dve.reciprocal(s, s))
                link(tt(cut3(sel), cut3(s), over(sm("router_bias"), NT), ADD))
                v = sel.rearrange("p (q n) -> p q n", n=GS)
                a, b_, c, d = (v[:, :, i] for i in range(4))
                link(tt(rt12[0], a, b_, MAX))
                link(tt(rt12[1], a, b_, MIN))
                link(tt(rt12[2], c, d, MAX))
                link(tt(rt12[3], c, d, MIN))
                link(tt(rt12[4], rt12[0], rt12[2], MAX))
                link(tt(rt12[5], rt12[0], rt12[2], MIN))
                link(tt(rt12[6], rt12[1], rt12[3], MAX))
                link(tt(rt12[7], rt12[5], rt12[6], MAX))
                link(tt(rt12[8], rt12[4], rt12[7], ADD))

                def pick(out, src, n, weights, m):
                    link(dve.tensor_reduce(m[0], cut3(src), AX.X, MAX))
                    link(tt(cut3(out), cut3(src), spread(m[0], n), EQ))
                    link(tt(cut3(out), cut3(out), over(weights, NT), MUL))
                    link(dve.tensor_reduce(m[1], cut3(out), AX.X, MAX))
                    link(tt(cut3(out), cut3(out), spread(m[1], n), EQ))

                pick(rt12[9], rt12[8], NG, fw[:, 0:NG], rt3[0:2])
                link(tt(msel.rearrange("p (q n) -> p q n", n=GS), v, spread(rt12[9], GS), MUL))
                link(ts(rt12[10], rt12[9], -1.0, BIG, ADD, MUL))
                link(tt(msel.rearrange("p (q n) -> p q n", n=GS), msel.rearrange("p (q n) -> p q n", n=GS), spread(rt12[10], GS), ADD))
                pick(oh1, msel, NE, fw[:, NG:], rt3[2:4])
                link(stt(ms2, oh1, -3 * BIG, msel, MUL, ADD))
                pick(oh2, ms2, NE, fw[:, NG:], rt3[4:6])
                link(tt(oh1, oh1, oh2, ADD))
                link(tt(oh1, oh1, s, MUL))
                link(dve.tensor_reduce(rt3[6], cut3(oh1), AX.X, ADD))
                link(dve.reciprocal(rt3[7], rt3[6]))
                link(tt(cut3(gates), cut3(oh1), spread(rt3[7], NE), MUL))
                dve.sem_inc(S["gates_ready"], 1)

            def moe(l):
                norm(l, 1)
                if l:
                    for n in ("gk", "gv"):
                        dve.wait_ge(outs[n], 16)
                dve.wait_ge(S["rt_exp"], l + 1)
                gates_of(l)
                link(dve.memset(yacc, 0.0))
                n_u = 4 * NT
                tot = NG * n_u * l
                gates3 = gates.rearrange("p (t e) -> p t e", t=NT)
                with dve.Fori(0, NG) as g:
                    def add(v):
                        t = v % NT
                        dve.wait_ge(S["dn_done"], g * n_u + (tot + v + 1))
                        tt(yacc3[:, t, :].rearrange("p (k n) -> p k n", k=2), yacc3[:, t, :].rearrange("p (k n) -> p k n", k=2),
                           ps[:, 4 + 2 * (v % 2):6 + 2 * (v % 2), :], ADD).then_inc(S["acc_ready"], 1)

                    dve.tensor_copy(gcur.rearrange("p (t e) -> p t e", t=NT), gates3[:, :, bass.ds(g * GS, GS)]).then_inc(S["gcur_ready"], 1)
                    dve.wait_ge(S["gcur_ready"], g + (NG * l + 1))
                    for u in range(n_u):
                        e, t = u // NT, u % NT
                        if u >= 3:
                            dve.wait_ge(S["acc_ready"], g * n_u + (tot + u - 1))
                        dve.wait_ge(S["sil_ready"], g * n_u + (tot + u + 1))
                        stt(act_b[:, 256 * (u % 2):256 * (u % 2) + 256], ps[:, u % 2, 256:512], gcur[:, GS * t + e:GS * t + e + 1],
                            sil[:, 256 * (u % 2):256 * (u % 2) + 256], MUL, MUL).then_inc(S["act_ready"], 1)
                        if u:
                            add(u - 1)
                    add(n_u - 1)
                residual(l, 5, "moe")

            dve.wait_ge(S["in_small"], 16)
            modulation(0)
            norm(0, 0)
            dve.wait_ge(S["h_ready"], 1)
            for i in range(2):
                for c in (0, 129, 386):
                    link(dve.memset(xr[i][:, c:c + 1], 0.0))
            dve.sem_inc(S["xr_used"], 1)
            b = take("dk")
            emptied_by(dve.tensor_copy(dk, b[:, 0:144]))
            dve.wait_ge(S["free_dve"], 1)
            dve.sem_inc(S["dk_copied"], 1)
            cw = sm("conv_w")
            for c in range(CONV_C):
                dve.wait_ge(S["xr_ready"], c + 1)
                r, o = xr[c % 2], xc3[:, c, :]
                link(ts(o, r[:, 1:386], cw[:, CONV_C + c:CONV_C + c + 1], None, MUL))
                link(stt(o, r[:, 0:385], cw[:, c:c + 1], o, MUL, ADD))
                stt(o, r[:, 2:387], cw[:, 2 * CONV_C + c:2 * CONV_C + c + 1], o, MUL, ADD).then_inc(S["xc_raw"], 1)
            for c in range(3):
                b = take("lat", c)
                emptied_by(dve.tensor_copy(latT[:, c, :], b[:, 0:T]))
            def by_tile(ap, d):
                return ap[:, 48 * d:48 * d + 48].rearrange("p (t n) -> p t n", t=NT)

            for d in range(2):
                link(tt(by_tile(e96[0], d), dk3[:, :, 0:HS], over(sm("dt_bias")[:, HS * d:HS * d + HS], NT), ADD))
            link(ts(e96[1], e96[0], -1.0, None, MUL))
            tt(e96[1], e96[0], e96[1], MIN).then_inc(S["e_in"], 1)
            dve.wait_ge(S["e_mid"], 1)
            link(stt(e96[2], e96[0], 0.0, e96[1], MAX, ADD))
            for d in range(2):
                link(stt(by_tile(e96[3], d), by_tile(e96[2], d), -1.0, over(e96[6][:, HS * d:HS * d + HS], NT), MUL, MUL))
            dve.sem_inc(S["dt_ready"], 1)
            b = take("cum")
            emptied_by(ts(e96[4], b[:, 0:96], -1.0, None, MUL))
            dve.wait_ge(S["free_dve"], emptied[index[("cum",)]][1])
            b = take("tot")
            link(tt(e96[9], b[:, 0:96], e96[4], ADD))
            emptied_by(dve.tensor_copy(e96[6], b[:, 0:96]))
            dve.wait_ge(S["free_dve"], emptied[index[("tot",)]][1])
            dve.sem_inc(S["cum_copied"], 1)
            dve.wait_ge(S["e_cum"], 1)
            link(tt(e96[7], e96[2], e96[9], MUL))
            nfull = 0
            for i, (t, full) in enumerate(STEPS):
                dve.wait_ge(S["xtok_ready"], i + 1)
                col = lambda d: slice(48 * d + HS * t, 48 * d + HS * t + HS)
                if full:
                    base = 8 * nfull
                    for d in range(2):
                        link(tt(cut(xdt[d], HS), cut(xtok, HS), spread(e96[2][:, col(d)], PS), MUL))

                    def segment(u):
                        q, d = u // 2, u % 2
                        b = take("bc", i, u)
                        if u >= 2:
                            dve.wait_ge(S["diag_done"], base + u - 1)
                        for h in range(4):
                            c = 48 * d + HS * t + 4 * q + h
                            ins = stt(dec[d][:, P * h:P * h + P], b[:, P * h:P * h + P], e96[4][:, c:c + 1], mask[d], ADD, ADD)
                        ins.then_inc(S["seg_ready"], 1)
                        dve.wait_ge(S["seg_ready"], base + u + 1)
                        dve.sem_inc(S["free_dve"], 1)

                    def scores(u):
                        q, d = u // 2, u % 2
                        dve.wait_ge(S["dec_ready"], base + u + 1)
                        if u == 0:
                            dve.wait_ge(S["g_ready"], nfull + 1)
                        tt(cut(dec[d], 4), cut(dec[d], 4), over(Gs2[q // 2], 4), MUL).then_inc(S["s_ready"], 1)

                    segment(0)
                    for u in range(8):
                        if u + 1 < 8:
                            segment(u + 1)
                        scores(u)
                    dve.wait_ge(S["diag_done"], base + 8)
                    link(tt(cut(ytok, HS), cut(xtok, HS), spread(sm("d_skip"), PS), MUL))
                    link(tt(ytok, ytok, ps[:, 5:7, :].rearrange("p a n -> p (a n)"), ADD))
                    if t:
                        for d in range(2):
                            for g in range(2):
                                b = take("off", i, d, g)
                                link(tt(cut(ytmp, 8), cut(b[:, 0:512], 8), spread(e96[5][:, 48 * d + HS * t + 8 * g:48 * d + HS * t + 8 * g + 8], PS), MUL))
                                dve.sem_inc(S["free_dve"], 1)
                                link(tt(ytok[:, 512 * g:512 * g + 512], ytok[:, 512 * g:512 * g + 512], ytmp, ADD))
                    dve.wait_ge(S["z_ready"], 3 * NT)
                    tt(ytok, ytok, zs3[:, t, :], MUL).then_inc(S["ysq_ready"], 1)
                    dve.wait_ge(S["ynorm_ready"], nfull + 1)
                    ts(ytok, ytok, ssd_r[:, 0:1], None, MUL).then_inc(S["ynormed"], 1)
                    after("yT", i, 1)
                    nfull += 1
                for d in STATES[i]:
                    link(tt(cut(xw, HS), cut(xtok, HS), spread(e96[7][:, col(d)], PS), MUL))
                    dve.sem_inc(S["xw_ready"], 1)
                    b = take("st", i, d)
                    for g in range(2):
                        r = slice(64 * g, 64 * g + 64)
                        dst = {(2, 1): s_b1, (1, 0): h0[0], (0, 0): h0[0], (0, 1): h0[1]}[t, d]
                        if t == 0:
                            ins = dve.tensor_copy(dst[r, :], b[r, :])
                        else:
                            cd = e96[8][r, 48 * d + HS * t + 8 * g:48 * d + HS * t + 8 * g + 8]
                            link(tt(cut(dst[r, :], 8), cut(h0[d][r, :], 8), spread(cd, PS), MUL))
                            ins = tt(dst[r, :], dst[r, :], b[r, :], ADD)
                        link(ins)
                    dve.sem_inc(S["free_dve"], 1)
                    dve.sem_inc(S["st_done"], 1)
                dve.sem_inc(S["xtok_used"], 1)
            tt(lsq, lat, lat, MUL).then_inc(S["lsq_ready"], 1)
            dve.wait_ge(S["lr_ready"], 2)
            for c in range(3):
                g = sm("q_a_norm")[:, c:c + 1] if c < 2 else sm("kv_a_norm")
                ins = stt(latT[:, c, :], latT[:, c, :], g, lr[c // 2], MUL, MUL)
            ins.then_inc(S["latn_ready"], 1)
            mkt3, msq3 = cut(mkt, HM), cut(msq, HM)
            rot = lambda n, t, w: sm(n)[:, w * (t - 1):w * t]
            for k in range(NT + 4):
                s = k - NT
                dve.wait_ge(S["qt_copied"], k + 1)
                if s >= 0:
                    kpe = dk3[:, s, HS:48] if s < NT else sm("kpe_cache")
                    link(dve.tensor_copy(mkt3[:, :, NOPE:QM], over(kpe, HM)))
                t = k if s < 0 else s
                on = t in (1, 2)
                qk_norm(k, mkt3, HM, QM, sm("q_norm" if s < 0 else "k_norm"), mss, msq3,
                        rot("cos_e", t, ROPE) if on else None, rot("sin_e", t, ROPE) if on else None, NOPE)
                dve.sem_inc(S["qk_ready"], 1)
            attention("mla", HM, mnm, mrs, mPb, msq, mot)
            modulation(1)
            residual(0, 2, "out")
            moe(0)
            norm(1, 0)
            for n in ("ckv", "kpe", "stf", "stb"):
                dve.wait_ge(outs[n], 16)
            dve.sem_inc(S["xr_used"], 1)
            for s in range(0, N_INO, 2):
                for t in range(NT):
                    b = take("in", s, t)
                    emptied_by(dve.tensor_copy(qkv3[:, t, 384 * s:384 * s + 384], b[:, 0:384]))
            dve.wait_ge(S["free_dve"], emptied[index[("in", 2, NT - 1)]][1])
            dve.wait_ge(S["qkv_ready"], 2 * NT)
            step = NT + 4
            for t in range(NT):
                for x, nh, g in ((qkv3[:, t, 0:1024], HQ, "gq_norm"), (qkv3[:, t, 1024:1280], HKV, "gk_norm")):
                    qk_norm(step, cut(x, nh), nh, HD, sm(g), gss[:, 0:nh], cut(gsq[:, 0:HD * nh], nh),
                            rot("cos_o", t, HD) if t else None, rot("sin_o", t, HD) if t else None, 0)
                    if nh == HKV:
                        if t:
                            after("gkT", t - 1)
                        for i in range(2):
                            link(dve.tensor_copy(cut(gkt, HKV)[:, :, 64 * i:64 * i + 64], cut(x, HKV)))
                    dve.sem_inc(S["qk_ready"], 1)
                    step += 1
            after("gkT", NT - 1)
            for i in range(2):
                link(dve.tensor_copy(cut(gkt, HKV)[:, :, 64 * i:64 * i + 64], cut(sm("k_cache"), HKV)))
            dve.sem_inc(S["qk_ready"], 1)
            attention("gqa", HQ, gnm, grs, gPb, gPTb, got)
            residual(1, 2, "out")
            moe(1)

        @block.gpsimd
        def _(pool):
            pool.wait_ge(S["dk_copied"], 1)
            pool.dma_start(kpe_d, dk3[:, 0, HS:48]).then_inc(outs["kpe"], 16)
            pool.wait_ge(S["st_done"], 4)
            pool.dma_start(stf_d, h0[0]).then_inc(outs["stf"], 16)
            pool.dma_start(stb_d, h0[1]).then_inc(outs["stb"], 16)
            pool.wait_ge(S["latn_ready"], 1)
            pool.dma_start(ckv_d, latT[:, 2, 0:P]).then_inc(outs["ckv"], 16)
            pool.wait_ge(S["qk_ready"], NT + 4 + 2)
            pool.dma_start(gk_d, qkv3[:, 0, 1024:1280]).then_inc(outs["gk"], 16)
            pool.dma_start(gv_d, qkv3[:, 0, 1280:1536]).then_inc(outs["gv"], 16)


def _constants():
    f = np.float32
    j, i = np.arange(P)[:, None], np.arange(P)[None, :]
    c = {"ident": (i == j).astype(f), "ones": np.ones((P, P), f),
         "tri_f": (j <= i).astype(f), "tri_b": (j >= i).astype(f),
         "mask_f": np.where(j <= i, f(0), f(-BIG)), "mask_b": np.where(j >= i, f(0), f(-BIG)),
         "first_wins": np.tile(np.concatenate([np.arange(NG, 0, -1), np.arange(NE, 0, -1)]).astype(f), (P, 1))}
    tok = np.arange(2 * P)
    for name, n in (("e", ROPE), ("o", HD)):
        half = n // 4
        inv = np.power(f(THETA), -np.arange(half, dtype=f) / f(half)).astype(f)
        cos, sin = [], []
        for pos in (tok // GRID_W, tok % GRID_W):
            ang = pos.astype(f)[:, None] * inv[None, :]
            cos += [np.cos(ang)] * 2
            sin += [-np.sin(ang), np.sin(ang)]
        for kind, parts in (("cos_", cos), ("sin_", sin)):
            a = np.concatenate(parts, axis=1).astype(f)
            c[kind + name] = a.reshape(2, P, n).transpose(1, 0, 2).reshape(P, 2 * n)
    return c


def _chunks(v):
    v = np.asarray(v)
    return np.ascontiguousarray(v.reshape(-1, P).T)


def _rows(v):
    return np.tile(np.asarray(v).reshape(1, -1), (P, 1))


def _kxn(w, cols):
    k, n = w.shape
    a = w.reshape(k // P, P, n // cols, cols).transpose(2, 1, 0, 3)
    return a.reshape(n // cols, P, -1)


def kernel(**inputs):
    import concourse.bacc as bacc
    from concourse.bass_utils import run_bass_kernel_spmd

    a = {k: np.asarray(v) for k, v in inputs.items()}
    w_in = a["w_in_even"][0]
    z, xbc, dt, ql, kv = np.split(w_in, (1024, 2304, 2320, 2576), axis=1)
    c = _constants()
    state = lambda s: s[0, 0].reshape(2, HG, PS, NS).transpose(0, 3, 1, 2).reshape(P, HG * PS)
    c.update(g_mix=_chunks(a["g_mix"]), g_ffn=_chunks(a["g_ffn"]), b_ada=_chunks(a["b_ada"]),
             conv_w=_chunks(a["ssd_conv_w"]), conv_b=_chunks(a["ssd_conv_b"]), ssd_norm=_chunks(a["ssd_norm"]),
             q_a_norm=_chunks(a["mla_q_a_norm"]), kv_a_norm=_chunks(a["mla_kv_a_norm"]),
             cond=np.stack([a["c_ctx"].reshape(DC, P), a["c"].reshape(DC, P)], axis=-1).transpose(1, 0, 2).reshape(P, 2 * DC),
             q_norm=_rows(a["mla_q_norm"]), k_norm=_rows(a["mla_k_norm"]), gq_norm=_rows(a["gqa_q_norm"]), gk_norm=_rows(a["gqa_k_norm"]),
             router_bias=_rows(a["router_bias"]),
             a_log=_rows(np.concatenate([a["ssd_a_log_fwd"][0], a["ssd_a_log_bwd"][0]])),
             dt_bias=_rows(np.concatenate([a["ssd_dt_bias_fwd"][0], a["ssd_dt_bias_bwd"][0]])),
             d_skip=_rows(a["ssd_d"]), ckv_cache=a["cache_mla_ckv"][0, 0].T, kpe_cache=a["cache_mla_kpe"][0, 0],
             k_cache=a["cache_gqa_k"][0, 0].reshape(P, -1), v_cache=a["cache_gqa_v"][0, 0].reshape(P, -1),
             h0=np.concatenate([state(a["state_ssd_fwd"]), state(a["state_ssd_bwd"])], axis=1),
             w_router=_kxn(a["w_router"], NE)[0], w_dk=_kxn(np.concatenate([dt, kv[:, P:]], axis=1), 48)[0],
             w_q_b=_kxn(a["mla_w_q_b"][0], 768)[0], w_kv_b=a["mla_w_kv_b"][0])
    small = np.concatenate([c[n].reshape(P, w) for n, w in SMALL], axis=1)

    slots = np.zeros((N_SLOTS, P, SLOT), w_in.dtype)
    for l, at in ((0, S_ADA0), (1, S_ADA1)):
        slots[at:at + N_ADA] = _kxn(a["w_ada"][l], 384)
    slots[S_INE:S_INE + N_INE] = _kxn(np.concatenate([xbc, ql, kv[:, :P], z], axis=1), 384)
    slots[S_OUTE:S_OUTE + N_OUTE] = _kxn(a["w_out_even"][0], 256)
    slots[S_INO:S_INO + N_INO] = _kxn(a["w_in_odd"][0], 384)
    wo = a["w_out_odd"][0]
    slots[S_OUTO:S_OUTO + 2] = _kxn(wo[:, :768], 384)
    slots[S_OUTO + 2, :, :2048] = _kxn(wo[:, 768:], 256)[0]
    for l, at in ((0, S_MOE0), (1, S_MOE1)):
        gu = np.concatenate([a["w_exp_gate"][l], a["w_exp_up"][l]], axis=2).reshape(NE, DC, P, 2 * FE).transpose(0, 2, 1, 3).reshape(NE, P, -1)
        dn = a["w_exp_down"][l].reshape(NE, 2, P, D).transpose(0, 2, 1, 3).reshape(NE, P, -1)
        slots[at:at + N_MOE] = np.concatenate([gu, dn], axis=2).reshape(NE, P, 2, SLOT).transpose(0, 2, 1, 3).reshape(N_MOE, P, SLOT)
    x = np.concatenate([a["x_prompt"][0], a["x_sample"][0]], axis=0)
    xt = np.ascontiguousarray(x.reshape(T, DC, P).transpose(2, 1, 0))

    nc = bacc.Bacc("TRN2", target_bir_lowering=False, num_devices=1)
    arrays = {"small_in": np.ascontiguousarray(small), "x_in": xt, "w_in": slots}
    ins = [nc.dram_tensor(n, v.shape, mybir.dt.from_np(v.dtype), kind="ExternalInput").ap() for n, v in arrays.items()]
    shapes = {"y_out": (P, DC, T), "stf_out": (P, HG * PS), "stb_out": (P, HG * PS), "ckv_out": (P, P), "kpe_out": (P, ROPE),
              "gk_out": (P, HKV * HD), "gv_out": (P, HKV * HD)}
    res = [nc.dram_tensor(n, s, mybir.dt.float32, kind="ExternalOutput").ap() for n, s in shapes.items()]
    build(nc, *ins, *res)
    r = run_bass_kernel_spmd(nc, [arrays], core_ids=[0]).results[0]
    y = np.asarray(r["y_out"]).transpose(2, 1, 0).reshape(T, D)
    unstate = lambda s: np.ascontiguousarray(np.asarray(s).reshape(2, NS, HG, PS).transpose(0, 2, 3, 1).reshape(1, 1, HS, PS, NS))
    return (np.ascontiguousarray(y[:P])[None], np.ascontiguousarray(y[P:])[None], unstate(r["stf_out"]), unstate(r["stb_out"]),
            np.ascontiguousarray(np.asarray(r["ckv_out"]).T)[None, None], np.asarray(r["kpe_out"])[None, None],
            np.asarray(r["gk_out"]).reshape(1, 1, P, HKV, HD), np.asarray(r["gv_out"]).reshape(1, 1, P, HKV, HD))
```

```python
import math
from contextlib import ExitStack

import numpy as np

import concourse.bass as bass
from concourse import mybir

P = 128
D = 1024
DC = D // P
T = 384
NT = T // P
DEPTH = 2
EPS = 1e-6
HS, PS, NS = 16, 64, 64
HG = HS // 2
HM, NOPE, ROPE, VM = 8, 64, 32, 64
QM = NOPE + ROPE
HQ, HKV, HD = 16, 4, 64
NE, NG, GS, FE = 16, 4, 4, 256
GRID_W = 64
THETA = 10000.0
CONV_C = 10
SLOT = 3072
RING = 8
N_ADA, N_INE, N_OUTE, N_MOE, N_INO, N_OUTO = 16, 7, 4, 32, 4, 3
S_ADA0 = 0
S_INE = S_ADA0 + N_ADA
S_ADA1 = S_INE + N_INE
S_OUTE = S_ADA1 + N_ADA
S_MOE0 = S_OUTE + N_OUTE
S_INO = S_MOE0 + N_MOE
S_OUTO = S_INO + N_INO
S_MOE1 = S_OUTO + N_OUTO
N_SLOTS = S_MOE1 + N_MOE
BIG = 1e30

SMALL = [("ident", P), ("ones", P), ("tri_f", P), ("tri_b", P), ("mask_f", P), ("mask_b", P),
         ("cos_e", 2 * ROPE), ("sin_e", 2 * ROPE), ("cos_o", 2 * HD), ("sin_o", 2 * HD),
         ("g_mix", DEPTH * DC), ("g_ffn", DEPTH * DC), ("b_ada", DEPTH * 48), ("conv_w", 3 * CONV_C), ("conv_b", CONV_C),
         ("ssd_norm", DC), ("q_a_norm", 2), ("kv_a_norm", 1), ("cond", 2 * DC),
         ("q_norm", QM), ("k_norm", QM), ("gq_norm", HD), ("gk_norm", HD), ("router_bias", NE),
         ("a_log", 2 * HS), ("dt_bias", 2 * HS), ("d_skip", HS), ("first_wins", NG + NE),
         ("slots", P), ("ckv_cache", P), ("kpe_cache", ROPE), ("k_cache", HKV * HD), ("v_cache", HKV * HD), ("h0", 2 * HG * PS),
         ("w_router", DC * NE), ("w_dk", DC * 48), ("w_q_b", 2 * HM * QM), ("w_kv_b", HM * (NOPE + VM))]
OFF, _at = {}, 0
for _n, _w in SMALL:
    OFF[_n] = (_at, _w)
    _at += _w
N_SMALL = _at


def build(nc, small_d, x_d, w_d, y_d, stf_d, stb_d, ckv_d, kpe_d, gk_d, gv_d):
    f32 = mybir.dt.float32
    ALU = mybir.AluOpType
    ACT = mybir.ActivationFunctionType
    AX = mybir.AxisListType
    MUL, ADD, SUB, MAX, MIN, EQ = ALU.mult, ALU.add, ALU.subtract, ALU.max, ALU.min, ALU.is_equal

    ctx = ExitStack()
    with ctx:
        sb = lambda name, n: ctx.enter_context(nc.sbuf_tensor(name, [P, n], f32))
        sem = lambda name: ctx.enter_context(nc.semaphore(name))
        ring = ctx.enter_context(nc.sbuf_tensor("ring", [P, RING, SLOT], f32))
        xT = ctx.enter_context(nc.sbuf_tensor("xT", [P, DC, T], f32))
        hTt = sb("hT", DC * T)
        small = sb("small", N_SMALL)
        misc = sb("misc", 256)
        U_SIZE = 15110
        U = sb("U", U_SIZE)
        ps = ctx.enter_context(nc.psum_tensor("ps", [P, 8, 512], f32))

        hT = hTt[:, :].rearrange("p (c t) -> p c t", c=DC)

        def sm(name):
            o, w = OFF[name]
            return small[:, o:o + w]

        ident, ones = sm("ident"), sm("ones")
        tri = [sm("tri_f"), sm("tri_b")]
        mask = [sm("mask_f"), sm("mask_b")]

        def region(base, *widths):
            out, at = [], base
            for w in widths:
                out.append(U[:, at:at + w])
                at += w
            assert at <= U_SIZE, at
            return out

        mod = [misc[:, 0:96], misc[:, 96:192]]
        condS = misc[:, 192:208]
        AB = misc[:, 208:240]
        ssd_r = misc[:, 240:241]
        zs, xc, oTy, oTm, lat, dk, e_sm = region(0, 3072, CONV_C * 385, 3072, 1536, 1152, 144, 1000)
        TAIL = 3072 + CONV_C * 385 + 3072 + 1536 + 1152 + 144 + 1000
        rn, _, sq_acc = region(TAIL, 384, 116, 384)
        mod_row = [U[0:2, TAIL + 896:TAIL + 1280], U[0:2, TAIL:TAIL + 384]]
        xr = [region(TAIL + 387 * i, 387)[0] for i in range(2)]
        zs3 = zs.rearrange("p (t n) -> p t n", t=NT)
        xc3 = xc.rearrange("p (c t) -> p c t", c=CONV_C)
        oTy3 = oTy.rearrange("p (c t) -> p c t", c=8)
        oTm3 = oTm.rearrange("p (c t) -> p c t", c=4)
        latT = lat.rearrange("p (c t) -> p c t", c=3)
        dk3 = dk.rearrange("p (t n) -> p t n", t=NT)
        e96 = [e_sm[:, 96 * i:96 * i + 96] for i in range(10)]
        xdt = [hTt[:, 0:1024], hTt[:, 1024:2048]]
        xtok = hTt[:, 2048:3072]
        dec = [oTm[:, 0:512], oTm[:, 512:1024]]
        xw = ytok = oTm[:, 0:1024]
        ytmp = oTm[:, 1024:1536]
        s_b1, Gs, Btok = region(TAIL, 512, 256, 128)
        h0 = [sm("h0")[:, 0:512], sm("h0")[:, 512:1024]]
        Gs2 = [Gs[:, 0:128], Gs[:, 128:256]]
        mkT, mv = region(0, HM * 512, 4 * HM * VM)
        mkT3 = mkT.rearrange("p (h n) -> p h n", h=HM)
        mv3 = mv.rearrange("p (s n) -> p s n", s=4)
        mqT3 = hTt[:, :].rearrange("p (h n) -> p h n", h=HM)
        msq = e_sm[:, 0:768]
        mss = e_sm[:, 768:776]
        mkt, = region(TAIL, HM * QM)
        m_att = region(3072 + CONV_C * 385 + 3072 + 1536, 4 * 384, 2 * 896, 24, 24)
        lsq = hTt[:, 0:1152]
        lr = [mkT[:, 0:384], mkT[:, 384:768]]
        qkv, gkT, oT, gkt, gsq, gP, gPT, gnm, grs, gss = region(
            0, NT * 1536, HKV * 512, 3072, 512, 1024, 4 * 384, 2 * 896, 48, 48, 16)
        g_att = [gP, gPT, gnm, grs]
        qkv3 = qkv.rearrange("p (t n) -> p t n", t=NT)
        gkT3 = gkT.rearrange("p (h n) -> p h n", h=HKV)
        gqT3 = hTt[:, :].rearrange("p (h n) -> p h n", h=8)
        oT3 = oT.rearrange("p (c t) -> p c t", c=8)
        htok, xg, xgT, S_sb, sel, yacc, sil, act_b, actT, rt = region(
            0, NT * D, D, NT * D, NT * T, NT * P, NT * D, 512, 512, 512, 1100)
        htok3 = htok.rearrange("p (t n) -> p t n", t=NT)
        xgT3 = xgT.rearrange("p (b n) -> p b n", b=NT)
        yacc3 = yacc.rearrange("p (b n) -> p b n", b=NT)
        rt48 = [rt[:, 48 * i:48 * i + 48] for i in range(12)]
        rt12 = [rt[:, 576 + 12 * i:576 + 12 * i + 12] for i in range(12)]
        rtT = sel[0:NE, 0:T]
        rt3 = [rt[:, 720 + 3 * i:720 + 3 * i + 3] for i in range(8)]
        gates = rt48[11]
        gates_g, pos_g = rt[:, 840:900], rt[:, 900:915]
        gslot = rt[:, 776:776 + NT * GS]
        gcur = rt[:, 824:824 + NT * GS]
        sil_of, act_of, actT_of = ([x[:, 0:256], x[:, 256:512], xg[:, 256 * i:256 * i + 256]] for i, x in enumerate((sil, act_b, actT)))
        pcol = rt[:, 804:807]
        flags_f = rt[:, 808:816]
        flags = rt[:, 816:824].bitcast(mybir.dt.int32)

        names = """in_small in_x cond_ready ada_done mod_ready sq_ready ss_used r_ready h_ready ab_ready slot_used job_done
            free_act free_dve chain_dve chain_act sq_sum h_scaled xr_ready xr_used xc_raw xc_ready z_ready lat_copied
            dk_copied e_in e_mid dt_ready cum_copied e_cum
            xtok_ready xtok_used xdt_ready g_ready seg_ready dec_ready s_ready diag_done xw_ready st_done
            ytok_ready ysq_ready ynorm_ready ynormed yT_ready ssd_done lsq_ready lr_ready latn_ready
            qt_copied qk_sq qk_r qk_ready kt_nope qkT_ready
            max_ready e_ready p_ready pt_ready pv_done o_ready x_new row_done row_copied
            qkv_ready rt_exp gates_ready flags_ready
            sel_ready sel_over_ready xg0_done xg1_done selT_done xg_by_act xg_by_dve xgT0_done xgT1_done xgT_by_act xgT_by_dve
            sc_done sc_used gcur_ready""".split()
        S = {n: sem(n) for n in names}
        slot_full = [sem(f"slot_full{i}") for i in range(RING)]
        steps = "au_done sil_ready act_ready tr_done trc_ready dn_done acc_ready".split()
        MAIN = {n: sem(n) for n in steps}
        OVER = {n: sem("over_" + n) for n in steps}
        outs = {n: sem("stored_" + n) for n in ("y", "stf", "stb", "ckv", "kpe", "gk", "gv")}

        jobs = []

        def job(name, by):
            jobs.append((name, by))

        STEPS = [(2, False), (1, True), (2, True), (0, True)]
        STATES = [(1,), (0,), (), (0, 1)]

        AHEAD = 3

        def attention_jobs(kind, heads):
            n = NT * heads
            for u in range(n + AHEAD):
                if u < n:
                    job((kind, "s", u), "A")
                if u >= AHEAD:
                    job((kind, "pT", u - AHEAD), "A")

        for l in range(DEPTH):
            job(("ss", l, 0), "A")
            if l == 0:
                job(("dk",), "D")
                for c in range(CONV_C):
                    job(("xbc", c), "A")
                for c in range(3):
                    job(("lat", c), "D")
                for i in range(3):
                    for t in range(NT):
                        job(("z", i, t), "A")
                job(("cum",), "D")
                job(("tot",), "D")
                for i, (t, full) in enumerate(STEPS):
                    job(("xt", i, 0), "A")
                    job(("xt", i, 1), "A")
                    job(("bt", i), "A")
                    if full:
                        job(("g", i, 0), "A")
                        job(("g", i, 1), "A")
                        for u in range(8):
                            job(("bc", i, u), "D")
                        if t:
                            for d in range(2):
                                for g in range(2):
                                    job(("off", i, d, g), "D")
                        job(("yT", i, 0), "A")
                        job(("yT", i, 1), "A")
                    for d in STATES[i]:
                        job(("st", i, d), "D")
                job(("sl", 0), "A")
                job(("sl", 1), "A")
                for t in range(NT):
                    job(("q", t, 0), "A")
                    job(("q", t, 1), "A")
                    job(("qT", t, 0), "A")
                    job(("qT", t, 1), "A")
                for s in range(4):
                    job(("kv", s, 0), "A")
                    job(("kv", s, 1), "A")
                    job(("kT", s, 0), "A")
                    job(("kT", s, 1), "A")
                attention_jobs("mla", HM)
            else:
                for s in range(N_INO):
                    for t in range(NT):
                        job(("in", s, t), "A" if s % 2 else "D")
                for t in range(NT):
                    job(("gqT", t, 0), "A")
                    job(("gqT", t, 1), "A")
                    job(("gkT", t), "A")
                job(("gkT", 3), "A")
                attention_jobs("gqa", HQ)
            for c in range(DC):
                job(("out", l, c), "D")
            job(("ss", l, 1), "A")
            job(("rt", l), "A")
            job(("rtT", l), "D")
            for j in range(2 * NT):
                job(("htok", l, j), "A")
            job(("pos", l), "D")
        RB = 5
        index = {n: i for i, (n, _) in enumerate(jobs)}
        assert len(index) == len(jobs)
        emptied, _cnt = [], {"A": 0, "D": 0}
        for n, by in jobs:
            _cnt[by] += 1
            emptied.append((by, _cnt[by]))
        free_of = {"A": S["free_act"], "D": S["free_dve"]}
        bank = lambda j: ps[:, j % RB, :]

        ADA_AT = {(i, u): n for n, (i, u) in enumerate([(i, u) for i in (1, 2, 3) for u in (0, 1, 3, 5, 6, 7)][:N_ADA])}
        SC_BANK = [6, 7, 4, 5]
        KSLOT = [0, 2, 3, 1]
        KEYS = [(0, 128), (128, 384), (128, 384)]
        XC0 = [0, 129, 257]
        TILE = [slice(P * t, P * t + P) for t in range(NT)]
        SEG = [slice(0, P), slice(P, T)]

        block = ctx.enter_context(nc.Block())

        @block.sync
        def _(sp):
            def load(n, at, wait):
                if wait is not None:
                    sp.wait_ge(S["slot_used"], wait)
                sp.dma_start(ring[:, at, :], w_d[bass.ds(n, 1), :, :].rearrange("a p n -> p (a n)")).then_inc(slot_full[at], 16)

            for n in range(RING):
                load(n, n, None)
            with sp.Fori(1, N_SLOTS // RING) as i:
                for j in range(RING):
                    load(i * RING + j, j, i * RING + (j - RING + 1))
            for n in range(N_SLOTS // RING * RING, N_SLOTS):
                load(n, n % RING, n - RING + 1)
            sp.wait_ge(S["x_new"], 4 * DC)
            sp.dma_start(y_d, xT[:, :, :]).then_inc(outs["y"], 16)
            for n in outs:
                sp.wait_ge(outs[n], 16)

        @block.tensor
        def _(pe):
            at = [0]

            def fill(*name):
                j = at[0]
                assert jobs[j][0] == name, (jobs[j], name)
                if j >= RB:
                    by, n = emptied[j - RB]
                    pe.wait_ge(free_of[by], n)
                at[0] += 1
                return bank(j)

            def filled(ins):
                ins.then_inc(S["job_done"], 1)

            def slot(n):
                pe.wait_ge(slot_full[n % RING], 16 * (n // RING + 1))
                return ring[:, n % RING, :]

            def used(ins):
                ins.then_inc(S["slot_used"], 1)

            mm = pe.matmul

            def ada(l, j):
                n = N_ADA * l + j
                if j == 0:
                    pe.wait_ge(S["cond_ready"], 1)
                    if l:
                        pe.wait_ge(S["mod_ready"], l)
                w = slot((S_ADA1 if l else S_ADA0) + j).rearrange("p (k n) -> p k n", k=DC)
                row = ps[0:2, 7 if l else 5 + j % 2, 0:384]
                if l and j:
                    turn_row(l, j - 1)
                elif j >= 2:
                    pe.wait_ge(S["row_copied"], n - 1)
                for k in range(DC):
                    ins = mm(row, condS[:, 2 * k:2 * k + 2], w[:, k, :], start=(k == 0), stop=(k == DC - 1))
                ins.then_inc(S["row_done"], 1)
                pe.drain().then_inc(S["slot_used"], 1)
                if not l and j:
                    turn_row(l, j - 1)
                if j == N_ADA - 1:
                    turn_row(l, j)
                    pe.drain().then_inc(S["ada_done"], 1)

            def turn_row(l, j):
                n = N_ADA * l + j
                pe.wait_ge(S["row_copied"], n + 1)
                for m in range(3):
                    c = 384 + 2 * (3 * j + m)
                    pe.transpose(ps[:, 7, c:c + 2], mod_row[0 if l else j % 2][:, P * m:P * m + P], ident[0:2, 0:2])

            def sum_squares(l, i):
                pe.wait_ge(S["sq_sum"], (DC - 1) * (2 * l + i + 1))
                b = fill("ss", l, i)
                filled(mm(b[:, 0:T], ones, sq_acc, start=True, stop=True))

            def h_chunk(l, i, k):
                pe.wait_ge(S["h_ready"], DC * (2 * l + i) + k + 1)

            def project(name, out, lhs, rhs, n=DC):
                for k in range(n):
                    ins = mm(out, lhs(k), rhs(k), start=(k == 0), stop=(k == n - 1))
                return ins

            def attention(kind, heads, q_of, k_of, v_of, places):
                Pb, PTb = places[:2]
                base = 0 if kind == "mla" else NT * HM
                pairs = 0 if kind == "mla" else HM // 2
                for u in range(NT * heads + AHEAD):
                    if u < NT * heads:
                        h, t = u // NT, u % NT
                        k0, nk = KEYS[t]
                        b = fill(kind, "s", u)
                        filled(mm(b[:, 0:nk], q_of(t, h), k_of(h, k0, nk), start=True, stop=True))
                    v = u - AHEAD
                    if v >= 0:
                        h, t = v // NT, v % NT
                        pe.wait_ge(S["p_ready"], base + v + 1)
                        b = fill(kind, "pT", v)
                        for k in range(KEYS[t][1] // P):
                            ins = pe.transpose(b[:, P * k:P * k + P], Pb[:, 384 * (v % 4) + P * k:384 * (v % 4) + P * k + P], ident)
                        filled(ins)
                        if t == 0 and h:
                            values(kind, h - 1, base, pairs, v_of, PTb)
                values(kind, heads - 1, base, pairs, v_of, PTb)

            def values(kind, h, base, pairs, v_of, PTb):
                pe.wait_ge(S["pt_ready"], base + NT * (h + 1))
                pair = pairs + h // 2
                if h % 2 == 0 and pair >= pairs + 2:
                    pe.wait_ge(S["o_ready"], pair - 1)
                r = slice(64 * (h % 2), 64 * (h % 2) + 64)
                pt = PTb[:, 896 * (h % 2):896 * (h % 2) + 896]
                mm(ps[r, 5 + pair % 2, 0:P], v_of(0, h), pt[:, 0:P], start=True, stop=True)
                for k in range(NT):
                    ins = mm(ps[r, 5 + pair % 2, P:T], v_of(1 + k, h), pt[:, P + 256 * k:P + 256 * k + 256], start=(k == 0), stop=(k == NT - 1))
                ins.then_inc(S["pv_done"], 1)

            def project_out(l, n_k, cols, first, src):
                pe.wait_ge(S["o_ready"], HM // 2 + (HQ // 2 if l else 0))
                for j, n in enumerate(cols):
                    w = slot(first + j)[:, 0:n_k * P * n].rearrange("p (k n) -> p k n", k=n_k)
                    for m in range(n):
                        b = fill("out", l, sum(cols[:j]) + m)
                        ins = project("out", b[:, 0:T], lambda k: w[:, k, P * m:P * m + P], src, n_k)
                        filled(ins)
                    pe.drain().then_inc(S["slot_used"], 1)

            def moe(l):
                sum_squares(l, 1)
                b = fill("rt", l)
                wr = sm("w_router").rearrange("p (k e) -> p k e", k=DC)
                for k in range(DC):
                    h_chunk(l, 1, k)
                    ins = mm(b[0:NE, 0:T], wr[:, k, :], hT[:, k, :], start=(k == 0), stop=(k == DC - 1))
                filled(ins)
                pe.wait_ge(S["rt_exp"], l + 1)
                b = fill("rtT", l)
                for t in range(NT):
                    ins = pe.transpose(b[:, NE * t:NE * t + NE], rtT[:, TILE[t]], ident[0:NE, 0:NE])
                filled(ins)
                for j in range(2 * NT):
                    b = fill("htok", l, j)
                    for c in range(4):
                        ins = pe.transpose(b[:, P * c:P * c + P], hT[:, 4 * (j % 2) + c, TILE[j // 2]], ident)
                    filled(ins)
                pe.wait_ge(S["gates_ready"], l + 1)
                b = fill("pos", l)
                for t in range(NT):
                    for v in range(t + 1):
                        mm(b[:, NG * t:NG * t + NG], ones if v < t else tri[0], rt12[9][:, NG * v:NG * v + NG], start=(v == 0), stop=(v == t))
                for v in range(NT):
                    ins = mm(b[:, 12:16], ones, rt12[9][:, NG * v:NG * v + NG], start=(v == 0), stop=(v == NT - 1))
                filled(ins)
                for by in "AD":
                    pe.wait_ge(free_of[by], max([n for o, n in emptied[:at[0]] if o == by]))
                pe.wait_ge(S["mod_ready"], 2)
                pe.wait_ge(S["flags_ready"], l + 1)
                first = S_MOE1 if l else S_MOE0
                with pe.Fori(0, NG) as g:
                    def count(per_group, n):
                        return g * per_group + (per_group * NG * l + n)

                    def gather(b):
                        if b:
                            pe.wait_ge(S["sel_over_ready"], count(2, b))
                            for k in ("xgT_by_act", "xgT_by_dve"):
                                pe.wait_ge(S[k], count(NT, b))
                        else:
                            pe.wait_ge(S["sel_ready"], g + ((NG + 1) * l + 1))
                        for h in range(2):
                            for t in range(NT):
                                ins = mm(ps[:, 4 + h, :], sel[:, P * t:P * t + P], htok3[:, t, 512 * h:512 * h + 512], start=(t == 0), stop=(t == NT - 1))
                            ins.then_inc(S["xg1_done" if h else "xg0_done"], 1)
                        for t in range(NT):
                            mm(ps[:, 6, 0:GS], sel[:, P * t:P * t + P], gcur[:, GS * t:GS * t + GS], start=(t == 0), stop=(t == NT - 1))
                        for t in range(NT):
                            ins = pe.transpose(ps[:, 7, P * t:P * t + P], sel[:, P * t:P * t + P], ident)
                        ins.then_inc(S["selT_done"], 1)
                        for h, by in enumerate(("xg_by_act", "xg_by_dve")):
                            pe.wait_ge(S[by], count(NT, b + 1))
                            for c in range(4):
                                ins = pe.transpose(ps[:, 2 + h, P * c:P * c + P], xg[:, 512 * h + P * c:512 * h + P * c + P], ident)
                            ins.then_inc(S["xgT1_done" if h else "xgT0_done"], 1)
                        if b:
                            for k in ("xgT_by_act", "xgT_by_dve"):
                                pe.wait_ge(S[k], count(NT, b + 1))

                    def up(e, b, M, bank_, per, n):
                        a1, a2 = (first + 2 * e) % RING, (first + 2 * e + 1) % RING
                        for k in range(DC):
                            if e == 0 and b == 0 and k % 4 == 0:
                                pe.wait_ge(S["xgT_by_act" if k else "xgT_by_dve"], count(NT, 1))
                            w = ring[:, a1, 512 * k:512 * k + 512] if k < 6 else ring[:, a2, 512 * (k - 6):512 * (k - 6) + 512]
                            ins = mm(ps[:, bank_, :], xgT3[:, b, P * k:P * k + P], w, start=(k == 0), stop=(k == DC - 1))
                        ins.then_inc(M["au_done"], 1)

                    def down(e, M, at_, bank_t, bank_y, per, n):
                        a2 = (first + 2 * e + 1) % RING
                        pe.wait_ge(M["act_ready"], count(per, n + 1))
                        for j in range(2):
                            ins = pe.transpose(ps[:, bank_t, P * j:P * j + P], act_of[at_][:, P * j:P * j + P], ident)
                        ins.then_inc(M["tr_done"], 1)
                        pe.wait_ge(M["trc_ready"], count(per, n + 1))
                        for h in range(2):
                            if n:
                                pe.wait_ge(M["acc_ready"], count(2 * per, 2 * n - 1 + h))
                            for j in range(2):
                                ins = mm(ps[:, bank_y + h, :], actT_of[at_][:, P * j:P * j + P],
                                         ring[:, a2, 1024 + 1024 * j + 512 * h:1024 + 1024 * j + 512 * h + 512], start=(j == 0), stop=(j == 1))
                            ins.then_inc(M["dn_done"], 1)

                    def scatter(b):
                        acc, last = (MAIN["acc_ready"], 2 * GS) if b == 0 else (OVER["acc_ready"], 4 * GS)
                        for c in range(DC):
                            if c in (0, 3):
                                pe.wait_ge(acc, count(last, last - (c == 0)))
                            if c >= 4:
                                pe.wait_ge(S["sc_used"], count(NT * DC, DC * b + c - 3))
                            mm(ps[:, SC_BANK[c % 4], 0:T], yacc3[:, b, P * c:P * c + P], S_sb[:, T * b:T * b + T],
                               start=True, stop=True).then_inc(S["sc_done"], 1)
                        pe.wait_ge(S["sc_used"], count(NT * DC, DC * b + DC))

                    over = [pe.value_load(flags[0:1, bass.ds(g * 2 + b, 1)], min_val=0, max_val=1) for b in range(2)]
                    gather(0)
                    for b in (1, 2):
                        with pe.If(over[b - 1]):
                            gather(b)
                        with pe.Else():
                            for k in ("xg0_done", "xg1_done", "selT_done", "xgT0_done", "xgT1_done"):
                                pe.wait_ge(S[k], count(NT, b))
                                pe.sem_inc(S[k], 1)
                    for e in range(GS):
                        for a in (first + 2 * e, first + 2 * e + 1):
                            pe.wait_ge(slot_full[a % RING], g * 16 + 16 * (a // RING + 1))
                        if e >= 2:
                            pe.wait_ge(MAIN["act_ready"], count(GS, e - 1))
                        up(e, 0, MAIN, e % 2, GS, e)
                        if e:
                            down(e - 1, MAIN, (e - 1) % 2, 2, 4, GS, e - 1)
                            pe.drain().then_inc(S["slot_used"], 2)
                        for b in (1, 2):
                            n = 2 * e + b - 1
                            with pe.If(over[b - 1]):
                                up(e, b, OVER, 3, 2 * GS, n)
                                down(e, OVER, 2, 3, 6, 2 * GS, n)
                                pe.wait_ge(OVER["acc_ready"], count(4 * GS, 2 * n + 2))
                            with pe.Else():
                                for k, m in (("au_done", 1), ("tr_done", 1), ("dn_done", 2)):
                                    if n:
                                        pe.wait_ge(OVER[k], count(2 * GS * m, n * m))
                                    pe.sem_inc(OVER[k], m)
                    down(GS - 1, MAIN, (GS - 1) % 2, 2, 4, GS, GS - 1)
                    pe.drain().then_inc(S["slot_used"], 2)
                    scatter(0)
                    for b in (1, 2):
                        with pe.If(over[b - 1]):
                            scatter(b)
                        with pe.Else():
                            pe.wait_ge(S["sc_done"], count(NT * DC, DC * b))
                            pe.sem_inc(S["sc_done"], DC)

            pe.wait_ge(S["in_small"], 16)
            for j in range(N_ADA):
                ada(0, j)
            sum_squares(0, 0)
            wdk = sm("w_dk").rearrange("p (k n) -> p k n", k=DC)
            b = fill("dk")
            for t in range(NT):
                for k in range(DC):
                    if t == 0:
                        h_chunk(0, 0, k)
                    ins = mm(b[:, 48 * t:48 * t + 48], hT[:, k, TILE[t]], wdk[:, k, :], start=(k == 0), stop=(k == DC - 1))
            filled(ins)
            for s in range(N_INE):
                w = slot(S_INE + s).rearrange("p (k n) -> p k n", k=DC)
                for m in range(3):
                    c = 3 * s + m
                    if c < 13:
                        b = fill("xbc", c) if c < CONV_C else fill("lat", c - CONV_C)
                        filled(project("in", b[:, 0:T], lambda k: w[:, k, P * m:P * m + P], lambda k: hT[:, k, :]))
                if s >= 4:
                    lo = P if s == 4 else 0
                    for t in range(NT):
                        b = fill("z", s - 4, t)
                        filled(project("z", b[:, 0:T - lo], lambda k: hT[:, k, TILE[t]], lambda k: w[:, k, lo:T]))
                pe.drain().then_inc(S["slot_used"], 1)
            pe.wait_ge(S["dt_ready"], 1)
            b = fill("cum")
            for d in range(2):
                ins = mm(b[:, 48 * d:48 * d + 48], tri[d], e96[3][:, 48 * d:48 * d + 48], start=True, stop=True)
            filled(ins)
            b = fill("tot")
            filled(mm(b[:, 0:96], ones, e96[3], start=True, stop=True))
            pe.wait_ge(S["xc_ready"], CONV_C)
            nfull = 0
            for i, (t, full) in enumerate(STEPS):
                c0 = XC0[t]
                for k in range(2):
                    b = fill("xt", i, k)
                    for c in range(4):
                        ins = pe.transpose(b[:, P * c:P * c + P], xc3[:, 4 * k + c, c0:c0 + P], ident)
                    filled(ins)
                b = fill("bt", i)
                filled(pe.transpose(b[:, 0:P], xc3[:, 8, c0:c0 + P], ident))
                if full:
                    for g in range(2):
                        b = fill("g", i, g)
                        filled(mm(b[:, 0:P], xc3[64 * g:64 * g + 64, 8, c0:c0 + P], xc3[64 * g:64 * g + 64, 9, c0:c0 + P], start=True, stop=True))
                    base = 8 * nfull

                    def cums(u):
                        q, d = u // 2, u % 2
                        b = fill("bc", i, u)
                        for h in range(4):
                            col = 48 * d + HS * t + 4 * q + h
                            ins = mm(b[:, P * h:P * h + P], e96[3][:, col:col + 1].broadcast_to([P, P]), tri[d], start=True, stop=True)
                        filled(ins)

                    def diag(u):
                        q, d = u // 2, u % 2
                        pe.wait_ge(S["s_ready"], base + u + 1)
                        for h in range(4):
                            hh = 4 * (q % 2) + h
                            ins = mm(ps[:, 5 + q // 2, 64 * hh:64 * hh + 64], dec[d][:, P * h:P * h + P],
                                     xdt[d][:, 64 * (4 * q + h):64 * (4 * q + h) + 64],
                                     start=(u % 4 == 0 and h == 0), stop=(d == 1), skip_group_check=True)
                        ins.then_inc(S["diag_done"], 1)

                    cums(0)
                    for u in range(8):
                        if u + 1 < 8:
                            cums(u + 1)
                        diag(u)
                        if (i, u) in ADA_AT:
                            ada(1, ADA_AT[i, u])
                    if t:
                        for d in range(2):
                            s_in = {(0, 1): h0[0], (0, 2): h0[0], (1, 2): h0[1], (1, 1): s_b1}[d, t]
                            if d == 0:
                                pe.wait_ge(S["st_done"], 1 if t == 1 else 2)
                            for g in range(2):
                                b = fill("off", i, d, g)
                                filled(mm(b[:, 0:512], xc3[64 * g:64 * g + 64, 9, c0:c0 + P], s_in[64 * g:64 * g + 64, :], start=True, stop=True))
                    pe.wait_ge(S["ynormed"], nfull + 1)
                    for k in range(2):
                        b = fill("yT", i, k)
                        for c in range(4):
                            ins = pe.transpose(b[:, P * c:P * c + P], ytok[:, 512 * k + P * c:512 * k + P * c + P], ident)
                        filled(ins)
                    nfull += 1
                for d in STATES[i]:
                    pe.wait_ge(S["xw_ready"], sum(len(x) for x in STATES[:i]) + STATES[i].index(d) + 1)
                    b = fill("st", i, d)
                    for g in range(2):
                        ins = mm(b[64 * g:64 * g + 64, 0:512], Btok[:, 64 * g:64 * g + 64], xw[:, 512 * g:512 * g + 512], start=True, stop=True)
                    filled(ins)
            pe.wait_ge(S["lsq_ready"], 1)
            b = fill("sl", 0)
            for k in range(2):
                ins = mm(b[:, 0:T], ones, lsq[:, T * k:T * k + T], start=(k == 0), stop=(k == 1))
            filled(ins)
            b = fill("sl", 1)
            filled(mm(b[:, 0:T], ones, lsq[:, 2 * T:3 * T], start=True, stop=True))
            pe.wait_ge(S["latn_ready"], 1)
            wq = sm("w_q_b").rearrange("p (k n) -> p k n", k=2)
            wkv = sm("w_kv_b")
            for t in range(NT):
                for hh in range(2):
                    b = fill("q", t, hh)
                    filled(project("q", b[:, 0:384], lambda k: latT[:, k, TILE[t]], lambda k: wq[:, k, 384 * hh:384 * hh + 384], 2))
                pe.wait_ge(S["qk_ready"], t + 1)
                for hh in range(2):
                    b = fill("qT", t, hh)
                    for h in range(4):
                        ins = pe.transpose(b[0:QM, P * h:P * h + P], mkt[:, QM * (4 * hh + h):QM * (4 * hh + h) + QM], ident)
                    filled(ins)
            for s in range(4):
                src = latT[:, 2, TILE[s]] if s < NT else sm("ckv_cache")
                for hh in range(2):
                    b = fill("kv", s, hh)
                    filled(mm(b[:, 0:512], src, wkv[:, 512 * hh:512 * hh + 512], start=True, stop=True))
                pe.wait_ge(S["qk_ready"], NT + s + 1)
                for hh in range(2):
                    b = fill("kT", s, hh)
                    for h in range(4):
                        ins = pe.transpose(b[0:QM, P * h:P * h + P], mkt[:, QM * (4 * hh + h):QM * (4 * hh + h) + QM], ident)
                    filled(ins)
            pe.wait_ge(S["qkT_ready"], 2 * (NT + 4))
            attention("mla", HM, lambda t, h: mqT3[0:QM, h, TILE[t]], lambda h, k0, nk: mkT3[0:QM, h, k0:k0 + nk],
                      lambda s, h: mv3[:, s, 64 * h:64 * h + 64], m_att)
            project_out(0, 12, (2, 2, 2, 2), S_OUTE, lambda k: oTy3[:, k, :] if k < 8 else oTm3[:, k - 8, :])
            moe(0)
            sum_squares(1, 0)
            for s in range(N_INO):
                w = slot(S_INO + s).rearrange("p (k n) -> p k n", k=DC)
                for t in range(NT):
                    b = fill("in", s, t)
                    for k in range(DC):
                        if s == 0 and t == 0:
                            h_chunk(1, 0, k)
                        ins = mm(b[:, 0:384], hT[:, k, TILE[t]], w[:, k, :], start=(k == 0), stop=(k == DC - 1))
                    filled(ins)
                pe.drain().then_inc(S["slot_used"], 1)
            for t in range(NT):
                pe.wait_ge(S["qk_ready"], NT + 4 + 2 * t + 1)
                for k in range(2):
                    b = fill("gqT", t, k)
                    for c in range(4):
                        ins = pe.transpose(b[:, P * c:P * c + P], qkv3[:, t, 512 * k + P * c:512 * k + P * c + P], ident)
                    filled(ins)
                pe.wait_ge(S["qk_ready"], NT + 4 + 2 * t + 2)
                b = fill("gkT", t)
                for c in range(4):
                    ins = pe.transpose(b[:, P * c:P * c + P], gkt[:, P * c:P * c + P], ident)
                filled(ins)
            pe.wait_ge(S["qk_ready"], NT + 4 + 2 * NT + 1)
            b = fill("gkT", 3)
            for c in range(4):
                ins = pe.transpose(b[:, P * c:P * c + P], gkt[:, P * c:P * c + P], ident)
            filled(ins)
            pe.wait_ge(S["qkT_ready"], 2 * (NT + 4) + 3 * NT + 1)
            attention("gqa", HQ, lambda t, h: gqT3[64 * (h % 2):64 * (h % 2) + 64, h // 2, TILE[t]],
                      lambda h, k0, nk: gkT3[64 * (h % 2):64 * (h % 2) + 64, h // 4, k0:k0 + nk],
                      lambda s, h: (sm("v_cache")[:, 64 * (h // 4):64 * (h // 4) + 64] if s == 1 else
                                    qkv3[:, {0: 0, 2: 1, 3: 2}[s], 1280 + 64 * (h // 4):1280 + 64 * (h // 4) + 64]), g_att)
            project_out(1, 8, (3, 3, 2), S_OUTO, lambda k: oT3[:, k, :])
            moe(1)

        @block.scalar
        def _(act):
            n_chain, n_taken = [0], [0]
            mine = [j for j, (_, by) in enumerate(jobs) if by == "A"]

            def link(ins):
                n_chain[0] += 1
                ins.then_inc(S["chain_act"], 1)
                act.wait_ge(S["chain_act"], n_chain[0])

            def take(*name):
                j = mine[n_taken[0]]
                assert jobs[j][0] == name, (jobs[j], name)
                act.wait_ge(S["job_done"], j + 1)
                n_taken[0] += 1
                return bank(j)

            def emptied_by(ins):
                ins.then_inc(S["free_act"], 1)

            def after(name):
                act.wait_ge(S["job_done"], index[name] + 1)

            A = act.activation

            def rsqrt(out, src, n, scale=1.0):
                link(A(out, src, ACT.Ln, bias=EPS, scale=1.0 / n))
                return A(out, out, ACT.Exp, bias=math.log(scale), scale=-0.5)

            act.dma_start(small[:, :], small_d).then_inc(S["in_small"], 16)
            act.dma_start(xT[:, :, :], x_d).then_inc(S["in_x"], 16)
            act.wait_ge(S["in_small"], 16)
            A(condS, sm("cond"), ACT.Silu).then_inc(S["cond_ready"], 1)

            def norm(l, i):
                for c in range(DC):
                    if l == 0 and i == 0:
                        act.wait_ge(S["in_x"], 16)
                    else:
                        act.wait_ge(S["x_new"], DC * (2 * l + i - 1) + c + 1)
                    A(hT[:, c, :], xT[:, c, :], ACT.Square).then_inc(S["sq_ready"], 1)
                b = take("ss", l, i)
                link(A(rn, b[:, 0:T], ACT.Ln, bias=EPS, scale=1.0 / D))
                A(rn, rn, ACT.Exp, scale=-0.5).then_inc(S["r_ready"], 1)
                act.wait_ge(S["r_ready"], 2 * l + i + 1)
                act.sem_inc(S["free_act"], 1)
                sh = mod[l][:, 16 * 3 * i:16 * (3 * i + 1)]
                for c in range(DC):
                    act.wait_ge(S["h_scaled"], DC * (2 * l + i) + c + 1)
                    for s in range(2):
                        ins = A(hT[:, c, SEG[s]], hT[:, c, SEG[s]], ACT.Identity, bias=sh[:, 2 * c + s:2 * c + s + 1])
                    ins.then_inc(S["h_ready"], 1)

            def attention(kind, heads, places):
                Pb, PTb, nm, rs = places
                base = 0 if kind == "mla" else NT * HM
                for n in ("ckv", "kpe") if kind == "mla" else ():
                    act.wait_ge(outs[n], 16)
                for u in range(NT * heads + AHEAD):
                    if u < NT * heads:
                        b = take(kind, "s", u)
                        act.wait_ge(S["max_ready"], base + u + 1)
                        if u >= 4:
                            after((kind, "pT", u - 4))
                        nk = KEYS[u % NT][1]
                        A(Pb[:, 384 * (u % 4):384 * (u % 4) + nk], b[:, 0:nk], ACT.Exp, bias=nm[:, u:u + 1],
                          accum_out=rs[:, u:u + 1]).then_inc(S["e_ready"], 1)
                        act.wait_ge(S["e_ready"], base + u + 1)
                        act.sem_inc(S["free_act"], 1)
                    v = u - AHEAD
                    if v >= 0:
                        h, t = v // NT, v % NT
                        b = take(kind, "pT", v)
                        if t == 0 and h >= 2:
                            act.wait_ge(S["pv_done"], base // NT + h - 1)
                        pt = PTb[:, 896 * (h % 2):896 * (h % 2) + 896]
                        out, src = pt[:, 0:P], b[:, 0:P]
                        if t:
                            out = pt[:, P:].rearrange("p (k q) -> p k q", k=3)[:, :, P * (t - 1):P * t]
                            src = b[:, 0:384].rearrange("p (k q) -> p k q", k=3)
                        act.copy(out, src).then_inc(S["pt_ready"], 1)
                        act.wait_ge(S["pt_ready"], base + v + 1)
                        act.sem_inc(S["free_act"], 1)

            def qk_rsqrt(n_step, ss, n, scale):
                act.wait_ge(S["qk_sq"], n_step + 1)
                rsqrt(ss, ss, n, scale).then_inc(S["qk_r"], 1)

            def moe(l):
                norm(l, 1)
                b = take("rt", l)
                A(rtT, b[0:NE, 0:T], ACT.Exp, scale=-1.0).then_inc(S["rt_exp"], 1)
                act.wait_ge(S["rt_exp"], l + 1)
                act.sem_inc(S["free_act"], 1)
                for n in ("gk", "gv") if l else ():
                    act.wait_ge(outs[n], 16)
                for j in range(2 * NT):
                    b = take("htok", l, j)
                    emptied_by(act.copy(htok3[:, j // 2, 512 * (j % 2):512 * (j % 2) + 512], b[:, :]))
                act.wait_ge(S["flags_ready"], l + 1)
                with act.Fori(0, NG) as g:
                    def count(per_group, n):
                        return g * per_group + (per_group * NG * l + n)

                    def gather(b):
                        act.wait_ge(S["xg0_done"], count(NT, b + 1))
                        act.copy(xg[:, 0:512], ps[:, 4, :]).then_inc(S["xg_by_act"], 1)
                        act.wait_ge(S["selT_done"], count(NT, b + 1))
                        act.copy(S_sb[:, T * b:T * b + T], ps[:, 7, 0:T])
                        act.wait_ge(S["xgT1_done"], count(NT, b + 1))
                        act.copy(xgT3[:, b, 512:1024], ps[:, 3, :]).then_inc(S["xgT_by_act"], 1)

                    def silu(M, at_, bank_, per, n):
                        act.wait_ge(M["au_done"], count(per, n + 1))
                        A(sil_of[at_], ps[:, bank_, 0:256], ACT.Silu).then_inc(M["sil_ready"], 1)

                    def turned_act(M, at_, bank_t, per, n):
                        act.wait_ge(M["tr_done"], count(per, n + 1))
                        act.copy(actT_of[at_], ps[:, bank_t, 0:256]).then_inc(M["trc_ready"], 1)

                    over = [act.value_load(flags[0:1, bass.ds(g * 2 + b, 1)], min_val=0, max_val=1) for b in range(2)]
                    gather(0)
                    for b in (1, 2):
                        with act.If(over[b - 1]):
                            gather(b)
                        with act.Else():
                            for k in ("xg_by_act", "xgT_by_act"):
                                act.wait_ge(S[k], count(NT, b))
                                act.sem_inc(S[k], 1)
                    for e in range(GS):
                        silu(MAIN, e % 2, e % 2, GS, e)
                        if e:
                            turned_act(MAIN, (e - 1) % 2, 2, GS, e - 1)
                        for b in (1, 2):
                            n = 2 * e + b - 1
                            with act.If(over[b - 1]):
                                silu(OVER, 2, 3, 2 * GS, n)
                                turned_act(OVER, 2, 3, 2 * GS, n)
                            with act.Else():
                                for k in ("sil_ready", "trc_ready"):
                                    if n:
                                        act.wait_ge(OVER[k], count(2 * GS, n))
                                    act.sem_inc(OVER[k], 1)
                    turned_act(MAIN, (GS - 1) % 2, 2, GS, GS - 1)

            def copy_row(l, j):
                n = N_ADA * l + j
                act.wait_ge(S["row_done"], n + 1)
                act.copy(mod_row[0 if l else j % 2], ps[0:2, 7 if l else 5 + j % 2, 0:384]).then_inc(S["row_copied"], 1)

            for j in range(N_ADA):
                copy_row(0, j)
            norm(0, 0)
            convb = sm("conv_b")

            def conv_silu(c):
                act.wait_ge(S["xc_raw"], c + 1)
                A(xc3[:, c, :], xc3[:, c, :], ACT.Silu, bias=convb[:, c:c + 1]).then_inc(S["xc_ready"], 1)

            for c in range(CONV_C):
                b = take("xbc", c)
                if c >= 2:
                    act.wait_ge(S["xc_raw"], c - 1)
                else:
                    act.wait_ge(S["xr_used"], 1)
                act.copy(xr[c % 2][:, 1:129], b[:, 0:P])
                act.copy(xr[c % 2][:, 130:386], b[:, P:T]).then_inc(S["xr_ready"], 1)
                act.wait_ge(S["xr_ready"], c + 1)
                act.sem_inc(S["free_act"], 1)
                if c:
                    conv_silu(c - 1)
            conv_silu(CONV_C - 1)
            for i, (lo, w) in enumerate([(0, 256), (256, 384), (640, 384)]):
                for t in range(NT):
                    b = take("z", i, t)
                    A(zs3[:, t, lo:lo + w], b[:, 0:w], ACT.Silu).then_inc(S["z_ready"], 1)
                    act.wait_ge(S["z_ready"], 3 * i + t + 1)
                    act.sem_inc(S["free_act"], 1)
            act.wait_ge(S["e_in"], 1)
            A(e96[6][:, 0:32], sm("a_log"), ACT.Exp)
            link(A(e96[1], e96[1], ACT.Exp))
            A(e96[1], e96[1], ACT.Ln, bias=1.0).then_inc(S["e_mid"], 1)
            act.wait_ge(S["cum_copied"], 1)
            A(e96[5], e96[4], ACT.Exp, scale=-1.0)
            A(e96[9], e96[9], ACT.Exp)
            A(e96[8], e96[6], ACT.Exp).then_inc(S["e_cum"], 1)
            nfull = 0
            ssdn = sm("ssd_norm")
            for i, (t, full) in enumerate(STEPS):
                if i:
                    act.wait_ge(S["xtok_used"], i)
                for k in range(2):
                    b = take("xt", i, k)
                    emptied_by(act.copy(xtok[:, 512 * k:512 * k + 512], b[:, :]))
                b = take("bt", i)
                emptied_by(act.copy(Btok, b[:, 0:P]))
                act.wait_ge(S["free_act"], emptied[index[("bt", i)]][1])
                act.sem_inc(S["xtok_ready"], 1)
                if full:
                    for g in range(2):
                        b = take("g", i, g)
                        emptied_by(act.copy(Gs2[g], b[:, 0:P]))
                    act.wait_ge(S["free_act"], emptied[index[("g", i, 1)]][1])
                    act.sem_inc(S["g_ready"], 1)
                    for u in range(8):
                        act.wait_ge(S["seg_ready"], 8 * nfull + u + 1)
                        A(dec[u % 2], dec[u % 2], ACT.Exp).then_inc(S["dec_ready"], 1)
                        if (i, u - 1) in ADA_AT:
                            copy_row(1, ADA_AT[i, u - 1])
                    if (i, 7) in ADA_AT:
                        copy_row(1, ADA_AT[i, 7])
                    act.wait_ge(S["ysq_ready"], nfull + 1)
                    link(A(zs3[:, t, :], ytok, ACT.Square, accum_out=ssd_r))
                    rsqrt(ssd_r, ssd_r, D).then_inc(S["ynorm_ready"], 1)
                    for k in range(2):
                        b = take("yT", i, k)
                        for c in range(4):
                            ins = A(oTy3[:, 4 * k + c, TILE[t]], b[:, P * c:P * c + P], ACT.Copy, scale=ssdn[:, 4 * k + c:4 * k + c + 1])
                        emptied_by(ins)
                    nfull += 1
            for k, n in ((0, 2 * P), (1, P)):
                b = take("sl", k)
                link(A(lr[k], b[:, 0:T], ACT.Ln, bias=EPS, scale=1.0 / n))
                act.sem_inc(S["free_act"], 1)
                A(lr[k], lr[k], ACT.Exp, scale=-0.5).then_inc(S["lr_ready"], 1)
            mkt3 = mkt.rearrange("p (h n) -> p h n", h=HM)

            def turn_qk(name, i, out):
                for hh in range(2):
                    b = take(name, i, hh)
                    act.copy(out(hh), b[0:QM, :].rearrange("p (h n) -> p h n", h=4)).then_inc(S["qkT_ready"], 1)
                    act.wait_ge(S["qkT_ready"], 2 * (i + (NT if name == "kT" else 0)) + hh + 1)
                    act.sem_inc(S["free_act"], 1)

            for t in range(NT):
                for hh in range(2):
                    b = take("q", t, hh)
                    emptied_by(act.copy(mkt[:, 384 * hh:384 * hh + 384], b[:, 0:384]))
                act.wait_ge(S["free_act"], emptied[index[("q", t, 1)]][1])
                act.sem_inc(S["qt_copied"], 1)
                qk_rsqrt(t, mss, QM, QM ** -0.5)
                turn_qk("qT", t, lambda hh: mqT3[0:QM, 4 * hh:4 * hh + 4, TILE[t]])
            for s in range(4):
                for hh in range(2):
                    b = take("kv", s, hh)
                    b3 = b[:, :].rearrange("p (h n) -> p h n", h=4)
                    act.copy(mkt3[:, 4 * hh:4 * hh + 4, 0:NOPE], b3[:, :, 0:NOPE])
                    emptied_by(act.copy(mv3[:, KSLOT[s], 256 * hh:256 * hh + 256].rearrange("p (h n) -> p h n", h=4), b3[:, :, NOPE:P]))
                act.wait_ge(S["free_act"], emptied[index[("kv", s, 1)]][1])
                act.sem_inc(S["qt_copied"], 1)
                qk_rsqrt(NT + s, mss, QM, 1.0)
                turn_qk("kT", s, lambda hh: mkT3[0:QM, 4 * hh:4 * hh + 4, P * KSLOT[s]:P * KSLOT[s] + P])
            attention("mla", HM, m_att)
            moe(0)
            norm(1, 0)
            for s in range(1, N_INO, 2):
                for t in range(NT):
                    b = take("in", s, t)
                    if s == 1 and t == 0:
                        act.wait_ge(S["xr_used"], 2)
                    act.copy(qkv3[:, t, 384 * s:384 * s + 384], b[:, 0:384]).then_inc(S["qkv_ready"], 1)
                    act.wait_ge(S["qkv_ready"], NT * (s // 2) + t + 1)
                    act.sem_inc(S["free_act"], 1)

            n_t = [2 * (NT + 4)]

            def turn_gqa(out, *name):
                b = take(*name)
                n_t[0] += 1
                act.copy(out, b[:, :].rearrange("p (h n) -> p h n", h=4)).then_inc(S["qkT_ready"], 1)
                act.wait_ge(S["qkT_ready"], n_t[0])
                act.sem_inc(S["free_act"], 1)

            for t in range(NT):
                qk_rsqrt(NT + 4 + 2 * t, gss[:, 0:HQ], HD, HD ** -0.5)
                for k in range(2):
                    turn_gqa(gqT3[:, 4 * k:4 * k + 4, TILE[t]], "gqT", t, k)
                qk_rsqrt(NT + 4 + 2 * t + 1, gss[:, 0:HKV], HD, 1.0)
                turn_gqa(gkT3[:, :, P * KSLOT[t]:P * KSLOT[t] + P], "gkT", t)
            turn_gqa(gkT3[:, :, P * KSLOT[3]:P * KSLOT[3] + P], "gkT", 3)
            attention("gqa", HQ, g_att)
            moe(1)

        @block.vector
        def _(dve):
            n_chain, n_taken = [0], [0]
            mine = [j for j, (_, by) in enumerate(jobs) if by == "D"]

            def link(ins):
                n_chain[0] += 1
                ins.then_inc(S["chain_dve"], 1)
                dve.wait_ge(S["chain_dve"], n_chain[0])

            def take(*name):
                j = mine[n_taken[0]]
                assert jobs[j][0] == name, (jobs[j], name)
                dve.wait_ge(S["job_done"], j + 1)
                n_taken[0] += 1
                return bank(j)

            def emptied_by(ins):
                ins.then_inc(S["free_dve"], 1)

            def after(*name):
                dve.wait_ge(S["job_done"], index[name] + 1)

            tt, ts, stt = dve.tensor_tensor, dve.tensor_scalar, dve.scalar_tensor_tensor

            def spread(ap, n):
                return ap.unsqueeze(2).broadcast_to([ap.shape[0], ap.shape[1], n])

            def over(ap, n):
                return ap.unsqueeze(1).broadcast_to([ap.shape[0], n, ap.shape[1]])

            def cut(ap, n):
                return ap.rearrange("p (h n) -> p h n", h=n)

            def modulation(l):
                dve.wait_ge(S["ada_done"], l + 1)
                b_ada = sm("b_ada")[:, 48 * l:48 * l + 48]
                tt(mod[l].rearrange("p (c n) -> p c n", n=2), ps[:, 7, 384:480].rearrange("p (c n) -> p c n", n=2),
                   spread(b_ada, 2), ADD).then_inc(S["mod_ready"], 1)
                dve.wait_ge(S["mod_ready"], l + 1)

            def norm(l, i):
                g = sm("g_ffn" if i else "g_mix")[:, DC * l:DC * l + DC]
                sc = mod[l][:, 16 * (3 * i + 1):16 * (3 * i + 2)]
                ab = AB[:, 16 * i:16 * i + 16]
                link(stt(cut(ab, 8), cut(sc, 8), 1.0, spread(g, 2), ADD, MUL))
                dve.wait_ge(S["r_ready"], 2 * l + i + 1)
                if l == 0 and i == 0:
                    dve.wait_ge(S["in_x"], 16)
                for c in range(DC):
                    for s in range(2):
                        ins = stt(hT[:, c, SEG[s]], xT[:, c, SEG[s]], ab[:, 2 * c + s:2 * c + s + 1], rn[:, SEG[s]], MUL, MUL)
                    ins.then_inc(S["h_scaled"], 1)

            def residual(l, part, name):
                gt = mod[l][:, 16 * part:16 * part + 16]
                for c in range(DC):
                    b = take(name, l, c)
                    for s in range(2):
                        ins = stt(xT[:, c, SEG[s]], b[:, SEG[s]], gt[:, 2 * c + s:2 * c + s + 1], xT[:, c, SEG[s]], MUL, ADD)
                    ins.then_inc(S["x_new"], 1)
                    dve.wait_ge(S["x_new"], DC * (2 * l + (part == 5)) + c + 1)
                    dve.sem_inc(S["free_dve"], 1)

            def rope(x, cos, sin, tmp, nh, n):
                q = n // 4
                x5 = x.rearrange("p h (a f n) -> p h a f n", a=2, f=2)
                t5 = tmp.rearrange("p h (a f n) -> p h a f n", a=2, f=2)
                s4 = sin.rearrange("p (a f n) -> p a f n", a=2, f=2)
                for a in range(2):
                    for f in range(2):
                        ins = tt(t5[:, :, a, f, :], x5[:, :, a, 1 - f, :], over(s4[:, a, f, :], nh), MUL)
                link(ins)
                link(tt(x, x, over(cos, nh), MUL))
                link(tt(x, x, tmp, ADD))

            def qk_norm(n_step, x, nh, n, gain, ss, tmp, cos, sin, rope_at):
                link(tt(tmp, x, x, MUL))
                dve.tensor_reduce(ss, tmp, AX.X, ADD).then_inc(S["qk_sq"], 1)
                dve.wait_ge(S["qk_r"], n_step + 1)
                link(tt(x, x, spread(ss, n), MUL))
                link(tt(x, x, over(gain, nh), MUL))
                if cos is not None:
                    rope(x[:, :, rope_at:n], cos, sin, tmp[:, :, rope_at:n], nh, n - rope_at)

            def attention(kind, heads, places, out):
                Pb, PTb, nm, rs = places
                base = 0 if kind == "mla" else NT * HM
                pairs = 0 if kind == "mla" else HM // 2
                for n in ("ckv", "kpe") if kind == "mla" else ():
                    dve.wait_ge(outs[n], 16)
                n_u = NT * heads
                for u in range(n_u + 1):
                    if u < n_u:
                        after(kind, "s", u)
                        dve.tensor_reduce(nm[:, u:u + 1], bank(index[(kind, "s", u)])[:, 0:KEYS[u % NT][1]], AX.X, MAX, negate=True).then_inc(S["max_ready"], 1)
                    v = u - 1
                    if v >= 0:
                        nk = KEYS[v % NT][1]
                        dve.wait_ge(S["e_ready"], base + v + 1)
                        link(dve.reciprocal(rs[:, v:v + 1], rs[:, v:v + 1]))
                        p = Pb[:, 384 * (v % 4):384 * (v % 4) + nk]
                        ts(p, p, rs[:, v:v + 1], None, MUL).then_inc(S["p_ready"], 1)
                    w = v - 8
                    if w >= 0 and w % 6 == 0:
                        pair_out(w // 6, pairs, base, out)
                for k in range((n_u - 1 - 8) // 6 + 1, heads // 2):
                    pair_out(k, pairs, base, out)

            def pair_out(k, pairs, base, out):
                dve.wait_ge(S["pv_done"], base // NT + 2 * k + 2)
                dve.tensor_copy(out[:, k, :], ps[:, 5 + (pairs + k) % 2, 0:T]).then_inc(S["o_ready"], 1)

            def gates_of(l):
                fw = sm("first_wins")
                s, sel, msel, key, oh1, ms2, oh2 = rt48[1], rt48[2], rt48[3], rt48[4], rt48[5], rt48[6], rt48[7]
                cut3 = lambda ap: ap.rearrange("p (t n) -> p t n", t=NT)
                b = take("rtT", l)
                ts(s, b[:, 0:48], 1.0, None, ADD).then_inc(S["free_dve"], 1)
                dve.wait_ge(S["free_dve"], emptied[index[("rtT", l)]][1])
                link(dve.reciprocal(s, s))
                link(tt(cut3(sel), cut3(s), over(sm("router_bias"), NT), ADD))
                v = sel.rearrange("p (q n) -> p q n", n=GS)
                a, b_, c, d = (v[:, :, i] for i in range(4))
                link(tt(rt12[0], a, b_, MAX))
                link(tt(rt12[1], a, b_, MIN))
                link(tt(rt12[2], c, d, MAX))
                link(tt(rt12[3], c, d, MIN))
                link(tt(rt12[4], rt12[0], rt12[2], MAX))
                link(tt(rt12[5], rt12[0], rt12[2], MIN))
                link(tt(rt12[6], rt12[1], rt12[3], MAX))
                link(tt(rt12[7], rt12[5], rt12[6], MAX))
                link(tt(rt12[8], rt12[4], rt12[7], ADD))

                def pick(out, src, n, weights, m):
                    link(dve.tensor_reduce(m[0], cut3(src), AX.X, MAX))
                    link(tt(cut3(out), cut3(src), spread(m[0], n), EQ))
                    link(tt(cut3(out), cut3(out), over(weights, NT), MUL))
                    link(dve.tensor_reduce(m[1], cut3(out), AX.X, MAX))
                    link(tt(cut3(out), cut3(out), spread(m[1], n), EQ))

                pick(rt12[9], rt12[8], NG, fw[:, 0:NG], rt3[0:2])
                link(tt(msel.rearrange("p (q n) -> p q n", n=GS), v, spread(rt12[9], GS), MUL))
                link(ts(rt12[10], rt12[9], -1.0, BIG, ADD, MUL))
                link(tt(msel.rearrange("p (q n) -> p q n", n=GS), msel.rearrange("p (q n) -> p q n", n=GS), spread(rt12[10], GS), ADD))
                pick(oh1, msel, NE, fw[:, NG:], rt3[2:4])
                link(stt(ms2, oh1, -3 * BIG, msel, MUL, ADD))
                pick(oh2, ms2, NE, fw[:, NG:], rt3[4:6])
                link(tt(oh1, oh1, oh2, ADD))
                link(tt(oh1, oh1, s, MUL))
                link(dve.tensor_reduce(rt3[6], cut3(oh1), AX.X, ADD))
                link(dve.reciprocal(rt3[7], rt3[6]))
                link(tt(cut3(gates), cut3(oh1), spread(rt3[7], NE), MUL))
                dve.sem_inc(S["gates_ready"], 1)
                link(dve.memset(rt[:, 888:915], 0.0))
                for t in range(NT):
                    link(dve.tensor_copy(gates_g[:, 0:48].rearrange("p (g t e) -> p g t e", g=NG, t=NT)[:, :, t, :],
                                         gates[:, NE * t:NE * t + NE].rearrange("p (g e) -> p g e", g=NG)))
                b = take("pos", l)
                by_tg = lambda ap: ap.rearrange("p (t g) -> p t g", t=NT)
                link(tt(pos_g[:, 0:12].rearrange("p (g t) -> p t g", g=NG), by_tg(b[:, 0:12]), by_tg(rt12[9]), MUL))
                for n in range(2):
                    link(ts(flags_f.rearrange("p (g n) -> p g n", n=2)[:, :, n], b[:, 12:16], float(P * (n + 1)), None, ALU.is_gt))
                link(dve.tensor_copy(flags, flags_f))
                dve.sem_inc(S["free_dve"], 1)
                dve.sem_inc(S["flags_ready"], 1)

            def moe(l):
                norm(l, 1)
                for n in ("gk", "gv") if l else ("ckv", "kpe"):
                    dve.wait_ge(outs[n], 16)
                gates_of(l)
                gt = mod[l][:, 16 * 5:16 * 6]

                def select(b):
                    for t in range(NT):
                        ins = ts(sel[:, P * t:P * t + P], sm("slots"), float(P * b), pcol[:, t:t + 1], ADD, EQ)
                    return ins

                dve.tensor_copy(gcur, gates_g[:, 0:NT * GS])
                link(dve.tensor_copy(pcol, pos_g[:, 0:NT]))
                select(0).then_inc(S["sel_ready"], 1)
                with dve.Fori(0, NG) as g:
                    def count(per_group, n):
                        return g * per_group + (per_group * NG * l + n)

                    def gather(b):
                        if b:
                            select(b).then_inc(S["sel_over_ready"], 1)
                        dve.wait_ge(S["xg1_done"], count(NT, b + 1))
                        dve.tensor_copy(xg[:, 512:1024], ps[:, 5, :]).then_inc(S["xg_by_dve"], 1)
                        dve.wait_ge(S["selT_done"], count(NT, b + 1))
                        dve.tensor_copy(gslot[:, GS * b:GS * b + GS], ps[:, 6, 0:GS])
                        dve.wait_ge(S["xgT0_done"], count(NT, b + 1))
                        dve.tensor_copy(xgT3[:, b, 0:512], ps[:, 2, :]).then_inc(S["xgT_by_dve"], 1)

                    def product(e, b, M, at_, bank_, per, n):
                        dve.wait_ge(M["sil_ready"], count(per, n + 1))
                        stt(act_of[at_], ps[:, bank_, 256:512], gslot[:, GS * b + e:GS * b + e + 1],
                            sil_of[at_], MUL, MUL).then_inc(M["act_ready"], 1)

                    def add(e, b, M, bank_y, per, n):
                        for h in range(2):
                            dve.wait_ge(M["dn_done"], count(2 * per, 2 * n + h + 1))
                            y = yacc3[:, b, 512 * h:512 * h + 512]
                            if e:
                                ins = tt(y, y, ps[:, bank_y + h, :], ADD)
                            else:
                                ins = dve.tensor_copy(y, ps[:, bank_y + h, :])
                            ins.then_inc(M["acc_ready"], 1)

                    def scatter(b):
                        for c in range(DC):
                            dve.wait_ge(S["sc_done"], count(NT * DC, DC * b + c + 1))
                            for q in range(2):
                                ins = stt(xT[:, c, SEG[q]], ps[:, SC_BANK[c % 4], SEG[q]], gt[:, 2 * c + q:2 * c + q + 1], xT[:, c, SEG[q]], MUL, ADD)
                            ins.then_inc(S["sc_used"], 1)

                    over = [dve.value_load(flags[0:1, bass.ds(g * 2 + b, 1)], min_val=0, max_val=1) for b in range(2)]
                    gather(0)
                    for b in (1, 2):
                        with dve.If(over[b - 1]):
                            gather(b)
                        with dve.Else():
                            for k in ("xg_by_dve", "xgT_by_dve"):
                                dve.wait_ge(S[k], count(NT, b))
                                dve.sem_inc(S[k], 1)
                            if b == 2:
                                dve.wait_ge(S["sel_over_ready"], count(2, 1))
                            dve.sem_inc(S["sel_over_ready"], 1)
                    for e in range(GS):
                        product(e, 0, MAIN, e % 2, e % 2, GS, e)
                        if e:
                            add(e - 1, 0, MAIN, 4, GS, e - 1)
                        for b in (1, 2):
                            n = 2 * e + b - 1
                            with dve.If(over[b - 1]):
                                product(e, b, OVER, 2, 3, 2 * GS, n)
                                add(e, b, OVER, 6, 2 * GS, n)
                            with dve.Else():
                                for k, m in (("act_ready", 1), ("acc_ready", 2)):
                                    if n:
                                        dve.wait_ge(OVER[k], count(2 * GS * m, n * m))
                                    dve.sem_inc(OVER[k], m)
                    dve.tensor_copy(gcur, gates_g[:, bass.ds(g * (NT * GS) + NT * GS, NT * GS)])
                    dve.tensor_copy(pcol, pos_g[:, bass.ds(g * NT + NT, NT)]).then_inc(S["gcur_ready"], 1)
                    dve.wait_ge(S["gcur_ready"], g + (NG * l + 1))
                    select(0).then_inc(S["sel_ready"], 1)
                    add(GS - 1, 0, MAIN, 4, GS, GS - 1)
                    scatter(0)
                    for b in (1, 2):
                        with dve.If(over[b - 1]):
                            scatter(b)
                        with dve.Else():
                            dve.wait_ge(S["sc_used"], count(NT * DC, DC * b))
                            dve.sem_inc(S["sc_used"], DC)
                dve.wait_ge(S["sc_used"], NT * DC * NG * (l + 1))
                dve.sem_inc(S["x_new"], DC)

            dve.wait_ge(S["in_small"], 16)
            modulation(0)
            norm(0, 0)
            dve.wait_ge(S["h_scaled"], DC)
            for i in range(2):
                for c in (0, 129, 386):
                    link(dve.memset(xr[i][:, c:c + 1], 0.0))
            dve.sem_inc(S["xr_used"], 1)
            b = take("dk")
            emptied_by(dve.tensor_copy(dk, b[:, 0:144]))
            dve.wait_ge(S["free_dve"], 1)
            dve.sem_inc(S["dk_copied"], 1)
            cw = sm("conv_w")
            for c in range(CONV_C):
                dve.wait_ge(S["xr_ready"], c + 1)
                r, o = xr[c % 2], xc3[:, c, :]
                link(ts(o, r[:, 1:386], cw[:, CONV_C + c:CONV_C + c + 1], None, MUL))
                link(stt(o, r[:, 0:385], cw[:, c:c + 1], o, MUL, ADD))
                stt(o, r[:, 2:387], cw[:, 2 * CONV_C + c:2 * CONV_C + c + 1], o, MUL, ADD).then_inc(S["xc_raw"], 1)
            for c in range(3):
                b = take("lat", c)
                emptied_by(dve.tensor_copy(latT[:, c, :], b[:, 0:T]))
            def by_tile(ap, d):
                return ap[:, 48 * d:48 * d + 48].rearrange("p (t n) -> p t n", t=NT)

            for d in range(2):
                link(tt(by_tile(e96[0], d), dk3[:, :, 0:HS], over(sm("dt_bias")[:, HS * d:HS * d + HS], NT), ADD))
            link(ts(e96[1], e96[0], -1.0, None, MUL))
            tt(e96[1], e96[0], e96[1], MIN).then_inc(S["e_in"], 1)
            dve.wait_ge(S["e_mid"], 1)
            link(stt(e96[2], e96[0], 0.0, e96[1], MAX, ADD))
            for d in range(2):
                link(stt(by_tile(e96[3], d), by_tile(e96[2], d), -1.0, over(e96[6][:, HS * d:HS * d + HS], NT), MUL, MUL))
            dve.sem_inc(S["dt_ready"], 1)
            b = take("cum")
            emptied_by(ts(e96[4], b[:, 0:96], -1.0, None, MUL))
            dve.wait_ge(S["free_dve"], emptied[index[("cum",)]][1])
            b = take("tot")
            link(tt(e96[9], b[:, 0:96], e96[4], ADD))
            emptied_by(dve.tensor_copy(e96[6], b[:, 0:96]))
            dve.wait_ge(S["free_dve"], emptied[index[("tot",)]][1])
            dve.sem_inc(S["cum_copied"], 1)
            dve.wait_ge(S["e_cum"], 1)
            link(tt(e96[7], e96[2], e96[9], MUL))
            nfull = 0
            for i, (t, full) in enumerate(STEPS):
                dve.wait_ge(S["xtok_ready"], i + 1)
                col = lambda d: slice(48 * d + HS * t, 48 * d + HS * t + HS)
                if full:
                    base = 8 * nfull
                    for d in range(2):
                        link(tt(cut(xdt[d], HS), cut(xtok, HS), spread(e96[2][:, col(d)], PS), MUL))

                    def segment(u):
                        q, d = u // 2, u % 2
                        b = take("bc", i, u)
                        if u >= 2:
                            dve.wait_ge(S["diag_done"], base + u - 1)
                        for h in range(4):
                            c = 48 * d + HS * t + 4 * q + h
                            ins = stt(dec[d][:, P * h:P * h + P], b[:, P * h:P * h + P], e96[4][:, c:c + 1], mask[d], ADD, ADD)
                        ins.then_inc(S["seg_ready"], 1)
                        dve.wait_ge(S["seg_ready"], base + u + 1)
                        dve.sem_inc(S["free_dve"], 1)

                    def scores(u):
                        q, d = u // 2, u % 2
                        dve.wait_ge(S["dec_ready"], base + u + 1)
                        if u == 0:
                            dve.wait_ge(S["g_ready"], nfull + 1)
                        tt(cut(dec[d], 4), cut(dec[d], 4), over(Gs2[q // 2], 4), MUL).then_inc(S["s_ready"], 1)

                    segment(0)
                    for u in range(8):
                        if u + 1 < 8:
                            segment(u + 1)
                        scores(u)
                    dve.wait_ge(S["diag_done"], base + 8)
                    link(tt(cut(ytok, HS), cut(xtok, HS), spread(sm("d_skip"), PS), MUL))
                    link(tt(ytok, ytok, ps[:, 5:7, :].rearrange("p a n -> p (a n)"), ADD))
                    if t:
                        for d in range(2):
                            for g in range(2):
                                b = take("off", i, d, g)
                                link(tt(cut(ytmp, 8), cut(b[:, 0:512], 8), spread(e96[5][:, 48 * d + HS * t + 8 * g:48 * d + HS * t + 8 * g + 8], PS), MUL))
                                dve.sem_inc(S["free_dve"], 1)
                                link(tt(ytok[:, 512 * g:512 * g + 512], ytok[:, 512 * g:512 * g + 512], ytmp, ADD))
                    dve.wait_ge(S["z_ready"], 3 * NT)
                    tt(ytok, ytok, zs3[:, t, :], MUL).then_inc(S["ysq_ready"], 1)
                    dve.wait_ge(S["ynorm_ready"], nfull + 1)
                    ts(ytok, ytok, ssd_r[:, 0:1], None, MUL).then_inc(S["ynormed"], 1)
                    after("yT", i, 1)
                    nfull += 1
                for d in STATES[i]:
                    link(tt(cut(xw, HS), cut(xtok, HS), spread(e96[7][:, col(d)], PS), MUL))
                    dve.sem_inc(S["xw_ready"], 1)
                    b = take("st", i, d)
                    for g in range(2):
                        r = slice(64 * g, 64 * g + 64)
                        dst = {(2, 1): s_b1, (1, 0): h0[0], (0, 0): h0[0], (0, 1): h0[1]}[t, d]
                        if t == 0:
                            ins = dve.tensor_copy(dst[r, :], b[r, :])
                        else:
                            cd = e96[8][r, 48 * d + HS * t + 8 * g:48 * d + HS * t + 8 * g + 8]
                            link(tt(cut(dst[r, :], 8), cut(h0[d][r, :], 8), spread(cd, PS), MUL))
                            ins = tt(dst[r, :], dst[r, :], b[r, :], ADD)
                        link(ins)
                    dve.sem_inc(S["free_dve"], 1)
                    dve.sem_inc(S["st_done"], 1)
                dve.sem_inc(S["xtok_used"], 1)
            tt(lsq, lat, lat, MUL).then_inc(S["lsq_ready"], 1)
            dve.wait_ge(S["lr_ready"], 2)
            for c in range(3):
                g = sm("q_a_norm")[:, c:c + 1] if c < 2 else sm("kv_a_norm")
                ins = stt(latT[:, c, :], latT[:, c, :], g, lr[c // 2], MUL, MUL)
            ins.then_inc(S["latn_ready"], 1)
            mkt3, msq3 = cut(mkt, HM), cut(msq, HM)
            rot = lambda n, t, w: sm(n)[:, w * (t - 1):w * t]
            for k in range(NT + 4):
                s = k - NT
                dve.wait_ge(S["qt_copied"], k + 1)
                if s >= 0:
                    kpe = dk3[:, s, HS:48] if s < NT else sm("kpe_cache")
                    link(dve.tensor_copy(mkt3[:, :, NOPE:QM], over(kpe, HM)))
                t = k if s < 0 else s
                on = t in (1, 2)
                qk_norm(k, mkt3, HM, QM, sm("q_norm" if s < 0 else "k_norm"), mss, msq3,
                        rot("cos_e", t, ROPE) if on else None, rot("sin_e", t, ROPE) if on else None, NOPE)
                dve.sem_inc(S["qk_ready"], 1)
            attention("mla", HM, m_att, oTm3)
            modulation(1)
            residual(0, 2, "out")
            moe(0)
            norm(1, 0)
            for n in ("ckv", "kpe", "stf", "stb"):
                dve.wait_ge(outs[n], 16)
            dve.sem_inc(S["xr_used"], 1)
            for s in range(0, N_INO, 2):
                for t in range(NT):
                    b = take("in", s, t)
                    emptied_by(dve.tensor_copy(qkv3[:, t, 384 * s:384 * s + 384], b[:, 0:384]))
            dve.wait_ge(S["free_dve"], emptied[index[("in", 2, NT - 1)]][1])
            dve.wait_ge(S["qkv_ready"], 2 * NT)
            step = NT + 4
            for t in range(NT):
                for x, nh, g in ((qkv3[:, t, 0:1024], HQ, "gq_norm"), (qkv3[:, t, 1024:1280], HKV, "gk_norm")):
                    qk_norm(step, cut(x, nh), nh, HD, sm(g), gss[:, 0:nh], cut(gsq[:, 0:HD * nh], nh),
                            rot("cos_o", t, HD) if t else None, rot("sin_o", t, HD) if t else None, 0)
                    if nh == HKV:
                        if t:
                            after("gkT", t - 1)
                        for i in range(2):
                            link(dve.tensor_copy(cut(gkt, HKV)[:, :, 64 * i:64 * i + 64], cut(x, HKV)))
                    dve.sem_inc(S["qk_ready"], 1)
                    step += 1
            after("gkT", NT - 1)
            for i in range(2):
                link(dve.tensor_copy(cut(gkt, HKV)[:, :, 64 * i:64 * i + 64], cut(sm("k_cache"), HKV)))
            dve.sem_inc(S["qk_ready"], 1)
            attention("gqa", HQ, g_att, oT3)
            residual(1, 2, "out")
            moe(1)

        @block.gpsimd
        def _(pool):
            def sum_chunks(l, i):
                n = 2 * l + i
                for c in range(1, DC):
                    pool.wait_ge(S["sq_ready"], DC * n + c + 1)
                    if c > 1:
                        pool.wait_ge(S["sq_sum"], (DC - 1) * n + c - 1)
                    pool.tensor_tensor(sq_acc, hT[:, 0, :] if c == 1 else sq_acc, hT[:, c, :], ADD).then_inc(S["sq_sum"], 1)

            sum_chunks(0, 0)
            pool.wait_ge(S["dk_copied"], 1)
            pool.dma_start(kpe_d, dk3[:, 0, HS:48]).then_inc(outs["kpe"], 16)
            pool.wait_ge(S["st_done"], 4)
            pool.dma_start(stf_d, h0[0]).then_inc(outs["stf"], 16)
            pool.dma_start(stb_d, h0[1]).then_inc(outs["stb"], 16)
            pool.wait_ge(S["latn_ready"], 1)
            pool.dma_start(ckv_d, latT[:, 2, 0:P]).then_inc(outs["ckv"], 16)
            for l, i in ((0, 1), (1, 0)):
                sum_chunks(l, i)
            pool.wait_ge(S["qk_ready"], NT + 4 + 2)
            pool.dma_start(gk_d, qkv3[:, 0, 1024:1280]).then_inc(outs["gk"], 16)
            pool.dma_start(gv_d, qkv3[:, 0, 1280:1536]).then_inc(outs["gv"], 16)
            sum_chunks(1, 1)


def _constants():
    f = np.float32
    j, i = np.arange(P)[:, None], np.arange(P)[None, :]
    c = {"ident": (i == j).astype(f), "ones": np.ones((P, P), f),
         "tri_f": (j <= i).astype(f), "tri_b": (j >= i).astype(f),
         "mask_f": np.where(j <= i, f(0), f(-BIG)), "mask_b": np.where(j >= i, f(0), f(-BIG)),
         "slots": np.tile(np.arange(1, P + 1).astype(f), (P, 1)),
         "first_wins": np.tile(np.concatenate([np.arange(NG, 0, -1), np.arange(NE, 0, -1)]).astype(f), (P, 1))}
    tok = np.arange(2 * P)
    for name, n in (("e", ROPE), ("o", HD)):
        half = n // 4
        inv = np.power(f(THETA), -np.arange(half, dtype=f) / f(half)).astype(f)
        cos, sin = [], []
        for pos in (tok // GRID_W, tok % GRID_W):
            ang = pos.astype(f)[:, None] * inv[None, :]
            cos += [np.cos(ang)] * 2
            sin += [-np.sin(ang), np.sin(ang)]
        for kind, parts in (("cos_", cos), ("sin_", sin)):
            a = np.concatenate(parts, axis=1).astype(f)
            c[kind + name] = a.reshape(2, P, n).transpose(1, 0, 2).reshape(P, 2 * n)
    return c


def _chunks(v):
    v = np.asarray(v)
    return np.ascontiguousarray(v.reshape(-1, P).T)


def _rows(v):
    return np.tile(np.asarray(v).reshape(1, -1), (P, 1))


def _kxn(w, cols):
    k, n = w.shape
    a = w.reshape(k // P, P, n // cols, cols).transpose(2, 1, 0, 3)
    return a.reshape(n // cols, P, -1)


def kernel(**inputs):
    import concourse.bacc as bacc
    from concourse.bass_utils import run_bass_kernel_spmd

    a = {k: np.asarray(v) for k, v in inputs.items()}
    w_in = a["w_in_even"][0]
    z, xbc, dt, ql, kv = np.split(w_in, (1024, 2304, 2320, 2576), axis=1)
    c = _constants()
    state = lambda s: s[0, 0].reshape(2, HG, PS, NS).transpose(0, 3, 1, 2).reshape(P, HG * PS)
    c.update(g_mix=_chunks(a["g_mix"]), g_ffn=_chunks(a["g_ffn"]), b_ada=_chunks(a["b_ada"]),
             conv_w=_chunks(a["ssd_conv_w"]), conv_b=_chunks(a["ssd_conv_b"]), ssd_norm=_chunks(a["ssd_norm"]),
             q_a_norm=_chunks(a["mla_q_a_norm"]), kv_a_norm=_chunks(a["mla_kv_a_norm"]),
             cond=np.stack([a["c_ctx"].reshape(DC, P), a["c"].reshape(DC, P)], axis=-1).transpose(1, 0, 2).reshape(P, 2 * DC),
             q_norm=_rows(a["mla_q_norm"]), k_norm=_rows(a["mla_k_norm"]), gq_norm=_rows(a["gqa_q_norm"]), gk_norm=_rows(a["gqa_k_norm"]),
             router_bias=_rows(a["router_bias"]),
             a_log=_rows(np.concatenate([a["ssd_a_log_fwd"][0], a["ssd_a_log_bwd"][0]])),
             dt_bias=_rows(np.concatenate([a["ssd_dt_bias_fwd"][0], a["ssd_dt_bias_bwd"][0]])),
             d_skip=_rows(a["ssd_d"]), ckv_cache=a["cache_mla_ckv"][0, 0].T, kpe_cache=a["cache_mla_kpe"][0, 0],
             k_cache=a["cache_gqa_k"][0, 0].reshape(P, -1), v_cache=a["cache_gqa_v"][0, 0].reshape(P, -1),
             h0=np.concatenate([state(a["state_ssd_fwd"]), state(a["state_ssd_bwd"])], axis=1),
             w_router=_kxn(a["w_router"], NE)[0], w_dk=_kxn(np.concatenate([dt, kv[:, P:]], axis=1), 48)[0],
             w_q_b=_kxn(a["mla_w_q_b"][0], 768)[0], w_kv_b=a["mla_w_kv_b"][0])
    small = np.concatenate([c[n].reshape(P, w) for n, w in SMALL], axis=1)

    slots = np.zeros((N_SLOTS, P, SLOT), w_in.dtype)
    for l, at in ((0, S_ADA0), (1, S_ADA1)):
        slots[at:at + N_ADA] = _kxn(a["w_ada"][l], 384)
    slots[S_INE:S_INE + N_INE] = _kxn(np.concatenate([xbc, ql, kv[:, :P], z], axis=1), 384)
    slots[S_OUTE:S_OUTE + N_OUTE] = _kxn(a["w_out_even"][0], 256)
    slots[S_INO:S_INO + N_INO] = _kxn(a["w_in_odd"][0], 384)
    wo = a["w_out_odd"][0]
    slots[S_OUTO:S_OUTO + 2] = _kxn(wo[:, :768], 384)
    slots[S_OUTO + 2, :, :2048] = _kxn(wo[:, 768:], 256)[0]
    for l, at in ((0, S_MOE0), (1, S_MOE1)):
        gu = np.concatenate([a["w_exp_gate"][l], a["w_exp_up"][l]], axis=2).reshape(NE, DC, P, 2 * FE).transpose(0, 2, 1, 3).reshape(NE, P, -1)
        dn = a["w_exp_down"][l].reshape(NE, 2, P, D).transpose(0, 2, 1, 3).reshape(NE, P, -1)
        slots[at:at + N_MOE] = np.concatenate([gu, dn], axis=2).reshape(NE, P, 2, SLOT).transpose(0, 2, 1, 3).reshape(N_MOE, P, SLOT)
    x = np.concatenate([a["x_prompt"][0], a["x_sample"][0]], axis=0)
    xt = np.ascontiguousarray(x.reshape(T, DC, P).transpose(2, 1, 0))

    nc = bacc.Bacc("TRN2", target_bir_lowering=False, num_devices=1)
    arrays = {"small_in": np.ascontiguousarray(small), "x_in": xt, "w_in": slots}
    ins = [nc.dram_tensor(n, v.shape, mybir.dt.from_np(v.dtype), kind="ExternalInput").ap() for n, v in arrays.items()]
    shapes = {"y_out": (P, DC, T), "stf_out": (P, HG * PS), "stb_out": (P, HG * PS), "ckv_out": (P, P), "kpe_out": (P, ROPE),
              "gk_out": (P, HKV * HD), "gv_out": (P, HKV * HD)}
    res = [nc.dram_tensor(n, s, mybir.dt.float32, kind="ExternalOutput").ap() for n, s in shapes.items()]
    build(nc, *ins, *res)
    r = run_bass_kernel_spmd(nc, [arrays], core_ids=[0]).results[0]
    y = np.asarray(r["y_out"]).transpose(2, 1, 0).reshape(T, D)
    unstate = lambda s: np.ascontiguousarray(np.asarray(s).reshape(2, NS, HG, PS).transpose(0, 2, 3, 1).reshape(1, 1, HS, PS, NS))
    return (np.ascontiguousarray(y[:P])[None], np.ascontiguousarray(y[P:])[None], unstate(r["stf_out"]), unstate(r["stb_out"]),
            np.ascontiguousarray(np.asarray(r["ckv_out"]).T)[None, None], np.asarray(r["kpe_out"])[None, None],
            np.asarray(r["gk_out"]).reshape(1, 1, P, HKV, HD), np.asarray(r["gv_out"]).reshape(1, 1, P, HKV, HD))
```

```python
from contextlib import ExitStack

import numpy as np

import concourse.bass as bass
from concourse import mybir

P = 128
D = 1024
DC = D // P
T = 384
NT = T // P
DEPTH = 2
EPS = 1e-6
HS, PS, NS = 16, 64, 64
HG = HS // 2
HM, NOPE, ROPE, VM = 8, 64, 32, 64
QM = NOPE + ROPE
HQ, HKV, HD = 16, 4, 64
NE, NG, GS, FE = 16, 4, 4, 256
GRID_W = 64
THETA = 10000.0
CONV_C = 10
SLOT = 3072
RING = 8
N_ADA, N_INE, N_OUTE, N_MOE, N_INO, N_OUTO = 16, 7, 4, 32, 4, 3
S_ADA0 = 0
N_FIRST = 6
S_INE = S_ADA0 + N_FIRST
S_ADA_LATE = S_INE + N_INE
S_OUTE = S_ADA_LATE + 2 * N_ADA - N_FIRST
S_MOE0 = S_OUTE + N_OUTE
S_INO = S_MOE0 + N_MOE
S_OUTO = S_INO + N_INO
S_MOE1 = S_OUTO + N_OUTO
N_SLOTS = S_MOE1 + N_MOE
BIG = 1e30

SMALL = [("ident", P), ("ones", P), ("cond", 2 * DC), ("g_mix", DEPTH * DC), ("b_ada", DEPTH * 48), ("tri_f", P), ("tri_b", P), ("mask_f", P), ("mask_b", P),
         ("cos_e", 2 * ROPE), ("sin_e", 2 * ROPE), ("cos_o", 2 * HD), ("sin_o", 2 * HD),
         ("g_ffn", DEPTH * DC), ("conv_w", 3 * CONV_C), ("conv_b", CONV_C),
         ("ssd_norm", DC), ("q_a_norm", 2), ("kv_a_norm", 1),
         ("q_norm", QM), ("k_norm", QM), ("gq_norm", HD), ("gk_norm", HD), ("router_bias", NE),
         ("a_log", 2 * HS), ("dt_bias", 2 * HS), ("d_skip", HS), ("first_wins", NG + NE),
         ("slots", P), ("ckv_cache", P), ("kpe_cache", ROPE), ("k_cache", HKV * HD), ("v_cache", HKV * HD), ("h0", 2 * HG * PS),
         ("w_router", DC * NE), ("w_dk", DC * 48), ("w_q_b", 2 * HM * QM), ("w_kv_b", HM * (NOPE + VM))]
OFF, _at = {}, 0
for _n, _w in SMALL:
    OFF[_n] = (_at, _w)
    _at += _w
N_SMALL = _at
N_SMALL_FIRST = OFF["tri_f"][0]


def build(nc, small_d, x_d, w_d, y_d, stf_d, stb_d, ckv_d, kpe_d, gk_d, gv_d):
    f32 = mybir.dt.float32
    ALU = mybir.AluOpType
    ACT = mybir.ActivationFunctionType
    AX = mybir.AxisListType
    MUL, ADD, MAX, MIN, EQ = ALU.mult, ALU.add, ALU.max, ALU.min, ALU.is_equal

    ctx = ExitStack()
    with ctx:
        sb = lambda name, n: ctx.enter_context(nc.sbuf_tensor(name, [P, n], f32))
        sem = lambda name: ctx.enter_context(nc.semaphore(name))
        ring = ctx.enter_context(nc.sbuf_tensor("ring", [P, RING, SLOT], f32))
        xT = ctx.enter_context(nc.sbuf_tensor("xT", [P, DC, T], f32))
        hTt = sb("hT", DC * T)
        small = sb("small", N_SMALL)
        misc = sb("misc", 256)
        U_SIZE = 15110
        U = sb("U", U_SIZE)
        ps = ctx.enter_context(nc.psum_tensor("ps", [P, 8, 512], f32))

        hT = hTt[:, :].rearrange("p (c t) -> p c t", c=DC)

        def sm(name):
            o, w = OFF[name]
            return small[:, o:o + w]

        ident, ones = sm("ident"), sm("ones")
        tri = [sm("tri_f"), sm("tri_b")]
        mask = [sm("mask_f"), sm("mask_b")]

        def region(base, *widths):
            out, at = [], base
            for w in widths:
                out.append(U[:, at:at + w])
                at += w
            assert at <= U_SIZE, at
            return out

        mod = [misc[:, 0:96], misc[:, 96:192]]
        condS = misc[:, 192:208]
        AB = misc[:, 208:240]
        ssd_r = misc[:, 240:241]
        zs, xc, oTy, oTm, lat, dk, e_sm = region(0, 3072, CONV_C * 385, 3072, 1536, 1152, 144, 1000)
        TAIL = 3072 + CONV_C * 385 + 3072 + 1536 + 1152 + 144 + 1000
        rn, _, sq_acc = region(TAIL, 384, 116, 384)
        mod_row = [U[0:2, TAIL + 896:TAIL + 1280], U[0:2, TAIL + 500:TAIL + 884]]
        xr = [region(TAIL + 387 * i, 387)[0] for i in range(2)]
        zs3 = zs.rearrange("p (t n) -> p t n", t=NT)
        xc3 = xc.rearrange("p (c t) -> p c t", c=CONV_C)
        oTy3 = oTy.rearrange("p (c t) -> p c t", c=8)
        oTm3 = oTm.rearrange("p (c t) -> p c t", c=4)
        latT = lat.rearrange("p (c t) -> p c t", c=3)
        dk3 = dk.rearrange("p (t n) -> p t n", t=NT)
        dk_f = e_sm[0:48, 0:T]
        e96 = [e_sm[:, 96 * i:96 * i + 96] for i in range(10)]
        xdt = [hTt[:, 0:1024], hTt[:, 1024:2048]]
        xtok = hTt[:, 2048:3072]
        dec = [oTm[:, 512 * i:512 * i + 512] for i in range(3)]
        xw = ytok = oTm[:, 0:1024]
        ytmp = oTm[:, 1024:1536]
        s_b1, Gs, Btok = region(TAIL, 512, 256, 128)
        h0 = [sm("h0")[:, 0:512], sm("h0")[:, 512:1024]]
        Gs2 = [Gs[:, 0:128], Gs[:, 128:256]]
        mkT, mv = region(0, HM * 512, 4 * HM * VM)
        mkT3 = mkT.rearrange("p (h n) -> p h n", h=HM)
        mv3 = mv.rearrange("p (s n) -> p s n", s=4)
        mqT3 = hTt[:, :].rearrange("p (h n) -> p h n", h=HM)
        mkt = [oTm[:, 768 * i:768 * i + 768] for i in range(2)]
        msq = [e_sm[:, 0:768], region(TAIL, 768)[0]]
        mss = [e_sm[:, 768:776], e_sm[:, 776:784]]
        m_att = region(3072 + CONV_C * 385 + 3072 + 1536, 4 * 384, 2 * 896, 24, 24)
        lsq, lr_both = hTt[:, 0:1152], hTt[:, 1152:1920]
        lr = [lr_both[:, 0:384], lr_both[:, 384:768]]
        qkv, gkT, oT, gkt0, gkt1, gkt2, gP, gPT, gnm, grs, gss = region(
            0, NT * 1536, HKV * 512, 3072, 512, 512, 512, 4 * 384, 2 * 896, 48, 48, NT * (HQ + HKV))
        gkt = [gkt0, gkt0, gkt1, gkt2]
        gsq = [oT[:, HQ * HD * t:HQ * HD * (t + 1)] for t in range(NT)] + [gP[:, HKV * HD * t:HKV * HD * (t + 1)] for t in range(NT)]
        gss = [gss[:, HQ * t:HQ * (t + 1)] for t in range(NT)] + [gss[:, NT * HQ + HKV * t:NT * HQ + HKV * (t + 1)] for t in range(NT)]
        g_att = [gP, gPT, gnm, grs]
        qkv3 = qkv.rearrange("p (t n) -> p t n", t=NT)
        gkT3 = gkT.rearrange("p (h n) -> p h n", h=HKV)
        gqT3 = hTt[:, :].rearrange("p (h n) -> p h n", h=8)
        oT3 = oT.rearrange("p (c t) -> p c t", c=8)
        htok, xg, xgT, S_sb, sel, yacc, sil, act_b, actT, rt = region(
            0, NT * D, D, NT * D, NT * T, NT * P, NT * D, 512, 512, 512, 1100)
        htok3 = htok.rearrange("p (t n) -> p t n", t=NT)
        xgT3 = xgT.rearrange("p (b n) -> p b n", b=NT)
        yacc3 = yacc.rearrange("p (b n) -> p b n", b=NT)
        rt48 = [rt[:, 48 * i:48 * i + 48] for i in range(12)]
        rt12 = [rt[:, 576 + 12 * i:576 + 12 * i + 12] for i in range(12)]
        rtT = sel[0:NE, 0:T]
        rt3 = [rt[:, 720 + 3 * i:720 + 3 * i + 3] for i in range(8)]
        gates = rt48[11]
        gates_g, pos_g = rt[:, 840:900], rt[:, 900:915]
        gslot = rt[:, 776:776 + NT * GS]
        gcur = rt[:, 824:824 + NT * GS]
        sil_of, act_of, actT_of = ([x[:, 0:256], x[:, 256:512], xg[:, 256 * i:256 * i + 256]] for i, x in enumerate((sil, act_b, actT)))
        pcol = rt[:, 804:807]
        flags_f = rt[:, 808:816]
        flags = rt[:, 816:824].bitcast(mybir.dt.int32)

        names = """in_first in_small in_x cond_ready ada_done mod_ready sq_ready r_ready h_ready slot_used job_done free_act
            free_dve chain_dve chain_act sq_sum h_scaled xr_ready xr_used xc_raw xc_ready z_ready dk_by_feature
            dk_copied e_in e_mid dt_ready cum_copied e_cum xtok_ready xtok_used g_ready seg_ready dec_ready s_ready
            diag_done xw_ready st_done ysq_ready ynorm_ready ynormed cache_keys gsq_ready lsq_ready lr_ready latn_ready
            qt_copied qk_sq qk_r qk_ready qkT_ready max_ready e_ready p_ready pt_ready pv_done o_ready x_new row_done
            row_copied qkv_ready rt_exp flags_ready group_found gcur_ready next_group""".split()
        S = {n: sem(n) for n in names}
        slot_full = [sem(f"slot_full{i}") for i in range(RING)]
        steps = """sel_ready xg0_done xg1_done selT_done xg_by_act xg_by_dve xgT0_done xgT1_done xgT_by_act xgT_by_dve
            au_done sil_ready act_ready tr_done trc_ready dn_done acc_ready sc_done sc_used""".split()
        PER_GROUP = {n: 1 for n in steps[:10]} | {n: GS for n in steps[10:15]} | {n: 2 * GS for n in steps[15:17]} | {n: DC for n in steps[17:]}
        BLOCK = [{n: sem(f"block{b}_{n}") for n in steps} for b in range(NT)]
        outs = {n: sem("stored_" + n) for n in ("y", "stf", "stb", "ckv", "kpe", "gk", "gv")}

        jobs = []

        def job(name, by):
            jobs.append((name, by))

        STEPS = [(2, False), (1, True), (2, True), (0, True)]
        STATES = [(1,), (0,), (), (0, 1)]

        N_PREP = NT + 4
        ORDER = [1, 2, 0]
        AHEAD = 3

        def attention_jobs(kind, heads):
            n = NT * heads
            for u in range(n + AHEAD):
                if u < n:
                    job((kind, "s", u), "A")
                if u >= AHEAD:
                    job((kind, "pT", u - AHEAD), "A")

        for l in range(DEPTH):
            job(("ss", l, 0), "A")
            if l == 0:
                job(("dk",), "D")
                for c in range(CONV_C):
                    job(("xbc", c), "A")
                    if c == 0:
                        job(("dkT",), "D")
                for c in range(3):
                    job(("lat", c), "D")
                for i in range(3):
                    for t in range(NT):
                        job(("z", i, t), "A")
                job(("cum",), "D")
                job(("tot",), "D")
                job(("sl", 0), "A")
                job(("sl", 1), "A")
                for i, (t, full) in enumerate(STEPS):
                    job(("xt", i, 0), "A")
                    job(("xt", i, 1), "A")
                    job(("bt", i), "A")
                    if full:
                        job(("g", i, 0), "A")
                        job(("g", i, 1), "A")
                        for u in range(8):
                            job(("bc", i, u), "D")
                        if t:
                            for d in range(2):
                                for g in range(2):
                                    job(("off", i, d, g), "D")
                        job(("yT", i, 0), "A")
                        job(("yT", i, 1), "A")
                    for d in STATES[i]:
                        job(("st", i, d), "D")
                for k in range(N_PREP + 1):
                    for hh in range(2):
                        if k < N_PREP:
                            job(("qkv", k, hh), "A")
                    for hh in range(2):
                        if k:
                            job(("qkT", k - 1, hh), "A")
                attention_jobs("mla", HM)
            else:
                for i in range(NT + 1):
                    for s in range(N_INO):
                        if i < NT:
                            job(("in", s, ORDER[i]), "A" if s % 2 else "D")
                    if i == 0:
                        job(("gkT", 3), "A")
                    if i:
                        job(("gqT", ORDER[i - 1], 0), "A")
                        job(("gqT", ORDER[i - 1], 1), "A")
                        job(("gkT", ORDER[i - 1]), "A")
                attention_jobs("gqa", HQ)
            for c in range(DC):
                job(("out", l, c), "D")
            job(("ss", l, 1), "A")
            job(("rt", l), "A")
            job(("rtT", l), "D")
            for j in range(2 * NT):
                job(("htok", l, j), "A")
            job(("pos", l), "D")
        RB = 5
        index = {n: i for i, (n, _) in enumerate(jobs)}
        assert len(index) == len(jobs)
        emptied, _cnt = [], {"A": 0, "D": 0}
        for n, by in jobs:
            _cnt[by] += 1
            emptied.append((by, _cnt[by]))
        free_of = {"A": S["free_act"], "D": S["free_dve"]}
        bank = lambda j: ps[:, j % RB, :]

        POINTS = [("dt", 1), ("cum", 1), ("state", 2)]
        for _i in (1, 2, 3):
            POINTS += [(("unit", _i, _u), 1) for _u in ((-1, 2, 5) if _i == 1 else (-1,))] + [(("tail", _i), 2), (("end", _i), 1)]
        POINTS += [(("mla", _k), 1) for _k in range(N_PREP + 1)]
        LATE = {}
        for _p, _n in POINTS:
            _done = sum(len(x) for x in LATE.values())
            LATE[_p] = list(range(N_FIRST + _done, N_FIRST + _done + _n))
        assert sum(len(x) for x in LATE.values()) == 2 * N_ADA - N_FIRST
        PARTS = [N_FIRST, N_ADA, 2 * N_ADA]
        SC_BANK = [6, 7, 4, 5]
        KSLOT = [0, 2, 3, 1]
        KEYS = [(0, 128), (128, 384), (128, 384)]
        XC0 = [0, 129, 257]
        TILE = [slice(P * t, P * t + P) for t in range(NT)]
        SEG = [slice(0, P), slice(P, T)]

        def by_size(engine, g, group):
            more = engine.value_load(flags[0:1, bass.ds(g * 2, 1)], min_val=0, max_val=1)
            with engine.If(more):
                still_more = engine.value_load(flags[0:1, bass.ds(g * 2 + 1, 1)], min_val=0, max_val=1)

                def beyond(step):
                    step(1)
                    with engine.If(still_more):
                        step(2)

                group(beyond)
            with engine.Else():
                group(lambda step: None)

        block = ctx.enter_context(nc.Block())

        @block.sync
        def _(sp):
            def load(n, at, wait):
                if wait is not None:
                    sp.wait_ge(S["slot_used"], wait)
                sp.dma_start(ring[:, at, :], w_d[bass.ds(n, 1), :, :].rearrange("a p n -> p (a n)")).then_inc(slot_full[at], 16)

            for n in range(RING):
                load(n, n, None)
                if n == 2:
                    sp.dma_start(xT[:, :, :], x_d).then_inc(S["in_x"], 16)
                if n == N_FIRST - 1:
                    sp.dma_start(small[:, N_SMALL_FIRST:], small_d[:, N_SMALL_FIRST:]).then_inc(S["in_small"], 16)
            with sp.Fori(1, N_SLOTS // RING) as i:
                for j in range(RING):
                    load(i * RING + j, j, i * RING + (j - RING + 1))
            for n in range(N_SLOTS // RING * RING, N_SLOTS):
                load(n, n % RING, n - RING + 1)
            sp.wait_ge(S["x_new"], 4 * DC)
            sp.dma_start(y_d, xT[:, :, :]).then_inc(outs["y"], 16)
            for n in outs:
                sp.wait_ge(outs[n], 16)

        @block.tensor
        def _(pe):
            at = [0]

            def fill(*name):
                j = at[0]
                assert jobs[j][0] == name, (jobs[j], name)
                if j >= RB:
                    by, n = emptied[j - RB]
                    pe.wait_ge(free_of[by], n)
                at[0] += 1
                return bank(j)

            def filled(ins):
                ins.then_inc(S["job_done"], 1)

            def slot(n):
                pe.wait_ge(slot_full[n % RING], 16 * (n // RING + 1))
                return ring[:, n % RING, :]

            def used(ins):
                ins.then_inc(S["slot_used"], 1)

            mm = pe.matmul

            def ada(n):
                if n == 0:
                    pe.wait_ge(S["cond_ready"], 1)
                if n in PARTS:
                    pe.wait_ge(S["mod_ready"], PARTS.index(n) + 1)
                late = n >= N_FIRST
                w = slot(S_ADA_LATE + n - N_FIRST if late else S_ADA0 + n).rearrange("p (k n) -> p k n", k=DC)
                row = ps[0:2, 7 if late else 5 + n % 2, 0:384]
                if late and n not in PARTS:
                    turn_row(n - 1)
                elif n >= 2 and not late:
                    pe.wait_ge(S["row_copied"], n - 1)
                for k in range(DC):
                    ins = mm(row, condS[:, 2 * k:2 * k + 2], w[:, k, :], start=(k == 0), stop=(k == DC - 1))
                ins.then_inc(S["row_done"], 1)
                if not late and n:
                    turn_row(n - 1)
                if n + 1 in PARTS:
                    turn_row(n)
                    pe.drain().then_inc(S["ada_done"], 1)

            def turn_row(n):
                pe.wait_ge(S["row_copied"], n + 1)
                for m in range(3):
                    c = 384 + 2 * (3 * (n % N_ADA) + m)
                    pe.transpose(ps[:, 7, c:c + 2], mod_row[0 if n >= N_FIRST else n % 2][:, P * m:P * m + P], ident[0:2, 0:2])

            def late_ada(*point):
                for n in LATE.get(point if len(point) > 1 else point[0], []):
                    ada(n)

            def sum_squares(l, i):
                b = fill("ss", l, i)
                if i:
                    pe.wait_ge(S["sq_sum"], (DC - 2) * (l + 1))
                    mm(b[:, 0:T], ones, sq_acc, start=True, stop=False)
                    pe.wait_ge(S["sq_ready"], DC * (2 * l + 2))
                    filled(mm(b[:, 0:T], ones, hT[:, DC - 1, :], start=False, stop=True))
                    return
                for k in range(DC):
                    pe.wait_ge(S["sq_ready"], 2 * DC * l + k + 1)
                    ins = mm(b[:, 0:T], ones, hT[:, k, :], start=(k == 0), stop=(k == DC - 1))
                filled(ins)

            def h_chunk(l, i, k):
                pe.wait_ge(S["h_ready"], DC * (2 * l + i) + k + 1)

            def project(name, out, lhs, rhs, n=DC):
                for k in range(n):
                    ins = mm(out, lhs(k), rhs(k), start=(k == 0), stop=(k == n - 1))
                return ins

            def attention(kind, heads, q_of, k_of, v_of, places):
                Pb, PTb = places[:2]
                base = 0 if kind == "mla" else NT * HM
                pairs = 0 if kind == "mla" else HM // 2
                for u in range(NT * heads + AHEAD):
                    if u < NT * heads:
                        h, t = u // NT, u % NT
                        k0, nk = KEYS[t]
                        b = fill(kind, "s", u)
                        filled(mm(b[:, 0:nk], q_of(t, h), k_of(h, k0, nk), start=True, stop=True))
                    v = u - AHEAD
                    if v >= 0:
                        h, t = v // NT, v % NT
                        pe.wait_ge(S["p_ready"], base + v + 1)
                        b = fill(kind, "pT", v)
                        for k in range(KEYS[t][1] // P):
                            ins = pe.transpose(b[:, P * k:P * k + P], Pb[:, 384 * (v % 4) + P * k:384 * (v % 4) + P * k + P], ident)
                        filled(ins)
                        if t == 1 and h:
                            values(kind, h - 1, base, pairs, v_of, PTb)
                values(kind, heads - 1, base, pairs, v_of, PTb)

            def values(kind, h, base, pairs, v_of, PTb):
                pe.wait_ge(S["pt_ready"], base + NT * (h + 1))
                pair = pairs + h // 2
                if h % 2 == 0 and pair >= pairs + 2:
                    pe.wait_ge(S["o_ready"], pair - 1)
                r = slice(64 * (h % 2), 64 * (h % 2) + 64)
                pt = PTb[:, 896 * (h % 2):896 * (h % 2) + 896]
                mm(ps[r, 5 + pair % 2, 0:P], v_of(0, h), pt[:, 0:P], start=True, stop=True)
                for k in range(NT):
                    ins = mm(ps[r, 5 + pair % 2, P:T], v_of(1 + k, h), pt[:, P + 256 * k:P + 256 * k + 256], start=(k == 0), stop=(k == NT - 1))
                ins.then_inc(S["pv_done"], 1)

            def project_out(l, n_k, cols, first, src):
                pe.wait_ge(S["o_ready"], HM // 2 + (HQ // 2 if l else 0))
                for j, n in enumerate(cols):
                    w = slot(first + j)[:, 0:n_k * P * n].rearrange("p (k n) -> p k n", k=n_k)
                    for m in range(n):
                        b = fill("out", l, sum(cols[:j]) + m)
                        ins = project("out", b[:, 0:T], lambda k: w[:, k, P * m:P * m + P], src, n_k)
                        filled(ins)
                    pe.drain().then_inc(S["slot_used"], 1)

            def moe(l):
                sum_squares(l, 1)
                b = fill("rt", l)
                wr = sm("w_router").rearrange("p (k e) -> p k e", k=DC)
                for k in range(DC):
                    h_chunk(l, 1, k)
                    ins = mm(b[0:NE, 0:T], wr[:, k, :], hT[:, k, :], start=(k == 0), stop=(k == DC - 1))
                filled(ins)
                pe.wait_ge(S["rt_exp"], l + 1)
                b = fill("rtT", l)
                for t in range(NT):
                    ins = pe.transpose(b[:, NE * t:NE * t + NE], rtT[:, TILE[t]], ident[0:NE, 0:NE])
                filled(ins)
                for j in range(2 * NT):
                    b = fill("htok", l, j)
                    for c in range(4):
                        ins = pe.transpose(b[:, P * c:P * c + P], hT[:, 4 * (j % 2) + c, TILE[j // 2]], ident)
                    filled(ins)
                pe.wait_ge(S["group_found"], l + 1)
                b = fill("pos", l)
                for t in range(NT):
                    for v in range(t + 1):
                        mm(b[:, NG * t:NG * t + NG], ones if v < t else tri[0], rt12[9][:, NG * v:NG * v + NG], start=(v == 0), stop=(v == t))
                for v in range(NT):
                    ins = mm(b[:, 12:16], ones, rt12[9][:, NG * v:NG * v + NG], start=(v == 0), stop=(v == NT - 1))
                filled(ins)
                for by in "AD":
                    pe.wait_ge(free_of[by], max([n for o, n in emptied[:at[0]] if o == by]))
                pe.wait_ge(S["mod_ready"], len(PARTS))
                pe.wait_ge(S["flags_ready"], l + 1)
                first = S_MOE1 if l else S_MOE0
                with pe.Fori(0, NG) as g:
                    def wait(b, step, n):
                        per = PER_GROUP[step]
                        pe.wait_ge(BLOCK[b][step], g * per + (per * NG * l + n))

                    def gather(b):
                        if b:
                            wait(b, "sel_ready", 1)
                        else:
                            pe.wait_ge(BLOCK[0]["sel_ready"], g + ((NG + 1) * l + 1))
                        if b:
                            wait(b - 1, "xgT_by_act", 1)
                            wait(b - 1, "xgT_by_dve", 1)
                        for h in range(2):
                            for t in range(NT):
                                ins = mm(ps[:, 4 + h, :], sel[:, P * t:P * t + P], htok3[:, t, 512 * h:512 * h + 512], start=(t == 0), stop=(t == NT - 1))
                            ins.then_inc(BLOCK[b]["xg1_done" if h else "xg0_done"], 1)
                        pe.wait_ge(S["gcur_ready"], g + ((NG + 1) * l + 1))
                        for t in range(NT):
                            mm(ps[:, 6, 0:GS], sel[:, P * t:P * t + P], gcur[:, GS * t:GS * t + GS], start=(t == 0), stop=(t == NT - 1))
                        for t in range(NT):
                            ins = pe.transpose(ps[:, 7, P * t:P * t + P], sel[:, P * t:P * t + P], ident)
                        ins.then_inc(BLOCK[b]["selT_done"], 1)
                        for h, by in enumerate(("xg_by_act", "xg_by_dve")):
                            wait(b, by, 1)
                            for c in range(4):
                                ins = pe.transpose(ps[:, 2 + h, P * c:P * c + P], xg[:, 512 * h + P * c:512 * h + P * c + P], ident)
                            ins.then_inc(BLOCK[b]["xgT1_done" if h else "xgT0_done"], 1)
                        if b:
                            wait(b, "xgT_by_act", 1)
                            wait(b, "xgT_by_dve", 1)

                    def up(e, b):
                        a1, a2 = (first + 2 * e) % RING, (first + 2 * e + 1) % RING
                        for k in range(DC):
                            if e == 0 and b == 0 and k % 4 == 0:
                                wait(0, "xgT_by_act" if k else "xgT_by_dve", 1)
                            w = ring[:, a1, 512 * k:512 * k + 512] if k < 6 else ring[:, a2, 512 * (k - 6):512 * (k - 6) + 512]
                            ins = mm(ps[:, 3 if b else e % 2, :], xgT3[:, b, P * k:P * k + P], w, start=(k == 0), stop=(k == DC - 1))
                            if e and b == 0 and k == 3:
                                turn_act(e - 1, 0)
                        ins.then_inc(BLOCK[b]["au_done"], 1)

                    def turn_act(e, b):
                        wait(b, "act_ready", e + 1)
                        for j in range(2):
                            ins = pe.transpose(ps[:, 3 if b else 2, P * j:P * j + P], act_of[2 if b else e % 2][:, P * j:P * j + P], ident)
                        ins.then_inc(BLOCK[b]["tr_done"], 1)

                    def down(e, b):
                        a2 = (first + 2 * e + 1) % RING
                        at_, bank_y = (2, 6) if b else (e % 2, 4)
                        wait(b, "trc_ready", e + 1)
                        for h in range(2):
                            if e:
                                wait(b, "acc_ready", 2 * e - 1 + h)
                            for j in range(2):
                                ins = mm(ps[:, bank_y + h, :], actT_of[at_][:, P * j:P * j + P],
                                         ring[:, a2, 1024 + 1024 * j + 512 * h:1024 + 1024 * j + 512 * h + 512], start=(j == 0), stop=(j == 1))
                            ins.then_inc(BLOCK[b]["dn_done"], 1)

                    def up_down(e, b):
                        up(e, b)
                        turn_act(e, b)
                        down(e, b)
                        wait(b, "acc_ready", 2 * e + 2)

                    def scatter(b):
                        for c in range(DC):
                            if c in (0, 3):
                                wait(b, "acc_ready", 2 * GS - (c == 0))
                            if c >= 4:
                                wait(b, "sc_used", c - 3)
                            mm(ps[:, SC_BANK[c % 4], 0:T], yacc3[:, b, P * c:P * c + P], S_sb[:, T * b:T * b + T],
                               start=True, stop=True).then_inc(BLOCK[b]["sc_done"], 1)
                        wait(b, "sc_used", DC)

                    def group(beyond):
                        gather(0)
                        beyond(gather)
                        for e in range(GS):
                            for a in (first + 2 * e, first + 2 * e + 1):
                                pe.wait_ge(slot_full[a % RING], g * 16 + 16 * (a // RING + 1))
                            if e >= 2:
                                wait(0, "act_ready", e - 1)
                            up(e, 0)
                            if e:
                                down(e - 1, 0)
                            beyond(lambda b: up_down(e, b))
                        turn_act(GS - 1, 0)
                        down(GS - 1, 0)
                        scatter(0)
                        beyond(scatter)

                    by_size(pe, g, group)

            pe.wait_ge(S["in_first"], 16)
            for n in range(N_FIRST):
                if n == N_FIRST - 1:
                    sum_squares(0, 0)
                ada(n)
            pe.wait_ge(S["in_small"], 16)
            wdk = sm("w_dk").rearrange("p (k n) -> p k n", k=DC)
            b = fill("dk")
            for k in range(DC):
                h_chunk(0, 0, k)
                ins = mm(b[0:48, 0:T], wdk[:, k, :], hT[:, k, :], start=(k == 0), stop=(k == DC - 1))
            filled(ins)
            for s in range(N_INE):
                w = slot(S_INE + s).rearrange("p (k n) -> p k n", k=DC)
                for m in range(3):
                    c = 3 * s + m
                    if c < 13:
                        b = fill("xbc", c) if c < CONV_C else fill("lat", c - CONV_C)
                        filled(project("in", b[:, 0:T], lambda k: w[:, k, P * m:P * m + P], lambda k: hT[:, k, :]))
                    if c == 0:
                        pe.wait_ge(S["dk_by_feature"], 1)
                        b = fill("dkT")
                        for t in range(NT):
                            ins = pe.transpose(b[:, 48 * t:48 * t + 48], dk_f[:, TILE[t]], ident[0:48, 0:48])
                        filled(ins)
                if s >= 4:
                    lo = P if s == 4 else 0
                    for t in range(NT):
                        b = fill("z", s - 4, t)
                        filled(project("z", b[:, 0:T - lo], lambda k: hT[:, k, TILE[t]], lambda k: w[:, k, lo:T]))
                pe.drain().then_inc(S["slot_used"], 1)
            late_ada("dt")
            pe.wait_ge(S["dt_ready"], 1)
            b = fill("cum")
            for d in range(2):
                ins = mm(b[:, 48 * d:48 * d + 48], tri[d], e96[3][:, 48 * d:48 * d + 48], start=True, stop=True)
            filled(ins)
            b = fill("tot")
            filled(mm(b[:, 0:96], ones, e96[3], start=True, stop=True))
            pe.wait_ge(S["lsq_ready"], 1)
            b = fill("sl", 0)
            for k in range(2):
                ins = mm(b[:, 0:T], ones, lsq[:, T * k:T * k + T], start=(k == 0), stop=(k == 1))
            filled(ins)
            b = fill("sl", 1)
            filled(mm(b[:, 0:T], ones, lsq[:, 2 * T:3 * T], start=True, stop=True))
            late_ada("cum")
            pe.wait_ge(S["xc_ready"], CONV_C)
            nfull = 0
            for i, (t, full) in enumerate(STEPS):
                c0 = XC0[t]
                for k in range(2):
                    b = fill("xt", i, k)
                    for c in range(4):
                        ins = pe.transpose(b[:, P * c:P * c + P], xc3[:, 4 * k + c, c0:c0 + P], ident)
                    filled(ins)
                b = fill("bt", i)
                filled(pe.transpose(b[:, 0:P], xc3[:, 8, c0:c0 + P], ident))
                if i == 0:
                    late_ada("state")
                if full:
                    for g in range(2):
                        b = fill("g", i, g)
                        filled(mm(b[:, 0:P], xc3[64 * g:64 * g + 64, 8, c0:c0 + P], xc3[64 * g:64 * g + 64, 9, c0:c0 + P], start=True, stop=True))
                    base = 8 * nfull

                    def cums(u):
                        q, d = u // 2, u % 2
                        b = fill("bc", i, u)
                        for h in range(4):
                            col = 48 * d + HS * t + 4 * q + h
                            ins = mm(b[:, P * h:P * h + P], e96[3][:, col:col + 1].broadcast_to([P, P]), tri[d], start=True, stop=True)
                        filled(ins)

                    def diag(u):
                        q, d = u // 2, u % 2
                        pe.wait_ge(S["s_ready"], base + u + 1)
                        for h in range(4):
                            hh = 4 * (q % 2) + h
                            ins = mm(ps[:, 5 + q // 2, 64 * hh:64 * hh + 64], dec[u % 3][:, P * h:P * h + P],
                                     xdt[d][:, 64 * (4 * q + h):64 * (4 * q + h) + 64],
                                     start=(u % 4 == 0 and h == 0), stop=(d == 1), skip_group_check=True)
                        ins.then_inc(S["diag_done"], 1)

                    cums(0)
                    cums(1)
                    late_ada("unit", i, -1)
                    for u in range(8):
                        if u + 2 < 8:
                            cums(u + 2)
                        diag(u)
                        late_ada("unit", i, u)
                    if t:
                        for d in range(2):
                            s_in = {(0, 1): h0[0], (0, 2): h0[0], (1, 2): h0[1], (1, 1): s_b1}[d, t]
                            if d == 0:
                                pe.wait_ge(S["st_done"], 1 if t == 1 else 2)
                            for g in range(2):
                                b = fill("off", i, d, g)
                                filled(mm(b[:, 0:512], xc3[64 * g:64 * g + 64, 9, c0:c0 + P], s_in[64 * g:64 * g + 64, :], start=True, stop=True))
                    late_ada("tail", i)
                    pe.wait_ge(S["ynormed"], nfull + 1)
                    for k in range(2):
                        b = fill("yT", i, k)
                        for c in range(4):
                            ins = pe.transpose(b[:, P * c:P * c + P], ytok[:, 512 * k + P * c:512 * k + P * c + P], ident)
                        filled(ins)
                    late_ada("end", i)
                    nfull += 1
                for d in STATES[i]:
                    pe.wait_ge(S["xw_ready"], sum(len(x) for x in STATES[:i]) + STATES[i].index(d) + 1)
                    b = fill("st", i, d)
                    for g in range(2):
                        ins = mm(b[64 * g:64 * g + 64, 0:512], Btok[:, 64 * g:64 * g + 64], xw[:, 512 * g:512 * g + 512], start=True, stop=True)
                    filled(ins)
            pe.wait_ge(S["latn_ready"], 1)
            wq = sm("w_q_b").rearrange("p (k n) -> p k n", k=2)
            wkv = sm("w_kv_b")
            for k in range(N_PREP + 1):
                if k < N_PREP:
                    s = k - NT
                    src = latT[:, 2, TILE[s]] if s < NT else sm("ckv_cache")
                    for hh in range(2):
                        b = fill("qkv", k, hh)
                        if s < 0:
                            ins = project("q", b[:, 0:384], lambda c: latT[:, c, TILE[k]], lambda c: wq[:, c, 384 * hh:384 * hh + 384], 2)
                        else:
                            ins = mm(b[:, 0:512], src, wkv[:, 512 * hh:512 * hh + 512], start=True, stop=True)
                        filled(ins)
                late_ada("mla", k)
                if k:
                    pe.wait_ge(S["qk_ready"], k)
                    for hh in range(2):
                        b = fill("qkT", k - 1, hh)
                        for h in range(4):
                            ins = pe.transpose(b[0:QM, P * h:P * h + P], mkt[(k - 1) % 2][:, QM * (4 * hh + h):QM * (4 * hh + h) + QM], ident)
                        filled(ins)
            pe.wait_ge(S["qkT_ready"], 2 * N_PREP)
            attention("mla", HM, lambda t, h: mqT3[0:QM, h, TILE[t]], lambda h, k0, nk: mkT3[0:QM, h, k0:k0 + nk],
                      lambda s, h: mv3[:, s, 64 * h:64 * h + 64], m_att)
            project_out(0, 12, (2, 2, 2, 2), S_OUTE, lambda k: oTy3[:, k, :] if k < 8 else oTm3[:, k - 8, :])
            moe(0)
            sum_squares(1, 0)
            def turn(name, src):
                b = fill(*name)
                for c in range(4):
                    ins = pe.transpose(b[:, P * c:P * c + P], src[:, P * c:P * c + P], ident)
                filled(ins)

            for i in range(NT + 1):
                for s in range(N_INO):
                    if i < NT:
                        t = ORDER[i]
                        w = slot(S_INO + s).rearrange("p (k n) -> p k n", k=DC)
                        b = fill("in", s, t)
                        for k in range(DC):
                            if s == 0 and i == 0:
                                h_chunk(1, 0, k)
                            ins = mm(b[:, 0:384], hT[:, k, TILE[t]], w[:, k, :], start=(k == 0), stop=(k == DC - 1))
                        filled(ins)
                        if i == NT - 1:
                            pe.drain().then_inc(S["slot_used"], 1)
                if i == 0:
                    pe.wait_ge(S["cache_keys"], 1)
                    turn(("gkT", 3), gkt[3])
                else:
                    t = ORDER[i - 1]
                    pe.wait_ge(S["qk_ready"], N_PREP + 2 * i - 1)
                    for k in range(2):
                        turn(("gqT", t, k), qkv3[:, t, 512 * k:512 * k + 512])
                    pe.wait_ge(S["qk_ready"], N_PREP + 2 * i)
                    turn(("gkT", t), gkt[t])
            pe.wait_ge(S["qkT_ready"], 2 * N_PREP + 3 * NT + 1)
            attention("gqa", HQ, lambda t, h: gqT3[64 * (h % 2):64 * (h % 2) + 64, h // 2, TILE[t]],
                      lambda h, k0, nk: gkT3[64 * (h % 2):64 * (h % 2) + 64, h // 4, k0:k0 + nk],
                      lambda s, h: (sm("v_cache")[:, 64 * (h // 4):64 * (h // 4) + 64] if s == 1 else
                                    qkv3[:, {0: 0, 2: 1, 3: 2}[s], 1280 + 64 * (h // 4):1280 + 64 * (h // 4) + 64]), g_att)
            project_out(1, 8, (3, 3, 2), S_OUTO, lambda k: oT3[:, k, :])
            moe(1)

        @block.scalar
        def _(act):
            n_chain, n_taken = [0], [0]
            mine = [j for j, (_, by) in enumerate(jobs) if by == "A"]

            def link(ins):
                n_chain[0] += 1
                ins.then_inc(S["chain_act"], 1)
                act.wait_ge(S["chain_act"], n_chain[0])

            def take(*name):
                j = mine[n_taken[0]]
                assert jobs[j][0] == name, (jobs[j], name)
                act.wait_ge(S["job_done"], j + 1)
                n_taken[0] += 1
                return bank(j)

            def emptied_by(ins):
                ins.then_inc(S["free_act"], 1)

            def after(name):
                act.wait_ge(S["job_done"], index[name] + 1)

            A = act.activation

            def root(out, src, n, scale=1.0):
                return A(out, src, ACT.Sqrt, bias=EPS / (scale * scale), scale=1.0 / (n * scale * scale))

            act.dma_start(small[:, 0:N_SMALL_FIRST], small_d[:, 0:N_SMALL_FIRST]).then_inc(S["in_first"], 16)
            act.wait_ge(S["in_first"], 16)
            A(condS, sm("cond"), ACT.Silu).then_inc(S["cond_ready"], 1)

            def norm(l, i):
                root_mean_square(l, i)
                shift(l, i)

            def root_mean_square(l, i):
                for c in range(DC):
                    if l == 0 and i == 0:
                        act.wait_ge(S["in_x"], 16)
                    else:
                        act.wait_ge(S["x_new"], DC * (2 * l + i - 1) + c + 1)
                    A(hT[:, c, :], xT[:, c, :], ACT.Square).then_inc(S["sq_ready"], 1)
                b = take("ss", l, i)
                root(rn, b[:, 0:T], D).then_inc(S["r_ready"], 1)
                act.wait_ge(S["r_ready"], 2 * l + i + 1)
                act.sem_inc(S["free_act"], 1)

            def shift(l, i):
                sh = mod[l][:, 16 * 3 * i:16 * (3 * i + 1)]
                for c in range(DC):
                    act.wait_ge(S["h_scaled"], DC * (2 * l + i) + c + 1)
                    for s in range(2):
                        ins = A(hT[:, c, SEG[s]], hT[:, c, SEG[s]], ACT.Identity, bias=sh[:, 2 * c + s:2 * c + s + 1])
                    ins.then_inc(S["h_ready"], 1)

            def attention(kind, heads, places):
                Pb, PTb, nm, rs = places
                base = 0 if kind == "mla" else NT * HM
                for n in ("ckv", "kpe") if kind == "mla" else ():
                    act.wait_ge(outs[n], 16)
                for u in range(NT * heads + AHEAD):
                    if u < NT * heads:
                        b = take(kind, "s", u)
                        act.wait_ge(S["max_ready"], base + u + 1)
                        if u >= 4:
                            after((kind, "pT", u - 4))
                        nk = KEYS[u % NT][1]
                        A(Pb[:, 384 * (u % 4):384 * (u % 4) + nk], b[:, 0:nk], ACT.Exp, bias=nm[:, u:u + 1],
                          accum_out=rs[:, u:u + 1]).then_inc(S["e_ready"], 1)
                        act.wait_ge(S["e_ready"], base + u + 1)
                        act.sem_inc(S["free_act"], 1)
                    v = u - AHEAD
                    if v >= 0:
                        h, t = v // NT, v % NT
                        b = take(kind, "pT", v)
                        if t == 0 and h >= 2:
                            act.wait_ge(S["pv_done"], base // NT + h - 1)
                        pt = PTb[:, 896 * (h % 2):896 * (h % 2) + 896]
                        out, src = pt[:, 0:P], b[:, 0:P]
                        if t:
                            out = pt[:, P:].rearrange("p (k q) -> p k q", k=3)[:, :, P * (t - 1):P * t]
                            src = b[:, 0:384].rearrange("p (k q) -> p k q", k=3)
                        act.copy(out, src).then_inc(S["pt_ready"], 1)
                        act.wait_ge(S["pt_ready"], base + v + 1)
                        act.sem_inc(S["free_act"], 1)

            def qk_root(n_step, ss, n, scale):
                act.wait_ge(S["qk_sq"], n_step + 1)
                root(ss, ss, n, scale).then_inc(S["qk_r"], 1)

            def moe(l):
                norm(l, 1)
                b = take("rt", l)
                A(rtT, b[0:NE, 0:T], ACT.Exp, scale=-1.0).then_inc(S["rt_exp"], 1)
                act.wait_ge(S["rt_exp"], l + 1)
                act.sem_inc(S["free_act"], 1)
                for n in ("gk", "gv") if l else ():
                    act.wait_ge(outs[n], 16)
                for j in range(2 * NT):
                    b = take("htok", l, j)
                    emptied_by(act.copy(htok3[:, j // 2, 512 * (j % 2):512 * (j % 2) + 512], b[:, :]))
                act.wait_ge(S["flags_ready"], l + 1)
                with act.Fori(0, NG) as g:
                    def wait(b, step, n):
                        per = PER_GROUP[step]
                        act.wait_ge(BLOCK[b][step], g * per + (per * NG * l + n))

                    def gather(b):
                        wait(b, "xg0_done", 1)
                        act.copy(xg[:, 0:512], ps[:, 4, :]).then_inc(BLOCK[b]["xg_by_act"], 1)
                        wait(b, "selT_done", 1)
                        act.copy(S_sb[:, T * b:T * b + T], ps[:, 7, 0:T])
                        wait(b, "xgT1_done", 1)
                        act.copy(xgT3[:, b, 512:1024], ps[:, 3, :]).then_inc(BLOCK[b]["xgT_by_act"], 1)

                    def silu(e, b):
                        wait(b, "au_done", e + 1)
                        A(sil_of[2 if b else e % 2], ps[:, 3 if b else e % 2, 0:256], ACT.Silu).then_inc(BLOCK[b]["sil_ready"], 1)

                    def turned_act(e, b):
                        wait(b, "tr_done", e + 1)
                        act.copy(actT_of[2 if b else e % 2], ps[:, 3 if b else 2, 0:256]).then_inc(BLOCK[b]["trc_ready"], 1)

                    def both(e, b):
                        silu(e, b)
                        turned_act(e, b)

                    def group(beyond):
                        gather(0)
                        beyond(gather)
                        for e in range(GS):
                            if e:
                                turned_act(e - 1, 0)
                            silu(e, 0)
                            beyond(lambda b: both(e, b))
                        turned_act(GS - 1, 0)

                    by_size(act, g, group)

            def copy_row(n):
                late = n >= N_FIRST
                act.wait_ge(S["row_done"], n + 1)
                act.sem_inc(S["slot_used"], 1)
                act.copy(mod_row[0 if late else n % 2], ps[0:2, 7 if late else 5 + n % 2, 0:384]).then_inc(S["row_copied"], 1)

            def late_rows(*point):
                for n in LATE.get(point if len(point) > 1 else point[0], []):
                    copy_row(n)

            for n in range(N_FIRST):
                if n == N_FIRST - 1:
                    root_mean_square(0, 0)
                copy_row(n)
            shift(0, 0)
            act.wait_ge(S["in_small"], 16)
            convb = sm("conv_b")

            def conv_silu(c):
                act.wait_ge(S["xc_raw"], c + 1)
                A(xc3[:, c, :], xc3[:, c, :], ACT.Silu, bias=convb[:, c:c + 1]).then_inc(S["xc_ready"], 1)

            for c in range(CONV_C):
                b = take("xbc", c)
                if c >= 2:
                    act.wait_ge(S["xc_raw"], c - 1)
                else:
                    act.wait_ge(S["xr_used"], 1)
                act.copy(xr[c % 2][:, 1:129], b[:, 0:P])
                act.copy(xr[c % 2][:, 130:386], b[:, P:T]).then_inc(S["xr_ready"], 1)
                act.wait_ge(S["xr_ready"], c + 1)
                act.sem_inc(S["free_act"], 1)
                if c:
                    conv_silu(c - 1)
            conv_silu(CONV_C - 1)
            for i, (lo, w) in enumerate([(0, 256), (256, 384), (640, 384)]):
                for t in range(NT):
                    b = take("z", i, t)
                    A(zs3[:, t, lo:lo + w], b[:, 0:w], ACT.Silu).then_inc(S["z_ready"], 1)
                    act.wait_ge(S["z_ready"], 3 * i + t + 1)
                    act.sem_inc(S["free_act"], 1)
            act.wait_ge(S["e_in"], 1)
            A(e96[6][:, 0:32], sm("a_log"), ACT.Exp)
            link(A(e96[1], e96[1], ACT.Exp))
            A(e96[1], e96[1], ACT.Ln, bias=1.0).then_inc(S["e_mid"], 1)
            late_rows("dt")
            for k, n in ((0, 2 * P), (1, P)):
                b = take("sl", k)
                root(lr[k], b[:, 0:T], n).then_inc(S["lr_ready"], 1)
                act.wait_ge(S["lr_ready"], k + 1)
                act.sem_inc(S["free_act"], 1)
            act.wait_ge(S["cum_copied"], 1)
            A(e96[5], e96[4], ACT.Exp, scale=-1.0)
            A(e96[9], e96[9], ACT.Exp)
            A(e96[8], e96[6], ACT.Exp).then_inc(S["e_cum"], 1)
            late_rows("cum")
            nfull = 0
            ssdn = sm("ssd_norm")
            for i, (t, full) in enumerate(STEPS):
                if i:
                    act.wait_ge(S["xtok_used"], i)
                for k in range(2):
                    b = take("xt", i, k)
                    emptied_by(act.copy(xtok[:, 512 * k:512 * k + 512], b[:, :]))
                b = take("bt", i)
                emptied_by(act.copy(Btok, b[:, 0:P]))
                act.wait_ge(S["free_act"], emptied[index[("bt", i)]][1])
                act.sem_inc(S["xtok_ready"], 1)
                if i == 0:
                    late_rows("state")
                if full:
                    for g in range(2):
                        b = take("g", i, g)
                        emptied_by(act.copy(Gs2[g], b[:, 0:P]))
                    act.wait_ge(S["free_act"], emptied[index[("g", i, 1)]][1])
                    act.sem_inc(S["g_ready"], 1)
                    for u in range(8):
                        act.wait_ge(S["seg_ready"], 8 * nfull + u + 1)
                        A(dec[u % 3], dec[u % 3], ACT.Exp).then_inc(S["dec_ready"], 1)
                        if u:
                            late_rows("unit", i, u - 2)
                    late_rows("unit", i, 6)
                    late_rows("unit", i, 7)
                    for n in LATE[("tail", i)][:1]:
                        copy_row(n)
                    act.wait_ge(S["ysq_ready"], nfull + 1)
                    link(A(zs3[:, t, :], ytok, ACT.Square, accum_out=ssd_r))
                    root(ssd_r, ssd_r, D).then_inc(S["ynorm_ready"], 1)
                    for n in LATE[("tail", i)][1:]:
                        copy_row(n)
                    for k in range(2):
                        b = take("yT", i, k)
                        for c in range(4):
                            ins = A(oTy3[:, 4 * k + c, TILE[t]], b[:, P * c:P * c + P], ACT.Copy, scale=ssdn[:, 4 * k + c:4 * k + c + 1])
                        emptied_by(ins)
                    late_rows("end", i)
                    nfull += 1
            by_head = lambda ap, n: ap.rearrange("p (h n) -> p h n", h=n)
            for k in range(N_PREP + 1):
                if k < N_PREP:
                    s, x, sq = k - NT, mkt[k % 2], msq[k % 2]
                    for hh in range(2):
                        b = take("qkv", k, hh)
                        if s < 0:
                            half = slice(384 * hh, 384 * hh + 384)
                            A(sq[:, half], b[:, 0:384], ACT.Square)
                            emptied_by(act.copy(x[:, half], b[:, 0:384]))
                        else:
                            b3, half = by_head(b[:, :], 4), slice(4 * hh, 4 * hh + 4)
                            A(by_head(sq, HM)[:, half, 0:NOPE], b3[:, :, 0:NOPE], ACT.Square)
                            act.copy(by_head(x, HM)[:, half, 0:NOPE], b3[:, :, 0:NOPE])
                            emptied_by(act.copy(by_head(mv3[:, KSLOT[s], 256 * hh:256 * hh + 256], 4), b3[:, :, NOPE:P]))
                    act.wait_ge(S["free_act"], emptied[index[("qkv", k, 1)]][1])
                    act.sem_inc(S["qt_copied"], 1)
                v = k - 1
                if k:
                    qk_root(v, mss[v % 2], QM, QM ** -0.5 if v < NT else 1.0)
                late_rows("mla", k)
                if k:
                    for hh in range(2):
                        b = take("qkT", v, hh)
                        half = slice(4 * hh, 4 * hh + 4)
                        out = mqT3[0:QM, half, TILE[v]] if v < NT else mkT3[0:QM, half, P * KSLOT[v - NT]:P * KSLOT[v - NT] + P]
                        act.copy(out, b[0:QM, :].rearrange("p (h n) -> p h n", h=4)).then_inc(S["qkT_ready"], 1)
                        act.wait_ge(S["qkT_ready"], 2 * v + hh + 1)
                        act.sem_inc(S["free_act"], 1)
            attention("mla", HM, m_att)
            moe(0)
            norm(1, 0)
            act.wait_ge(S["xr_used"], 2)
            n_t = [2 * N_PREP]

            def turn_gqa(out, *name):
                b = take(*name)
                n_t[0] += 1
                act.copy(out, b[:, :].rearrange("p (h n) -> p h n", h=4)).then_inc(S["qkT_ready"], 1)
                act.wait_ge(S["qkT_ready"], n_t[0])
                act.sem_inc(S["free_act"], 1)

            for i in range(NT + 1):
                if i < NT:
                    t = ORDER[i]
                    for s in (1, 3):
                        b = take("in", s, t)
                        act.copy(qkv3[:, t, 384 * s:384 * s + 384], b[:, 0:384]).then_inc(S["qkv_ready"], 1)
                        act.wait_ge(S["qkv_ready"], 2 * i + s // 2 + 1)
                        act.sem_inc(S["free_act"], 1)
                    act.wait_ge(S["free_dve"], emptied[index[("in", 2, t)]][1])
                    A(gsq[t], qkv3[:, t, 0:HQ * HD], ACT.Square).then_inc(S["gsq_ready"], 1)
                    qk_root(N_PREP + 2 * i, gss[t], HD, HD ** -0.5)
                    qk_root(N_PREP + 2 * i + 1, gss[NT + t], HD, 1.0)
                if i == 0:
                    turn_gqa(gkT3[:, :, P * KSLOT[3]:P * KSLOT[3] + P], "gkT", 3)
                else:
                    t = ORDER[i - 1]
                    for k in range(2):
                        turn_gqa(gqT3[:, 4 * k:4 * k + 4, TILE[t]], "gqT", t, k)
                    turn_gqa(gkT3[:, :, P * KSLOT[t]:P * KSLOT[t] + P], "gkT", t)
            attention("gqa", HQ, g_att)
            moe(1)

        @block.vector
        def _(dve):
            n_chain, n_taken = [0], [0]
            mine = [j for j, (_, by) in enumerate(jobs) if by == "D"]

            def link(ins):
                n_chain[0] += 1
                ins.then_inc(S["chain_dve"], 1)
                dve.wait_ge(S["chain_dve"], n_chain[0])

            def take(*name):
                j = mine[n_taken[0]]
                assert jobs[j][0] == name, (jobs[j], name)
                dve.wait_ge(S["job_done"], j + 1)
                n_taken[0] += 1
                return bank(j)

            def emptied_by(ins):
                ins.then_inc(S["free_dve"], 1)

            def after(*name):
                dve.wait_ge(S["job_done"], index[name] + 1)

            tt, ts, stt = dve.tensor_tensor, dve.tensor_scalar, dve.scalar_tensor_tensor

            def spread(ap, n):
                return ap.unsqueeze(2).broadcast_to([ap.shape[0], ap.shape[1], n])

            def over(ap, n):
                return ap.unsqueeze(1).broadcast_to([ap.shape[0], n, ap.shape[1]])

            def cut(ap, n):
                return ap.rearrange("p (h n) -> p h n", h=n)

            def modulation(part):
                lo, hi = ([0] + PARTS)[part], PARTS[part]
                l, lo, hi = lo // N_ADA, 3 * (lo % N_ADA), 3 * ((hi - 1) % N_ADA + 1)
                dve.wait_ge(S["ada_done"], part + 1)
                tt(mod[l][:, 2 * lo:2 * hi].rearrange("p (c n) -> p c n", n=2), ps[:, 7, 384 + 2 * lo:384 + 2 * hi].rearrange("p (c n) -> p c n", n=2),
                   spread(sm("b_ada")[:, 48 * l + lo:48 * l + hi], 2), ADD).then_inc(S["mod_ready"], 1)
                dve.wait_ge(S["mod_ready"], part + 1)

            def normaliser(l, i):
                dve.wait_ge(S["r_ready"], 2 * l + i + 1)
                link(dve.reciprocal(rn, rn))

            def norm(l, i):
                g = sm("g_ffn" if i else "g_mix")[:, DC * l:DC * l + DC]
                sc = mod[l][:, 16 * (3 * i + 1):16 * (3 * i + 2)]
                ab = AB[:, 16 * i:16 * i + 16]
                link(stt(cut(ab, 8), cut(sc, 8), 1.0, spread(g, 2), ADD, MUL))
                if l or i:
                    normaliser(l, i)
                for c in range(DC):
                    for s in range(2):
                        ins = stt(hT[:, c, SEG[s]], xT[:, c, SEG[s]], ab[:, 2 * c + s:2 * c + s + 1], rn[:, SEG[s]], MUL, MUL)
                    ins.then_inc(S["h_scaled"], 1)

            def residual(l, part, name):
                gt = mod[l][:, 16 * part:16 * part + 16]
                for c in range(DC):
                    b = take(name, l, c)
                    for s in range(2):
                        ins = stt(xT[:, c, SEG[s]], b[:, SEG[s]], gt[:, 2 * c + s:2 * c + s + 1], xT[:, c, SEG[s]], MUL, ADD)
                    ins.then_inc(S["x_new"], 1)
                    dve.wait_ge(S["x_new"], DC * (2 * l + (part == 5)) + c + 1)
                    dve.sem_inc(S["free_dve"], 1)

            def rope(x, cos, sin, tmp, nh, n):
                q = n // 4
                x5 = x.rearrange("p h (a f n) -> p h a f n", a=2, f=2)
                t5 = tmp.rearrange("p h (a f n) -> p h a f n", a=2, f=2)
                s4 = sin.rearrange("p (a f n) -> p a f n", a=2, f=2)
                for a in range(2):
                    for f in range(2):
                        ins = tt(t5[:, :, a, f, :], x5[:, :, a, 1 - f, :], over(s4[:, a, f, :], nh), MUL)
                link(ins)
                link(tt(x, x, over(cos, nh), MUL))
                link(tt(x, x, tmp, ADD))

            def sum_heads(ss, sq):
                dve.tensor_reduce(ss, sq, AX.X, ADD).then_inc(S["qk_sq"], 1)

            def qk_norm(n_step, x, nh, n, gain, ss, tmp, cos, sin, rope_at):
                dve.wait_ge(S["qk_r"], n_step + 1)
                link(dve.reciprocal(ss, ss))
                link(tt(x, x, spread(ss, n), MUL))
                link(tt(x, x, over(gain, nh), MUL))
                if cos is not None:
                    rope(x[:, :, rope_at:n], cos, sin, tmp[:, :, rope_at:n], nh, n - rope_at)

            def attention(kind, heads, places, out):
                Pb, PTb, nm, rs = places
                base = 0 if kind == "mla" else NT * HM
                pairs = 0 if kind == "mla" else HM // 2
                for n in ("ckv", "kpe") if kind == "mla" else ():
                    dve.wait_ge(outs[n], 16)
                n_u = NT * heads
                for u in range(n_u + 1):
                    if u < n_u:
                        after(kind, "s", u)
                        dve.tensor_reduce(nm[:, u:u + 1], bank(index[(kind, "s", u)])[:, 0:KEYS[u % NT][1]], AX.X, MAX, negate=True).then_inc(S["max_ready"], 1)
                    v = u - 1
                    if v >= 0:
                        nk = KEYS[v % NT][1]
                        dve.wait_ge(S["e_ready"], base + v + 1)
                        link(dve.reciprocal(rs[:, v:v + 1], rs[:, v:v + 1]))
                        p = Pb[:, 384 * (v % 4):384 * (v % 4) + nk]
                        ts(p, p, rs[:, v:v + 1], None, MUL).then_inc(S["p_ready"], 1)
                    w = v - 10
                    if w >= 0 and w % 6 == 0:
                        pair_out(w // 6, pairs, base, out)
                for k in range((n_u - 1 - 10) // 6 + 1, heads // 2):
                    pair_out(k, pairs, base, out)

            def pair_out(k, pairs, base, out):
                dve.wait_ge(S["pv_done"], base // NT + 2 * k + 2)
                dve.tensor_copy(out[:, k, :], ps[:, 5 + (pairs + k) % 2, 0:T]).then_inc(S["o_ready"], 1)

            def gates_of(l):
                fw = sm("first_wins")
                s, sel, msel, key, oh1, ms2, oh2 = rt48[1], rt48[2], rt48[3], rt48[4], rt48[5], rt48[6], rt48[7]
                cut3 = lambda ap: ap.rearrange("p (t n) -> p t n", t=NT)
                b = take("rtT", l)
                ts(s, b[:, 0:48], 1.0, None, ADD).then_inc(S["free_dve"], 1)
                dve.wait_ge(S["free_dve"], emptied[index[("rtT", l)]][1])
                link(dve.reciprocal(s, s))
                link(tt(cut3(sel), cut3(s), over(sm("router_bias"), NT), ADD))
                v = sel.rearrange("p (q n) -> p q n", n=GS)
                pair = rt[:, 920:992].rearrange("p (q n) -> p q n", n=6)
                tt(pair[:, :, 0:3], v[:, :, 0:3], v[:, :, 1:4], ADD)
                tt(pair[:, :, 3:5], v[:, :, 0:2], v[:, :, 2:4], ADD)
                link(tt(pair[:, :, 5:6], v[:, :, 0:1], v[:, :, 3:4], ADD))
                link(dve.tensor_reduce(rt12[8], pair, AX.X, MAX))

                def pick(out, src, n, weights, m):
                    link(dve.tensor_reduce(m[0], cut3(src), AX.X, MAX))
                    link(tt(cut3(out), cut3(src), spread(m[0], n), EQ))
                    link(tt(cut3(out), cut3(out), over(weights, NT), MUL))
                    link(dve.tensor_reduce(m[1], cut3(out), AX.X, MAX))
                    link(tt(cut3(out), cut3(out), spread(m[1], n), EQ))

                pick(rt12[9], rt12[8], NG, fw[:, 0:NG], rt3[0:2])
                dve.sem_inc(S["group_found"], 1)
                tt(msel.rearrange("p (q n) -> p q n", n=GS), v, spread(rt12[9], GS), MUL)
                link(ts(rt12[10], rt12[9], -1.0, BIG, ADD, MUL))
                link(tt(msel.rearrange("p (q n) -> p q n", n=GS), msel.rearrange("p (q n) -> p q n", n=GS), spread(rt12[10], GS), ADD))
                pick(oh1, msel, NE, fw[:, NG:], rt3[2:4])
                by_tg = lambda ap: ap.rearrange("p (t g) -> p t g", t=NT)
                b = take("pos", l)
                tt(pos_g[:, 0:12].rearrange("p (g t) -> p t g", g=NG), by_tg(b[:, 0:12]), by_tg(rt12[9]), MUL)
                for n in range(2):
                    ins = ts(flags_f.rearrange("p (g n) -> p g n", n=2)[:, :, n], b[:, 12:16], float(P * (n + 1)), None, ALU.is_gt)
                link(ins)
                dve.tensor_copy(pcol, pos_g[:, 0:NT])
                link(dve.tensor_copy(flags, flags_f))
                dve.sem_inc(S["free_dve"], 1)
                dve.sem_inc(S["flags_ready"], 1)
                select(0).then_inc(BLOCK[0]["sel_ready"], 1)
                link(stt(ms2, oh1, -3 * BIG, msel, MUL, ADD))
                pick(oh2, ms2, NE, fw[:, NG:], rt3[4:6])
                link(tt(oh1, oh1, oh2, ADD))
                link(tt(oh1, oh1, s, MUL))
                link(dve.tensor_reduce(rt3[6], cut3(oh1), AX.X, ADD))
                link(dve.reciprocal(rt3[7], rt3[6]))
                link(tt(cut3(gates), cut3(oh1), spread(rt3[7], NE), MUL))
                dve.memset(rt[:, 888:900], 0.0)
                dve.memset(rt[:, 912:915], 0.0)
                for t in range(NT):
                    ins = dve.tensor_copy(gates_g[:, 0:48].rearrange("p (g t e) -> p g t e", g=NG, t=NT)[:, :, t, :],
                                          gates[:, NE * t:NE * t + NE].rearrange("p (g e) -> p g e", g=NG))
                link(ins)
                dve.tensor_copy(gcur, gates_g[:, 0:NT * GS]).then_inc(S["gcur_ready"], 1)

            def select(b):
                for t in range(NT):
                    ins = ts(sel[:, P * t:P * t + P], sm("slots"), float(P * b), pcol[:, t:t + 1], ADD, EQ)
                return ins

            def moe(l):
                norm(l, 1)
                for n in ("gk", "gv") if l else ("ckv", "kpe"):
                    dve.wait_ge(outs[n], 16)
                gates_of(l)
                gt = mod[l][:, 16 * 5:16 * 6]
                with dve.Fori(0, NG) as g:
                    def wait(b, step, n):
                        per = PER_GROUP[step]
                        dve.wait_ge(BLOCK[b][step], g * per + (per * NG * l + n))

                    def gather(b):
                        if b:
                            select(b).then_inc(BLOCK[b]["sel_ready"], 1)
                        wait(b, "xg1_done", 1)
                        dve.tensor_copy(xg[:, 512:1024], ps[:, 5, :]).then_inc(BLOCK[b]["xg_by_dve"], 1)
                        wait(b, "selT_done", 1)
                        dve.tensor_copy(gslot[:, GS * b:GS * b + GS], ps[:, 6, 0:GS])
                        wait(b, "xgT0_done", 1)
                        dve.tensor_copy(xgT3[:, b, 0:512], ps[:, 2, :]).then_inc(BLOCK[b]["xgT_by_dve"], 1)

                    def product(e, b):
                        wait(b, "sil_ready", e + 1)
                        at_, bank_ = (2, 3) if b else (e % 2, e % 2)
                        stt(act_of[at_], ps[:, bank_, 256:512], gslot[:, GS * b + e:GS * b + e + 1],
                            sil_of[at_], MUL, MUL).then_inc(BLOCK[b]["act_ready"], 1)

                    def add(e, b):
                        for h in range(2):
                            wait(b, "dn_done", 2 * e + h + 1)
                            if h and b == 0:
                                dve.sem_inc(S["slot_used"], 2)
                            y, part = yacc3[:, b, 512 * h:512 * h + 512], ps[:, (6 if b else 4) + h, :]
                            ins = tt(y, y, part, ADD) if e else dve.tensor_copy(y, part)
                            ins.then_inc(BLOCK[b]["acc_ready"], 1)

                    def both(e, b):
                        product(e, b)
                        add(e, b)

                    def scatter(b):
                        for c in range(DC):
                            wait(b, "sc_done", c + 1)
                            for q in range(2):
                                ins = stt(xT[:, c, SEG[q]], ps[:, SC_BANK[c % 4], SEG[q]], gt[:, 2 * c + q:2 * c + q + 1], xT[:, c, SEG[q]], MUL, ADD)
                            ins.then_inc(BLOCK[b]["sc_used"], 1)

                    def group(beyond):
                        gather(0)
                        beyond(gather)
                        for e in range(GS):
                            product(e, 0)
                            if e:
                                add(e - 1, 0)
                            beyond(lambda b: both(e, b))
                        dve.tensor_copy(pcol, pos_g[:, bass.ds(g * NT + NT, NT)]).then_inc(S["next_group"], 1)
                        dve.tensor_copy(gcur, gates_g[:, bass.ds(g * (NT * GS) + NT * GS, NT * GS)]).then_inc(S["gcur_ready"], 1)
                        dve.wait_ge(S["next_group"], g + (NG * l + 1))
                        select(0).then_inc(BLOCK[0]["sel_ready"], 1)
                        add(GS - 1, 0)
                        scatter(0)
                        beyond(scatter)

                    by_size(dve, g, group)
                for b in range(NT):
                    dve.wait_ge(BLOCK[b]["sc_used"], DC * NG * (l + 1))
                dve.sem_inc(S["x_new"], DC)

            dve.wait_ge(S["in_first"], 16)
            dve.wait_ge(S["in_x"], 16)
            normaliser(0, 0)
            modulation(0)
            norm(0, 0)
            dve.wait_ge(S["in_small"], 16)
            dve.wait_ge(S["h_scaled"], DC)
            for i in range(2):
                for c in (0, 129, 386):
                    link(dve.memset(xr[i][:, c:c + 1], 0.0))
            dve.sem_inc(S["xr_used"], 1)
            b = take("dk")
            dve.tensor_copy(dk_f, b[0:48, 0:T]).then_inc(S["dk_by_feature"], 1)
            dve.wait_ge(S["dk_by_feature"], 1)
            dve.sem_inc(S["free_dve"], 1)
            b = take("dkT")
            emptied_by(dve.tensor_copy(dk, b[:, 0:144]))
            dve.wait_ge(S["free_dve"], emptied[index[("dkT",)]][1])
            dve.sem_inc(S["dk_copied"], 1)
            cw = sm("conv_w")
            for c in range(CONV_C):
                dve.wait_ge(S["xr_ready"], c + 1)
                r, o = xr[c % 2], xc3[:, c, :]
                link(ts(o, r[:, 1:386], cw[:, CONV_C + c:CONV_C + c + 1], None, MUL))
                link(stt(o, r[:, 0:385], cw[:, c:c + 1], o, MUL, ADD))
                stt(o, r[:, 2:387], cw[:, 2 * CONV_C + c:2 * CONV_C + c + 1], o, MUL, ADD).then_inc(S["xc_raw"], 1)
            for c in range(3):
                b = take("lat", c)
                emptied_by(dve.tensor_copy(latT[:, c, :], b[:, 0:T]))
            def by_tile(ap, d):
                return ap[:, 48 * d:48 * d + 48].rearrange("p (t n) -> p t n", t=NT)

            for d in range(2):
                link(tt(by_tile(e96[0], d), dk3[:, :, 0:HS], over(sm("dt_bias")[:, HS * d:HS * d + HS], NT), ADD))
            link(ts(e96[1], e96[0], -1.0, None, MUL))
            tt(e96[1], e96[0], e96[1], MIN).then_inc(S["e_in"], 1)
            dve.wait_ge(S["e_mid"], 1)
            link(stt(e96[2], e96[0], 0.0, e96[1], MAX, ADD))
            for d in range(2):
                link(stt(by_tile(e96[3], d), by_tile(e96[2], d), -1.0, over(e96[6][:, HS * d:HS * d + HS], NT), MUL, MUL))
            dve.sem_inc(S["dt_ready"], 1)
            after("z", 2, NT - 1)
            tt(lsq, lat, lat, MUL).then_inc(S["lsq_ready"], 1)
            b = take("cum")
            emptied_by(ts(e96[4], b[:, 0:96], -1.0, None, MUL))
            dve.wait_ge(S["free_dve"], emptied[index[("cum",)]][1])
            b = take("tot")
            link(tt(e96[9], b[:, 0:96], e96[4], ADD))
            emptied_by(dve.tensor_copy(e96[6], b[:, 0:96]))
            dve.wait_ge(S["free_dve"], emptied[index[("tot",)]][1])
            dve.sem_inc(S["cum_copied"], 1)
            dve.wait_ge(S["e_cum"], 1)
            link(tt(e96[7], e96[2], e96[9], MUL))
            dve.wait_ge(S["lr_ready"], 2)
            link(dve.reciprocal(lr_both, lr_both))
            for c in range(3):
                g = sm("q_a_norm")[:, c:c + 1] if c < 2 else sm("kv_a_norm")
                ins = stt(latT[:, c, :], latT[:, c, :], g, lr[c // 2], MUL, MUL)
            ins.then_inc(S["latn_ready"], 1)
            nfull = 0
            for i, (t, full) in enumerate(STEPS):
                dve.wait_ge(S["xtok_ready"], i + 1)
                if i == 2:
                    modulation(1)
                col = lambda d: slice(48 * d + HS * t, 48 * d + HS * t + HS)
                if full:
                    base = 8 * nfull
                    for d in range(2):
                        link(tt(cut(xdt[d], HS), cut(xtok, HS), spread(e96[2][:, col(d)], PS), MUL))

                    def segment(u):
                        q, d = u // 2, u % 2
                        b = take("bc", i, u)
                        if u >= 3:
                            dve.wait_ge(S["diag_done"], base + u - 2)
                        for h in range(4):
                            c = 48 * d + HS * t + 4 * q + h
                            ins = stt(dec[u % 3][:, P * h:P * h + P], b[:, P * h:P * h + P], e96[4][:, c:c + 1], mask[d], ADD, ADD)
                        ins.then_inc(S["seg_ready"], 1)
                        dve.wait_ge(S["seg_ready"], base + u + 1)
                        dve.sem_inc(S["free_dve"], 1)

                    def scores(u):
                        q, d = u // 2, u % 2
                        dve.wait_ge(S["dec_ready"], base + u + 1)
                        if u == 0:
                            dve.wait_ge(S["g_ready"], nfull + 1)
                        tt(cut(dec[u % 3], 4), cut(dec[u % 3], 4), over(Gs2[q // 2], 4), MUL).then_inc(S["s_ready"], 1)

                    segment(0)
                    segment(1)
                    for u in range(8):
                        scores(u)
                        if u + 2 < 8:
                            segment(u + 2)
                    dve.wait_ge(S["diag_done"], base + 8)
                    link(tt(cut(ytok, HS), cut(xtok, HS), spread(sm("d_skip"), PS), MUL))
                    link(tt(ytok, ytok, ps[:, 5:7, :].rearrange("p a n -> p (a n)"), ADD))
                    if t:
                        for d in range(2):
                            for g in range(2):
                                b = take("off", i, d, g)
                                link(tt(cut(ytmp, 8), cut(b[:, 0:512], 8), spread(e96[5][:, 48 * d + HS * t + 8 * g:48 * d + HS * t + 8 * g + 8], PS), MUL))
                                dve.sem_inc(S["free_dve"], 1)
                                link(tt(ytok[:, 512 * g:512 * g + 512], ytok[:, 512 * g:512 * g + 512], ytmp, ADD))
                    dve.wait_ge(S["z_ready"], 3 * NT)
                    tt(ytok, ytok, zs3[:, t, :], MUL).then_inc(S["ysq_ready"], 1)
                    dve.wait_ge(S["ynorm_ready"], nfull + 1)
                    link(dve.reciprocal(ssd_r, ssd_r))
                    ts(ytok, ytok, ssd_r[:, 0:1], None, MUL).then_inc(S["ynormed"], 1)
                    after("yT", i, 1)
                    nfull += 1
                for d in STATES[i]:
                    link(tt(cut(xw, HS), cut(xtok, HS), spread(e96[7][:, col(d)], PS), MUL))
                    dve.sem_inc(S["xw_ready"], 1)
                    b = take("st", i, d)
                    for g in range(2):
                        r = slice(64 * g, 64 * g + 64)
                        dst = {(2, 1): s_b1, (1, 0): h0[0], (0, 0): h0[0], (0, 1): h0[1]}[t, d]
                        if t == 0:
                            ins = dve.tensor_copy(dst[r, :], b[r, :])
                        else:
                            cd = e96[8][r, 48 * d + HS * t + 8 * g:48 * d + HS * t + 8 * g + 8]
                            link(tt(cut(dst[r, :], 8), cut(h0[d][r, :], 8), spread(cd, PS), MUL))
                            ins = tt(dst[r, :], dst[r, :], b[r, :], ADD)
                        link(ins)
                    dve.sem_inc(S["free_dve"], 1)
                    dve.sem_inc(S["st_done"], 1)
                dve.sem_inc(S["xtok_used"], 1)
            rot = lambda n, t, w: sm(n)[:, w * (t - 1):w * t]
            for k in range(N_PREP + 1):
                if k < N_PREP:
                    s, x, sq = k - NT, cut(mkt[k % 2], HM), cut(msq[k % 2], HM)
                    if s >= 0:
                        if k >= 2:
                            after("qkT", k - 2, 1)
                        kpe = dk3[:, s, HS:48] if s < NT else sm("kpe_cache")
                        dve.tensor_copy(x[:, :, NOPE:QM], over(kpe, HM))
                        link(tt(sq[:, :, NOPE:QM], over(kpe, HM), over(kpe, HM), MUL))
                    dve.wait_ge(S["qt_copied"], k + 1)
                    sum_heads(mss[k % 2], sq)
                if k:
                    v = k - 1
                    s = v - NT
                    t = v if s < 0 else s
                    on = t in (1, 2)
                    qk_norm(v, cut(mkt[v % 2], HM), HM, QM, sm("q_norm" if s < 0 else "k_norm"), mss[v % 2], cut(msq[v % 2], HM),
                            rot("cos_e", t, ROPE) if on else None, rot("sin_e", t, ROPE) if on else None, NOPE)
                    dve.sem_inc(S["qk_ready"], 1)
            attention("mla", HM, m_att, oTm3)
            modulation(2)
            residual(0, 2, "out")
            moe(0)
            norm(1, 0)
            for n in ("ckv", "kpe", "stf", "stb"):
                dve.wait_ge(outs[n], 16)
            dve.sem_inc(S["xr_used"], 1)
            def double(out, src):
                for i in range(2):
                    ins = dve.tensor_copy(cut(out, HKV)[:, :, 64 * i:64 * i + 64], cut(src, HKV))
                return ins

            double(gkt[3], sm("k_cache")).then_inc(S["cache_keys"], 1)
            for i, t in enumerate(ORDER):
                for s in (0, 2):
                    b = take("in", s, t)
                    emptied_by(dve.tensor_copy(qkv3[:, t, 384 * s:384 * s + 384], b[:, 0:384]))
                q, k = qkv3[:, t, 0:1024], qkv3[:, t, 1024:1280]
                dve.wait_ge(S["gsq_ready"], i + 1)
                sum_heads(gss[t], cut(gsq[t], HQ))
                dve.wait_ge(S["free_dve"], emptied[index[("in", 2, t)]][1])
                dve.wait_ge(S["qkv_ready"], 2 * i + 2)
                link(tt(gsq[NT + t], k, k, MUL))
                sum_heads(gss[NT + t], cut(gsq[NT + t], HKV))
                for j, (x, nh, g, v) in enumerate(((q, HQ, "gq_norm", t), (k, HKV, "gk_norm", NT + t))):
                    qk_norm(N_PREP + 2 * i + j, cut(x, nh), nh, HD, sm(g), gss[v], cut(gsq[v], nh),
                            rot("cos_o", t, HD) if t else None, rot("sin_o", t, HD) if t else None, 0)
                    if j:
                        if i == 2:
                            after("gkT", ORDER[0])
                        link(double(gkt[t], x))
                    dve.sem_inc(S["qk_ready"], 1)
            attention("gqa", HQ, g_att, oT3)
            residual(1, 2, "out")
            moe(1)

        @block.gpsimd
        def _(pool):
            def sum_chunks(l):
                for c in range(1, DC - 1):
                    pool.wait_ge(S["sq_ready"], DC * (2 * l + 1) + c + 1)
                    if c > 1:
                        pool.wait_ge(S["sq_sum"], (DC - 2) * l + c - 1)
                    pool.tensor_tensor(sq_acc, hT[:, 0, :] if c == 1 else sq_acc, hT[:, c, :], ADD).then_inc(S["sq_sum"], 1)

            def even_out(l):
                pool.wait_ge(S["flags_ready"], l + 1)
                with pool.Fori(0, NG) as g:
                    pool.wait_ge(BLOCK[0]["xg0_done"], g + (NG * l + 1))
                    for b in (1, 2):
                        more = pool.value_load(flags[0:1, bass.ds(g * 2 + b - 1, 1)], min_val=0, max_val=1)
                        with pool.If(more):
                            pass
                        with pool.Else():
                            for n in steps:
                                pool.sem_inc(BLOCK[b][n], PER_GROUP[n])

            pool.wait_ge(S["dk_copied"], 1)
            pool.dma_start(kpe_d, dk3[:, 0, HS:48]).then_inc(outs["kpe"], 16)
            pool.wait_ge(S["st_done"], 4)
            pool.dma_start(stf_d, h0[0]).then_inc(outs["stf"], 16)
            pool.dma_start(stb_d, h0[1]).then_inc(outs["stb"], 16)
            pool.wait_ge(S["latn_ready"], 1)
            pool.dma_start(ckv_d, latT[:, 2, 0:P]).then_inc(outs["ckv"], 16)
            sum_chunks(0)
            even_out(0)
            pool.wait_ge(S["qk_ready"], N_PREP + 2 * NT)
            pool.dma_start(gk_d, qkv3[:, 0, 1024:1280]).then_inc(outs["gk"], 16)
            pool.dma_start(gv_d, qkv3[:, 0, 1280:1536]).then_inc(outs["gv"], 16)
            sum_chunks(1)
            even_out(1)


def _constants():
    f = np.float32
    j, i = np.arange(P)[:, None], np.arange(P)[None, :]
    c = {"ident": (i == j).astype(f), "ones": np.ones((P, P), f),
         "tri_f": (j <= i).astype(f), "tri_b": (j >= i).astype(f),
         "mask_f": np.where(j <= i, f(0), f(-BIG)), "mask_b": np.where(j >= i, f(0), f(-BIG)),
         "slots": np.tile(np.arange(1, P + 1).astype(f), (P, 1)),
         "first_wins": np.tile(np.concatenate([np.arange(NG, 0, -1), np.arange(NE, 0, -1)]).astype(f), (P, 1))}
    tok = np.arange(2 * P)
    for name, n in (("e", ROPE), ("o", HD)):
        half = n // 4
        inv = np.power(f(THETA), -np.arange(half, dtype=f) / f(half)).astype(f)
        cos, sin = [], []
        for pos in (tok // GRID_W, tok % GRID_W):
            ang = pos.astype(f)[:, None] * inv[None, :]
            cos += [np.cos(ang)] * 2
            sin += [-np.sin(ang), np.sin(ang)]
        for kind, parts in (("cos_", cos), ("sin_", sin)):
            a = np.concatenate(parts, axis=1).astype(f)
            c[kind + name] = a.reshape(2, P, n).transpose(1, 0, 2).reshape(P, 2 * n)
    return c


def _chunks(v):
    v = np.asarray(v)
    return np.ascontiguousarray(v.reshape(-1, P).T)


def _rows(v):
    return np.tile(np.asarray(v).reshape(1, -1), (P, 1))


def _kxn(w, cols):
    k, n = w.shape
    a = w.reshape(k // P, P, n // cols, cols).transpose(2, 1, 0, 3)
    return a.reshape(n // cols, P, -1)


def kernel(**inputs):
    import concourse.bacc as bacc
    from concourse.bass_utils import run_bass_kernel_spmd

    a = {k: np.asarray(v) for k, v in inputs.items()}
    w_in = a["w_in_even"][0]
    z, xbc, dt, ql, kv = np.split(w_in, (1024, 2304, 2320, 2576), axis=1)
    c = _constants()
    state = lambda s: s[0, 0].reshape(2, HG, PS, NS).transpose(0, 3, 1, 2).reshape(P, HG * PS)
    c.update(g_mix=_chunks(a["g_mix"]), g_ffn=_chunks(a["g_ffn"]), b_ada=_chunks(a["b_ada"]),
             conv_w=_chunks(a["ssd_conv_w"]), conv_b=_chunks(a["ssd_conv_b"]), ssd_norm=_chunks(a["ssd_norm"]),
             q_a_norm=_chunks(a["mla_q_a_norm"]), kv_a_norm=_chunks(a["mla_kv_a_norm"]),
             cond=np.stack([a["c_ctx"].reshape(DC, P), a["c"].reshape(DC, P)], axis=-1).transpose(1, 0, 2).reshape(P, 2 * DC),
             q_norm=_rows(a["mla_q_norm"]), k_norm=_rows(a["mla_k_norm"]), gq_norm=_rows(a["gqa_q_norm"]), gk_norm=_rows(a["gqa_k_norm"]),
             router_bias=_rows(a["router_bias"]),
             a_log=_rows(np.concatenate([a["ssd_a_log_fwd"][0], a["ssd_a_log_bwd"][0]])),
             dt_bias=_rows(np.concatenate([a["ssd_dt_bias_fwd"][0], a["ssd_dt_bias_bwd"][0]])),
             d_skip=_rows(a["ssd_d"]), ckv_cache=a["cache_mla_ckv"][0, 0].T, kpe_cache=a["cache_mla_kpe"][0, 0],
             k_cache=a["cache_gqa_k"][0, 0].reshape(P, -1), v_cache=a["cache_gqa_v"][0, 0].reshape(P, -1),
             h0=np.concatenate([state(a["state_ssd_fwd"]), state(a["state_ssd_bwd"])], axis=1),
             w_router=_kxn(a["w_router"], NE)[0], w_dk=_kxn(np.concatenate([dt, kv[:, P:]], axis=1), 48)[0],
             w_q_b=_kxn(a["mla_w_q_b"][0], 768)[0], w_kv_b=a["mla_w_kv_b"][0])
    small = np.concatenate([c[n].reshape(P, w) for n, w in SMALL], axis=1)

    slots = np.zeros((N_SLOTS, P, SLOT), w_in.dtype)
    ada = [_kxn(a["w_ada"][l], 384) for l in range(DEPTH)]
    slots[S_ADA0:S_ADA0 + N_FIRST] = ada[0][:N_FIRST]
    slots[S_ADA_LATE:S_OUTE] = np.concatenate([ada[0][N_FIRST:], ada[1]])
    slots[S_INE:S_INE + N_INE] = _kxn(np.concatenate([xbc, ql, kv[:, :P], z], axis=1), 384)
    slots[S_OUTE:S_OUTE + N_OUTE] = _kxn(a["w_out_even"][0], 256)
    slots[S_INO:S_INO + N_INO] = _kxn(a["w_in_odd"][0], 384)
    wo = a["w_out_odd"][0]
    slots[S_OUTO:S_OUTO + 2] = _kxn(wo[:, :768], 384)
    slots[S_OUTO + 2, :, :2048] = _kxn(wo[:, 768:], 256)[0]
    for l, at in ((0, S_MOE0), (1, S_MOE1)):
        gu = np.concatenate([a["w_exp_gate"][l], a["w_exp_up"][l]], axis=2).reshape(NE, DC, P, 2 * FE).transpose(0, 2, 1, 3).reshape(NE, P, -1)
        dn = a["w_exp_down"][l].reshape(NE, 2, P, D).transpose(0, 2, 1, 3).reshape(NE, P, -1)
        slots[at:at + N_MOE] = np.concatenate([gu, dn], axis=2).reshape(NE, P, 2, SLOT).transpose(0, 2, 1, 3).reshape(N_MOE, P, SLOT)
    x = np.concatenate([a["x_prompt"][0], a["x_sample"][0]], axis=0)
    xt = np.ascontiguousarray(x.reshape(T, DC, P).transpose(2, 1, 0))

    nc = bacc.Bacc("TRN2", target_bir_lowering=False, num_devices=1)
    arrays = {"small_in": np.ascontiguousarray(small), "x_in": xt, "w_in": slots}
    ins = [nc.dram_tensor(n, v.shape, mybir.dt.from_np(v.dtype), kind="ExternalInput").ap() for n, v in arrays.items()]
    shapes = {"y_out": (P, DC, T), "stf_out": (P, HG * PS), "stb_out": (P, HG * PS), "ckv_out": (P, P), "kpe_out": (P, ROPE),
              "gk_out": (P, HKV * HD), "gv_out": (P, HKV * HD)}
    res = [nc.dram_tensor(n, s, mybir.dt.float32, kind="ExternalOutput").ap() for n, s in shapes.items()]
    build(nc, *ins, *res)
    r = run_bass_kernel_spmd(nc, [arrays], core_ids=[0]).results[0]
    y = np.asarray(r["y_out"]).transpose(2, 1, 0).reshape(T, D)
    unstate = lambda s: np.ascontiguousarray(np.asarray(s).reshape(2, NS, HG, PS).transpose(0, 2, 3, 1).reshape(1, 1, HS, PS, NS))
    return (np.ascontiguousarray(y[:P])[None], np.ascontiguousarray(y[P:])[None], unstate(r["stf_out"]), unstate(r["stb_out"]),
            np.ascontiguousarray(np.asarray(r["ckv_out"]).T)[None, None], np.asarray(r["kpe_out"])[None, None],
            np.asarray(r["gk_out"]).reshape(1, 1, P, HKV, HD), np.asarray(r["gv_out"]).reshape(1, 1, P, HKV, HD))
```
